# Optimizing a Trainium2 kernel written in Bass

```python
import math
import jax, jax.numpy as jnp
from jax import lax
import numpy as np

D_MODEL = 1024
BATCH = 1
SEQ = 256
DEPTH = 2

D_FF = 2816
FFN_HALF = 0.5
DN_HEAD_DIM = 128
DN_HEADS = D_MODEL // 128
DN_WIDTH = DN_HEADS * DN_HEAD_DIM
DN_CONV = 4
DN_CHUNK = 64
SB_HEAD_DIM = 128
SB_HEADS = D_MODEL // 128
SB_WIDTH = SB_HEADS * SB_HEAD_DIM
SB_BLOCK = 128
IN_SIZES = (3 * DN_WIDTH, DN_WIDTH, DN_HEADS, DN_HEADS, SB_WIDTH, SB_WIDTH, SB_WIDTH, D_MODEL, D_MODEL)
N_IN = 4 * DN_WIDTH + 2 * DN_HEADS + 3 * SB_WIDTH + 2 * D_MODEL
RMS_EPS = 1e-6
L2_EPS = 1e-6


def rmsnorm(x, gain):
    xf = x.astype(jnp.float32)
    y = xf * lax.rsqrt(jnp.mean(xf * xf, axis=-1, keepdims=True) + RMS_EPS)
    return (y * gain.astype(jnp.float32)).astype(x.dtype)

def l2norm(x):
    xf = x.astype(jnp.float32)
    return xf * lax.rsqrt(jnp.sum(xf * xf, axis=-1, keepdims=True) + L2_EPS)

def swiglu(h, w_in, w_out):
    gate, up = jnp.split(h @ w_in, 2, axis=-1)
    return (jax.nn.silu(gate) * up) @ w_out

def causal_depthwise_conv(x, w):
    width, ch = w.shape
    return lax.conv_general_dilated(
        x, w[:, None, :], window_strides=(1,), padding=((width - 1, 0),),
        dimension_numbers=("NWC", "WIO", "NWC"), feature_group_count=ch)

def split_cols(proj):
    parts, start = [], 0
    for size in IN_SIZES:
        parts.append(proj[..., start:start + size])
        start += size
    return parts

def to_heads(t, n_heads, head_dim):
    b, s, _ = t.shape
    return t.reshape(b, s, n_heads, head_dim).transpose(0, 2, 1, 3)

def gated_delta_rule_chunked(q, k, v, g, beta):
    b, h, t, dk = q.shape
    dv = v.shape[-1]
    c = DN_CHUNK
    n = t // c
    q = (q * (dk ** -0.5)).reshape(b, h, n, c, dk)
    k = k.reshape(b, h, n, c, dk)
    v = v.astype(jnp.float32).reshape(b, h, n, c, dv)
    beta = beta.reshape(b, h, n, c)
    g = lax.cumsum(g.reshape(b, h, n, c), axis=3)
    idx = jnp.arange(c)
    lower_incl = idx[:, None] >= idx[None, :]
    strict = idx[:, None] > idx[None, :]
    decay = jnp.exp(jnp.where(lower_incl, g[..., :, None] - g[..., None, :], -jnp.inf))
    k_beta = k * beta[..., None]
    lmat = jnp.where(strict, jnp.einsum("bhnid,bhnjd->bhnij", k_beta, k) * decay, 0.0)
    amat = lmat + jnp.eye(c, dtype=jnp.float32)
    rhs = jnp.concatenate([v * beta[..., None], k_beta * jnp.exp(g)[..., None]], axis=-1)
    sol = lax.linalg.triangular_solve(amat, rhs, left_side=True, lower=True, unit_diagonal=True)
    u, w = sol[..., :dv], sol[..., dv:]
    attn_intra = jnp.einsum("bhnid,bhnjd->bhnij", q, k) * decay
    q_dec = q * jnp.exp(g)[..., None]
    g_last = g[..., -1]
    k_dec = k * jnp.exp(g_last[..., None] - g)[..., None]

    def chunk_step(state, inp):
        q_i, k_i, u_i, w_i, a_i, gl_i = inp
        v_new = u_i - jnp.einsum("bhcd,bhdv->bhcv", w_i, state)
        o_i = jnp.einsum("bhcd,bhdv->bhcv", q_i, state) + jnp.einsum("bhij,bhjv->bhiv", a_i, v_new)
        state = state * jnp.exp(gl_i)[..., None, None] + jnp.einsum("bhcd,bhcv->bhdv", k_i, v_new)
        return state, o_i

    chunk_first = lambda arr: jnp.moveaxis(arr, 2, 0)
    s0 = jnp.zeros((b, h, dk, dv), jnp.float32)
    _, o = lax.scan(chunk_step, s0, (chunk_first(q_dec), chunk_first(k_dec), chunk_first(u),
                                     chunk_first(w), chunk_first(attn_intra), chunk_first(g_last)))
    return jnp.moveaxis(o, 0, 2).reshape(b, h, t, dv)

def stick_breaking_attention(q, k, v):
    t = q.shape[2]
    scale = q.shape[-1] ** -0.5
    outs = []
    for blk in range(t // SB_BLOCK):
        t0, t1 = blk * SB_BLOCK, (blk + 1) * SB_BLOCK
        z = jnp.einsum("bhqd,bhkd->bhqk", q[:, :, t0:t1], k[:, :, :t1]).astype(jnp.float32) * scale
        causal = jnp.arange(t1)[None, :] < (t0 + jnp.arange(SB_BLOCK))[:, None]
        log_1mb = jnp.where(causal, -jax.nn.softplus(z), 0.0)
        survive = lax.cumsum(log_1mb, axis=3, reverse=True) - log_1mb
        weights = jnp.where(causal, jnp.exp(jax.nn.log_sigmoid(z) + survive), 0.0)
        outs.append(jnp.einsum("bhqk,bhkd->bhqd", weights.astype(v.dtype), v[:, :, :t1]))
    return jnp.concatenate(outs, axis=2)

def hybrid_mixer(h, w_in, conv_w, a_log, dt_bias, dn_out_norm, sb_q_norm, sb_k_norm,
                 w_branch_a, w_branch_b, w_out):
    b, t, _ = h.shape
    dn_qkv, dn_z, dn_b, dn_a, sb_q, sb_k, sb_v, gate_a, gate_b = split_cols(h @ w_in)
    qkv = jax.nn.silu(causal_depthwise_conv(dn_qkv, conv_w))
    q, k, v = jnp.split(qkv, 3, axis=-1)
    q = l2norm(to_heads(q, DN_HEADS, DN_HEAD_DIM))
    k = l2norm(to_heads(k, DN_HEADS, DN_HEAD_DIM))
    v = to_heads(v, DN_HEADS, DN_HEAD_DIM)
    beta = jax.nn.sigmoid(dn_b.astype(jnp.float32)).transpose(0, 2, 1)
    g = (-jnp.exp(a_log.astype(jnp.float32))
         * jax.nn.softplus(dn_a.astype(jnp.float32) + dt_bias.astype(jnp.float32))).transpose(0, 2, 1)
    o_a = gated_delta_rule_chunked(q, k, v, g, beta).transpose(0, 2, 1, 3)
    o_a = rmsnorm(o_a, dn_out_norm) * jax.nn.silu(dn_z.reshape(b, t, DN_HEADS, DN_HEAD_DIM).astype(jnp.float32))
    y_a = o_a.reshape(b, t, DN_WIDTH).astype(h.dtype) @ w_branch_a
    qb = rmsnorm(to_heads(sb_q, SB_HEADS, SB_HEAD_DIM), sb_q_norm)
    kb = rmsnorm(to_heads(sb_k, SB_HEADS, SB_HEAD_DIM), sb_k_norm)
    vb = to_heads(sb_v, SB_HEADS, SB_HEAD_DIM)
    o_b = stick_breaking_attention(qb, kb, vb).transpose(0, 2, 1, 3).reshape(b, t, SB_WIDTH)
    y_b = o_b @ w_branch_b
    merged = jax.nn.sigmoid(gate_a) * y_a + jax.nn.sigmoid(gate_b) * y_b
    return merged @ w_out

def first_inputs(seed: int = 0) -> dict:
    key = jax.random.key(seed)
    ks = jax.random.split(key, 20)
    L = DEPTH

    def dense(k, shape, fan_in):
        return jax.random.normal(k, shape, jnp.float32) * (fan_in ** -0.5)

    def gain(k, shape):
        return 1.0 + 0.1 * jax.random.normal(k, shape, jnp.float32)

    dt = jnp.exp(jax.random.uniform(ks[8], (L, DN_HEADS), jnp.float32, math.log(1e-3), math.log(1e-1)))
    return {
        "x": jax.random.normal(ks[0], (BATCH, SEQ, D_MODEL), jnp.float32),
        "ffn1_norm": gain(ks[1], (L, D_MODEL)),
        "ffn1_w_in": dense(ks[2], (L, D_MODEL, 2 * D_FF), D_MODEL),
        "ffn1_w_out": dense(ks[3], (L, D_FF, D_MODEL), D_FF),
        "mix_norm": gain(ks[4], (L, D_MODEL)),
        "w_in": dense(ks[5], (L, D_MODEL, N_IN), D_MODEL),
        "dn_conv_w": dense(ks[6], (L, DN_CONV, 3 * DN_WIDTH), DN_CONV),
        "dn_a_log": jnp.log(jax.random.uniform(ks[7], (L, DN_HEADS), jnp.float32, 1.0, 16.0)),
        "dn_dt_bias": dt + jnp.log(-jnp.expm1(-dt)),
        "dn_out_norm": gain(ks[9], (L, DN_HEAD_DIM)),
        "sb_q_norm": gain(ks[10], (L, SB_HEAD_DIM)),
        "sb_k_norm": gain(ks[11], (L, SB_HEAD_DIM)),
        "w_branch_a": dense(ks[12], (L, DN_WIDTH, D_MODEL), DN_WIDTH),
        "w_branch_b": dense(ks[13], (L, SB_WIDTH, D_MODEL), SB_WIDTH),
        "w_out": dense(ks[14], (L, D_MODEL, D_MODEL), D_MODEL),
        "ffn2_norm": gain(ks[15], (L, D_MODEL)),
        "ffn2_w_in": dense(ks[16], (L, D_MODEL, 2 * D_FF), D_MODEL),
        "ffn2_w_out": dense(ks[17], (L, D_FF, D_MODEL), D_FF),
    }

def first_block(x, ffn1_norm, ffn1_w_in, ffn1_w_out, mix_norm, w_in, dn_conv_w, dn_a_log, dn_dt_bias,
              dn_out_norm, sb_q_norm, sb_k_norm, w_branch_a, w_branch_b, w_out,
              ffn2_norm, ffn2_w_in, ffn2_w_out):
    for l in range(DEPTH):
        x = x + FFN_HALF * swiglu(rmsnorm(x, ffn1_norm[l]), ffn1_w_in[l], ffn1_w_out[l])
        x = x + hybrid_mixer(rmsnorm(x, mix_norm[l]), w_in[l], dn_conv_w[l], dn_a_log[l], dn_dt_bias[l],
                             dn_out_norm[l], sb_q_norm[l], sb_k_norm[l],
                             w_branch_a[l], w_branch_b[l], w_out[l])
        x = x + FFN_HALF * swiglu(rmsnorm(x, ffn2_norm[l]), ffn2_w_in[l], ffn2_w_out[l])
    return x


GRID_W = 64
Q_BLOCK = 128
ROPE_THETA = 10000.0
EPS = 1e-6
MLA_HEADS = 6
MLA_NOPE = 64
MLA_ROPE = 32
MLA_V = 64
MLA_Q_RANK = 256
MLA_KV_RANK = 128
GQA_HEADS = 6
GQA_KV_HEADS = 2
GQA_DIM = 64
GMLP_GROUPS = 4
GMLP_DIM = 64
GMLP_CHUNK = 128
W_A = MLA_HEADS * MLA_V
W_B = GQA_HEADS * GQA_DIM
W_C = GMLP_GROUPS * GMLP_DIM
D_MIX = W_A + W_B + W_C
IN_SPLITS = (MLA_Q_RANK, MLA_KV_RANK, MLA_ROPE, W_B, GQA_KV_HEADS * GQA_DIM, GQA_KV_HEADS * GQA_DIM, 2 * W_C)
D_IN = 1568
MEM_TOKENS = 256
MEM_HEADS = 4
MEM_DIM = 128
CONV_W = 3


def rms_norm(x, g):
    xf = x.astype(jnp.float32)
    y = xf * lax.rsqrt(jnp.mean(xf * xf, axis=-1, keepdims=True) + EPS)
    return (y * g.astype(jnp.float32)).astype(x.dtype)

def axial_rope_table(S, d_rot):
    rows = S // GRID_W
    row = jnp.repeat(jnp.arange(rows, dtype=jnp.float32), GRID_W)
    col = jnp.tile(jnp.arange(GRID_W, dtype=jnp.float32), rows)
    n = d_rot // 4
    inv = ROPE_THETA ** (-jnp.arange(n, dtype=jnp.float32) / n)
    ang = jnp.concatenate([row[:, None] * inv, col[:, None] * inv], axis=-1)
    return jnp.cos(ang)[:, None, :], jnp.sin(ang)[:, None, :]

def apply_rope(x, cos, sin):
    d = x.shape[-1]
    xp = x.reshape(*x.shape[:-1], d // 2, 2)
    a, b = xp[..., 0], xp[..., 1]
    c, s = cos.astype(x.dtype), sin.astype(x.dtype)
    return jnp.stack([a * c - b * s, a * s + b * c], axis=-1).reshape(x.shape)

def block_attention(q, k, v, scale):
    B, S, H, dk = q.shape
    Hk, dv = k.shape[2], v.shape[-1]
    G = H // Hk
    nb = S // Q_BLOCK
    qb = q.reshape(B, nb, Q_BLOCK, Hk, G, dk).transpose(1, 0, 2, 3, 4, 5)

    def one_block(qi):
        s = jnp.einsum('bqhgd,bkhd->bhgqk', qi, k, preferred_element_type=jnp.float32) * scale
        p = jax.nn.softmax(s, axis=-1).astype(v.dtype)
        return jnp.einsum('bhgqk,bkhe->bqhge', p, v)

    ob = lax.map(one_block, qb)
    return ob.transpose(1, 0, 2, 3, 4, 5).reshape(B, S, H * dv)

def hybrid_mixer_2(h, rope_a, rope_b, w_in, mla_q_norm, mla_w_uq, mla_kv_norm, mla_w_ukv,
                 gqa_q_norm, gqa_k_norm, gmlp_v_norm, gmlp_w_s, gmlp_b_s, out_norm, w_out):
    B, S, _ = h.shape
    z = h @ w_in
    offs = [int(i) for i in np.cumsum(IN_SPLITS)[:-1]]
    c_q, c_kv, k_rope, g_q, g_k, g_v, g_m = jnp.split(z, offs, axis=-1)

    qa = (rms_norm(c_q, mla_q_norm) @ mla_w_uq).reshape(B, S, MLA_HEADS, MLA_NOPE + MLA_ROPE)
    q_nope, q_pe = qa[..., :MLA_NOPE], apply_rope(qa[..., MLA_NOPE:], *rope_a)
    kva = (rms_norm(c_kv, mla_kv_norm) @ mla_w_ukv).reshape(B, S, MLA_HEADS, MLA_NOPE + MLA_V)
    k_nope, v_a = kva[..., :MLA_NOPE], kva[..., MLA_NOPE:]
    k_pe = apply_rope(k_rope.reshape(B, S, 1, MLA_ROPE), *rope_a)
    q_a = jnp.concatenate([q_nope, q_pe], axis=-1)
    k_a = jnp.concatenate([k_nope, jnp.broadcast_to(k_pe, (B, S, MLA_HEADS, MLA_ROPE))], axis=-1)
    y_a = block_attention(q_a, k_a, v_a, (MLA_NOPE + MLA_ROPE) ** -0.5)

    q_b = apply_rope(rms_norm(g_q.reshape(B, S, GQA_HEADS, GQA_DIM), gqa_q_norm), *rope_b)
    k_b = apply_rope(rms_norm(g_k.reshape(B, S, GQA_KV_HEADS, GQA_DIM), gqa_k_norm), *rope_b)
    v_b = g_v.reshape(B, S, GQA_KV_HEADS, GQA_DIM)
    y_b = block_attention(q_b, k_b, v_b, GQA_DIM ** -0.5)

    g_m = jax.nn.gelu(g_m)
    u, vv = g_m[..., :W_C], g_m[..., W_C:]
    vv = rms_norm(vv, gmlp_v_norm).reshape(B, S // GMLP_CHUNK, GMLP_CHUNK, GMLP_GROUPS, GMLP_DIM)
    mixed = jnp.einsum('gpq,bnqgc->bnpgc', gmlp_w_s, vv) + gmlp_b_s.T[None, None, :, :, None]
    y_c = u * mixed.reshape(B, S, W_C)

    y = jnp.concatenate([rms_norm(y_a, out_norm[:W_A]),
                         rms_norm(y_b, out_norm[W_A:W_A + W_B]),
                         rms_norm(y_c, out_norm[W_A + W_B:])], axis=-1)
    return y @ w_out

def memory_cross_attention(h, mem, mem_kv_norm, mem_w_q, mem_w_kv, mem_w_o):
    B, S, _ = h.shape
    T = mem.shape[1]
    q = (h @ mem_w_q).reshape(B, S, MEM_HEADS, MEM_DIM)
    kv = rms_norm(mem, mem_kv_norm) @ mem_w_kv
    k = kv[..., :MEM_HEADS * MEM_DIM].reshape(B, T, MEM_HEADS, MEM_DIM)
    v = kv[..., MEM_HEADS * MEM_DIM:].reshape(B, T, MEM_HEADS, MEM_DIM)
    return block_attention(q, k, v, MEM_DIM ** -0.5) @ mem_w_o

def conv_gated_ffn(h, w_up, conv_w, conv_b, w_down):
    a = h @ w_up
    ap = jnp.pad(a, ((0, 0), (1, 1), (0, 0)))
    a = ap[:, :-2] * conv_w[0] + ap[:, 1:-1] * conv_w[1] + ap[:, 2:] * conv_w[2] + conv_b
    gate, val = a[..., :D_FF], a[..., D_FF:]
    return (jax.nn.silu(gate) * val) @ w_down

def second_inputs(seed: int = 0) -> dict:
    key = jax.random.key(seed)
    ks = iter(jax.random.split(key, 48))

    def nrm(shape, scale):
        return jax.random.normal(next(ks), shape, jnp.float32) * scale

    def gain(shape):
        return 1.0 + nrm(shape, 0.05)

    L = DEPTH
    return {
        "x": nrm((BATCH, SEQ, D_MODEL), 1.0),
        "mem": nrm((BATCH, MEM_TOKENS, D_MODEL), 1.0),
        "mix_norm": gain((L, D_MODEL)),
        "w_in": nrm((L, D_MODEL, D_IN), D_MODEL ** -0.5),
        "mla_q_norm": gain((L, MLA_Q_RANK)),
        "mla_w_uq": nrm((L, MLA_Q_RANK, MLA_HEADS * (MLA_NOPE + MLA_ROPE)), MLA_Q_RANK ** -0.5),
        "mla_kv_norm": gain((L, MLA_KV_RANK)),
        "mla_w_ukv": nrm((L, MLA_KV_RANK, MLA_HEADS * (MLA_NOPE + MLA_V)), MLA_KV_RANK ** -0.5),
        "gqa_q_norm": gain((L, GQA_DIM)),
        "gqa_k_norm": gain((L, GQA_DIM)),
        "gmlp_v_norm": gain((L, W_C)),
        "gmlp_w_s": nrm((L, GMLP_GROUPS, GMLP_CHUNK, GMLP_CHUNK), GMLP_CHUNK ** -0.5),
        "gmlp_b_s": gain((L, GMLP_GROUPS, GMLP_CHUNK)),
        "out_norm": gain((L, D_MIX)),
        "w_out": nrm((L, D_MIX, D_MODEL), D_MIX ** -0.5),
        "mem_x_norm": gain((L, D_MODEL)),
        "mem_kv_norm": gain((L, D_MODEL)),
        "mem_w_q": nrm((L, D_MODEL, MEM_HEADS * MEM_DIM), D_MODEL ** -0.5),
        "mem_w_kv": nrm((L, D_MODEL, 2 * MEM_HEADS * MEM_DIM), D_MODEL ** -0.5),
        "mem_w_o": nrm((L, MEM_HEADS * MEM_DIM, D_MODEL), (MEM_HEADS * MEM_DIM) ** -0.5),
        "ffn_norm": gain((L, D_MODEL)),
        "ffn_w_up": nrm((L, D_MODEL, 2 * D_FF), D_MODEL ** -0.5),
        "ffn_conv_w": nrm((L, CONV_W, 2 * D_FF), CONV_W ** -0.5),
        "ffn_conv_b": nrm((L, 2 * D_FF), 0.01),
        "ffn_w_down": nrm((L, D_FF, D_MODEL), D_FF ** -0.5),
        "final_norm": gain((D_MODEL,)),
    }

def second_block(x, mem, mix_norm, w_in, mla_q_norm, mla_w_uq, mla_kv_norm, mla_w_ukv,
              gqa_q_norm, gqa_k_norm, gmlp_v_norm, gmlp_w_s, gmlp_b_s, out_norm, w_out,
              mem_x_norm, mem_kv_norm, mem_w_q, mem_w_kv, mem_w_o,
              ffn_norm, ffn_w_up, ffn_conv_w, ffn_conv_b, ffn_w_down, final_norm):
    S = x.shape[1]
    rope_a = axial_rope_table(S, MLA_ROPE)
    rope_b = axial_rope_table(S, GQA_DIM)
    for l in range(DEPTH):
        h = rms_norm(x, mix_norm[l])
        x = x + hybrid_mixer_2(h, rope_a, rope_b, w_in[l], mla_q_norm[l], mla_w_uq[l], mla_kv_norm[l],
                             mla_w_ukv[l], gqa_q_norm[l], gqa_k_norm[l], gmlp_v_norm[l], gmlp_w_s[l],
                             gmlp_b_s[l], out_norm[l], w_out[l])
        h = rms_norm(x, mem_x_norm[l])
        x = x + memory_cross_attention(h, mem, mem_kv_norm[l], mem_w_q[l], mem_w_kv[l], mem_w_o[l])
        h = rms_norm(x, ffn_norm[l])
        x = x + conv_gated_ffn(h, ffn_w_up[l], ffn_conv_w[l], ffn_conv_b[l], ffn_w_down[l])
    return rms_norm(x, final_norm)


def setup_inputs(seed=0):
    out = dict(first_inputs(seed))
    for name, value in second_inputs(seed + 1).items():
        if name != "x":
            out[name + "_2"] = value
    return out


def reference(
    x, ffn1_norm, ffn1_w_in, ffn1_w_out, mix_norm, w_in, dn_conv_w, dn_a_log, dn_dt_bias,
    dn_out_norm, sb_q_norm, sb_k_norm, w_branch_a, w_branch_b, w_out, ffn2_norm, ffn2_w_in,
    ffn2_w_out, mem_2, mix_norm_2, w_in_2, mla_q_norm_2, mla_w_uq_2, mla_kv_norm_2, mla_w_ukv_2,
    gqa_q_norm_2, gqa_k_norm_2, gmlp_v_norm_2, gmlp_w_s_2, gmlp_b_s_2, out_norm_2, w_out_2,
    mem_x_norm_2, mem_kv_norm_2, mem_w_q_2, mem_w_kv_2, mem_w_o_2, ffn_norm_2, ffn_w_up_2,
    ffn_conv_w_2, ffn_conv_b_2, ffn_w_down_2, final_norm_2,
):
    x = first_block(
        x, ffn1_norm, ffn1_w_in, ffn1_w_out, mix_norm, w_in, dn_conv_w, dn_a_log, dn_dt_bias,
        dn_out_norm, sb_q_norm, sb_k_norm, w_branch_a, w_branch_b, w_out, ffn2_norm, ffn2_w_in,
        ffn2_w_out,
    )
    return second_block(
        x, mem_2, mix_norm_2, w_in_2, mla_q_norm_2, mla_w_uq_2, mla_kv_norm_2, mla_w_ukv_2,
        gqa_q_norm_2, gqa_k_norm_2, gmlp_v_norm_2, gmlp_w_s_2, gmlp_b_s_2, out_norm_2, w_out_2,
        mem_x_norm_2, mem_kv_norm_2, mem_w_q_2, mem_w_kv_2, mem_w_o_2, ffn_norm_2, ffn_w_up_2,
        ffn_conv_w_2, ffn_conv_b_2, ffn_w_down_2, final_norm_2,
    )


_drawn_inputs = setup_inputs


def setup_inputs(seed=0):
    import zlib

    import numpy as np

    out = dict(_drawn_inputs(seed))
    spreads = {}
    factors = {'mla_q_norm_2': 3.368,
     'gqa_q_norm_2': 4.169,
     'gqa_k_norm_2': 4.681,
     'gmlp_v_norm_2': 3.744,
     'gmlp_b_s_2': 4.189,
     'mem_x_norm_2': 8.0,
     'mem_kv_norm_2': 8.0,
     'ffn_conv_b_2': 8.0}
    for name, (base, spread) in spreads.items():
        noise = np.random.default_rng([zlib.crc32(name.encode()), seed]).standard_normal(out[name].shape)
        drawn = base * np.exp(spread * noise) if base else spread * noise
        out[name] = __import__('jax').numpy.asarray(drawn.astype(out[name].dtype))
    for name, factor in factors.items():
        out[name] = (out[name] * factor).astype(out[name].dtype)
    return out
```

```python
from contextlib import ExitStack

import numpy as np

import concourse.bass as bass
from concourse import mybir

F32 = mybir.dt.float32
F32R = mybir.dt.float32r
ALU = mybir.AluOpType
ACT = mybir.ActivationFunctionType
AX_X = mybir.AxisListType.X

P = 128
D = 1024
S = 256
ST = S // P
KB = D // P
DFF = 2816
FB = DFF // P
NCH = FB // 2
DEPTH = 2
RING = 3
UNIT = 2048
EPS = 1e-6

HEADS = 8
CHUNK = 64
NPAIR = HEADS // 2
B_COL = 4 * D
A_COL = B_COL + HEADS
SB_COL = A_COL + HEADS
GA_COL = SB_COL + 3 * D
GB_COL = GA_COL + D
FFN_UNITS = 3 * NCH
MIX1_UNITS = 51
LAYER1_TURNS = (2 * FFN_UNITS + MIX1_UNITS) // RING
V1_FFN1, V1_MIX, V1_FFN2, V1_CONV, V1_ON, V1_SBQ, V1_SBK = 0, 8, 16, 24, 120, 121, 122
V1_LOADS = 9

MLA_H, GQA_H = 6, 6
MLA_DK, NOPE, ROPE = 96, 64, 32
MIX2_UNITS = 9 + 4 + 4 + 2 + 2
LAYER2_TURNS = (MIX2_UNITS + FFN_UNITS) // RING
V2_MIX, V2_CQ, V2_CKV, V2_GQ, V2_GK, V2_ON, V2_MEMX, V2_MEMKV, V2_FFN, V2_CB, V2_BS = 0, 8, 10, 11, 12, 13, 21, 29, 37, 45, 89
V2_TAP = (128, 128 + 44, 256)
V2_LOADS = 18
W2_COLS = [(0, 256), (256, 160), (416, 384), (416, 384), (800, 256), (1056, 256), (1312, 256)]

CONSTS = ["ident", "ones", "halves", "tri", "rot", "chunk", "inv0", "inv1", "inv2", "inv3", "inv4", "inv5",
          "sbneg", "sbadd", "cosa", "sina", "cosb", "sinb", "scan"]
CONST_W = {"sbneg": 384, "sbadd": 384, "cosa": 256, "sina": 256, "cosb": 256, "sinb": 256, "scan": 256}
CONST_AT, _w = {}, 0
for _name in CONSTS:
    CONST_AT[_name] = (_w, CONST_W.get(_name, 128))
    _w += CONST_W.get(_name, 128)
CONST_TOTAL = _w


def constants():
    c = np.zeros((P, CONST_TOTAL), np.float32)

    def put(name, value):
        at, w = CONST_AT[name]
        c[:value.shape[0], at:at + value.shape[1]] = value

    j, i = np.arange(P)[:, None], np.arange(P)[None, :]
    put("ident", (j == i).astype(np.float32))
    put("ones", np.ones((P, P), np.float32))
    put("halves", (j // 64 == i // 64).astype(np.float32))
    put("tri", (j >= i).astype(np.float32))
    rot = np.zeros((P, P), np.float32)
    rot[np.arange(1, P, 2), np.arange(0, P, 2)] = -1.0
    rot[np.arange(0, P, 2), np.arange(1, P, 2)] = 1.0
    put("rot", rot)
    put("chunk", ((j // CHUNK == i // CHUNK) & (j <= i)).astype(np.float32))
    for n in range(6):
        s = 1 << n
        put(f"inv{n}", ((j // (2 * s) == i // (2 * s)) & ((i // s) % 2 == 1) & ((j // s) % 2 == 0)).astype(np.float32))
    before = (j < i).astype(np.float32)
    full = np.concatenate([before, np.ones((P, P), np.float32), before], axis=1)
    put("sbneg", -full)
    put("sbadd", np.where(full > 0, 0.0, -1e30).astype(np.float32))

    def table(d_rot):
        t = np.arange(S, dtype=np.float32)
        row, col = np.floor(t / 64), t % 64
        n = d_rot // 4
        inv = (np.float32(10000.0) ** (-np.arange(n, dtype=np.float32) / np.float32(n))).astype(np.float32)
        ang = np.concatenate([row[:, None] * inv, col[:, None] * inv], axis=-1).astype(np.float32)
        return np.repeat(np.cos(ang), 2, axis=1).T.astype(np.float32), np.repeat(np.sin(ang), 2, axis=1).T.astype(np.float32)

    ca, sa = table(ROPE)
    put("cosa", np.concatenate([np.ones((NOPE, S), np.float32), ca]))
    put("sina", np.concatenate([np.zeros((NOPE, S), np.float32), sa]))
    cb, sbb = table(64)
    put("cosb", np.concatenate([cb, cb]))
    put("sinb", np.concatenate([sbb, sbb]))
    put("scan", np.broadcast_to((np.arange(S) % CHUNK != 0).astype(np.float32), (P, S)))
    return c


class Steps:

    def __init__(self, names):
        self.names = list(names)
        assert len(set(self.names)) == len(self.names)
        self.count = len(self.names)

    def at(self, stage, name):
        return self.count * stage + (self.names.index(name) + 1)


class Own:

    def __init__(self, eng, sem):
        self.eng, self.sem, self.n = eng, sem, 0

    def restart(self):
        self.eng.sem_clear(self.sem)
        self.n = 0

    def link(self, ins):
        self.n += 1
        ins.then_inc(self.sem, 1)
        self.eng.wait_ge(self.sem, self.n)


LEVELS = 5
DELTA_PE = Steps(["sums", "rows", "gram", "tok", "xt"] + [f"{a}{i}" for i in range(LEVELS) for a in "pq"]
                 + ["uw", "kv0", "ws1", "kv1", "ws2", "kv2", "ws3", "o", "osum"])
DELTA_ACT = Steps(["silu", "sq", "rs", "decay", "x"] + [f"p{i}" for i in range(LEVELS)] + ["uw", "osq", "ors"])
DELTA_DVE = Steps(["diff", "qkn", "lt", "m0", "tok"]
                  + sum([([f"m{i + 1}"] if i + 1 < LEVELS else []) + [f"t{i}"] for i in range(LEVELS)], [])
                  + ["s0", "v1", "s1", "v2", "s2", "v3", "o"])
SB_PE = Steps(["sums", "z", "tri", "pv"])
SB_ACT = Steps(["sq", "rs", "soft", "w", "o"])
SB_DVE = Steps(["qkn", "nsp", "ex", "o"])
ROWS_ACT = Steps(["ln", "eg"])
ROWS_DVE = Steps(["g", "beg", "cols"])
M2_BATCHES = 6
M2_PE = Steps(["sums", "rope", "qrope", "wst", "mix", "s0"]
              + sum([([f"s{b + 1}"] if b + 1 < M2_BATCHES else []) + [f"t{b}", f"v{b}"] for b in range(M2_BATCHES)], []))
M2_ACT = Steps(["sq", "gv", "rs", "gelu", "vrs", "qa", "kv", "wst", "e0"]
               + sum([([f"e{b + 1}"] if b + 1 < M2_BATCHES else []) + [f"pt{b}"] for b in range(M2_BATCHES)], []) + ["seg"])
M2_DVE = Steps(["cn", "gn", "kpe", "gr", "qr", "vn", "mix", "mx0"]
               + sum([([f"mx{b + 1}"] if b + 1 < M2_BATCHES else []) + [f"o{b}"] for b in range(M2_BATCHES)], []))
ME_BATCHES = 2
ME_PE = Steps(["s0"] + sum([([f"s{b + 1}"] if b + 1 < ME_BATCHES else []) + [f"t{b}", f"v{b}"] for b in range(ME_BATCHES)], []))
ME_ACT = Steps(["kv0", "kv1", "kv2", "kv3", "q0", "q1", "e0"]
               + sum([([f"e{b + 1}"] if b + 1 < ME_BATCHES else []) + [f"pt{b}", f"oh{b}"] for b in range(ME_BATCHES)], []))
ME_DVE = Steps(["mx0"] + sum([([f"mx{b + 1}"] if b + 1 < ME_BATCHES else []) + [f"pn{b}", f"ol{b}"] for b in range(ME_BATCHES)], []))

DELTA_BG = {0: [6, 7, 8, 9], 1: [10, 11, 12, 13], 2: [14, 15, 16, 17], 3: list(range(18, 27))}
SB_BG = {0: [30, 31, 32, 33], 1: [34, 35, 36, 37], 2: [38, 39, 40, 41, 42], 3: []}


def spread(units, n):
    return [units[len(units) * i // n:len(units) * (i + 1) // n] for i in range(n)]


def mix1_unit(r):
    if r < 2:
        return "ba"[r], 0, (B_COL, A_COL)[r], 128
    if r < 18:
        c, kind = divmod(r - 2, 4)
        return "qkvz"[kind], c, kind * D + 256 * c, 256
    if r < 30:
        c, kind = divmod(r - 18, 3)
        return ("sq", "sk", "sv")[kind], c, SB_COL + kind * D + 256 * c, 256
    if r < 34:
        return "wa", r - 30, 256 * (r - 30), 256
    if r < 38:
        return "ga", r - 34, GA_COL + 256 * (r - 34), 256
    if r < 41:
        return "gb", r - 38, GB_COL + 256 * (r - 38), 256
    if r < 43:
        return "gb", 3, GB_COL + 768 + 128 * (r - 41), 128
    if r < 47:
        return "wb", r - 43, 256 * (r - 43), 256
    return "wo", r - 47, 256 * (r - 47), 256


def build_program(nc, a, const, out):
    ctx = ExitStack()
    with ctx:
        def sb(name, shape, dt=F32):
            return ctx.enter_context(nc.sbuf_tensor("sb_" + name, shape, dt))

        def sem(name):
            return ctx.enter_context(nc.semaphore(name))

        ps = ctx.enter_context(nc.psum_tensor("ps", [P, 8, 512], F32))
        raw = sb("raw", [P, RING, UNIT])
        hi = sb("hi", [P, RING, UNIT], F32R)
        lo = sb("lo", [P, RING, UNIT], F32R)
        x = sb("x", [P, ST, D])
        hT_h = sb("hT_h", [P, KB, S], F32R)
        hT_l = sb("hT_l", [P, KB, S], F32R)
        o_h = sb("o_h", [P, KB, S], F32R)
        o_l = sb("o_l", [P, KB, S], F32R)
        qT = sb("qT", [P, KB, S])
        kT = sb("kT", [P, KB, S])
        vT = sb("vT", [P, KB, S])
        zT = sb("zT", [P, KB, S])
        tok = sb("tok", [P, ST, D])
        sq = sb("sq", [P, 2, 512])
        rs = sb("rs", [P, 2, 512])
        decay, attn, lmat, mlev, xinv, yinv, plev, u_v, w_k, k_dec, q_dec = (
            sb(n, [P, 512]) for n in ("decay", "attn", "lmat", "mlev", "xinv", "yinv", "plev", "u_v", "w_k", "k_dec", "q_dec"))
        state = sb("state", [P, 3, 2, P])
        cst = sb("const", [P, CONST_TOTAL])
        stage = sb("stage", [P, 3, P])
        vec1 = sb("vec1", [P, P])
        vec2 = sb("vec2", [P, 3 * P])
        beta_r, g_r, eg_r = (sb(n, [HEADS, S]) for n in ("beta_r", "g_r", "eg_r"))
        tcol = sb("tcol", [P, 4, ST, HEADS])
        egl = sb("egl", [P, 2, 4])
        hcol = sb("hcol", [HEADS, 4])
        gcol = sb("gcol", [P, 4])
        eps_t = sb("eps", [P, 1])
        ss = sb("ss", [P, 8])
        rstd = sb("rstd", [P, 8])
        negmax = sb("negmax", [P, 2, 4])
        psum_p = sb("psum_p", [P, 2, 4])
        rinv = sb("rinv", [P, 2, 4])
        sqf = sq[:].rearrange("p a n -> p (a n)")
        rsf = rs[:].rearrange("p a n -> p (a n)")
        act_h = o_h[:, 0:2, :].rearrange("p a n -> p (a n)")
        act_l = o_l[:, 0:2, :].rearrange("p a n -> p (a n)")
        sil, prod = xinv, yinv
        junk = kT[:].rearrange("p (t k) n -> p t (k n)", t=ST)
        memx = zT[:].rearrange("p (t k) n -> p t (k n)", t=ST)

        def cc(name):
            at, w = CONST_AT[name]
            return cst[:, at:at + w]

        def over(ap, n, axis=1):
            v = ap.unsqueeze(axis)
            shape = list(v.shape)
            shape[axis] = n
            return v.to_broadcast(shape)

        mem_v = vT[:, 0:4, :].rearrange("p (t k) n -> p t (k n)", t=ST)
        gain_row = vT[:, 0:4, :].rearrange("p k n -> p (k n)")
        result = qT[:].rearrange("p (t k) n -> p t (k n)", t=ST)
        ident = cc("ident")

        start_loaded = sem("start_loaded")
        loads_begun = sem("loads_begun")
        raw_loaded = [sem(f"raw_loaded{i}") for i in range(RING)]
        heads_loaded = [sem("heads_loaded0"), sem("heads_loaded1")]
        hi_ready, lo_ready, unit_done = sem("hi_ready"), sem("lo_ready"), sem("unit_done")
        vec_loaded, vec_taken, vec_ready = sem("vec_loaded"), sem("vec_taken"), sem("vec_ready")
        zeroed, eps_ready = sem("zeroed"), sem("eps_ready")
        rstd_ready, xn_ready, tr_ready, hh_ready, h_ready = (sem(n) for n in ("rstd_ready", "xn_ready", "tr_ready", "hh_ready", "h_ready"))
        x_ready, added = sem("x_ready"), sem("added")
        sil_ready, gate_used, up_used, act_ready = (sem(n) for n in ("sil_ready", "gate_used", "up_used", "act_ready"))
        bank_free = [sem("bank_free0"), sem("bank_free1")]
        rows_act, rows_dve, rows_pe = sem("rows_act"), sem("rows_dve"), sem("rows_pe")
        dl_pe, dl_act, dl_dve = sem("delta_pe"), sem("delta_act"), sem("delta_dve")
        sb_pe, sb_act, sb_dve = sem("sb_pe"), sem("sb_act"), sem("sb_dve")
        gate_a, gated_a, gate_b = sem("gate_a"), sem("gated_a"), sem("gate_b")
        merged_ready = sem("merged_ready")
        m2_pe, m2_act, m2_dve = sem("m2_pe"), sem("m2_act"), sem("m2_dve")
        me_pe, me_act, me_dve = sem("me_pe"), sem("me_act"), sem("me_dve")
        mem_loaded = sem("mem_loaded")
        out_ready, out_stored = sem("out_ready"), sem("out_stored")
        act_own, dve_own = sem("act_own"), sem("dve_own")

        block = ctx.enter_context(nc.Block())

        def of_layer(name, l):
            return a[name][bass.ds(l, 1)]

        @block.sync
        def _(sp):
            def load(b, k, src, kk, n):
                slot = k % RING
                sp.wait_ge(lo_ready, RING * b + (k + 1))
                sp.sem_inc(loads_begun, 1)
                dst = raw[:, slot, 0:kk * n].rearrange("p (k n) -> p k n", k=kk)
                sp.dma_start(dst, src).then_inc(raw_loaded[slot], 16)

            def load_heads(b, k, src):
                slot = k % RING
                sp.wait_ge(lo_ready, RING * b + (k + 1))
                sp.sem_inc(loads_begun, 1)
                dst = raw[:, slot, 0:4 * 384].rearrange("p (k j h e) -> p k j h e", k=4, j=3, h=2)
                src = src.rearrange("o (k p) (h j e) -> p (o k) h j e", p=P, h=2, j=3)
                for h in range(2):
                    for j in range(3):
                        done = heads_loaded[k % 2] if h + j else raw_loaded[slot]
                        sp.dma_start(dst[:, :, j, h, :], src[:, :, h, j, :]).then_inc(done, 16)

            def cols(w, l, c0, n):
                return of_layer(w, l)[:, :, bass.ds(c0, n)].rearrange("o (k p) n -> p (o k) n", p=P)

            def rows(w, l, r0, n):
                return of_layer(w, l)[:, bass.ds(r0, n), :].rearrange("o (k p) n -> p (o k) n", p=P)

            def ffn(w_in, w_out, l, b):
                gate = lambda k, c, bb=0: load(b + bb, k, cols(w_in, l, 256 * c, 256), 8, 256)
                up = lambda k, c, bb=0: load(b + bb, k, cols(w_in, l, DFF + 256 * c, 256), 8, 256)
                down = lambda k, c, bb=0: load(b + bb, k, rows(w_out, l, 256 * c, 256), 2, D)
                gate(0, 0), up(1, 0), gate(2, 1), up(3, 1), down(4, 0)
                with sp.Fori(1, NCH - 1) as j:
                    gate(2, j + 1, j), up(3, j + 1, j), down(4, j, j)
                down(2, NCH - 1, NCH - 1)

            sp.dma_start(cst[:], const).then_inc(start_loaded, 16)
            sp.dma_start(x[:], a["x"].rearrange("o (t p) d -> p (o t) d", p=P)).then_inc(start_loaded, 16)

            with sp.Fori(0, DEPTH) as l:
                sp.wait_ge(vec_taken, l)
                sp.wait_ge(zeroed, 1)
                for at, name, n in ((V1_FFN1, "ffn1_norm", 8), (V1_MIX, "mix_norm", 8), (V1_FFN2, "ffn2_norm", 8),
                                    (V1_ON, "dn_out_norm", 1), (V1_SBQ, "sb_q_norm", 1), (V1_SBK, "sb_k_norm", 1)):
                    sp.dma_start(stage[at:at + n, 0, :], of_layer(name, l).rearrange("o (r n) -> (o r) n", n=P)).then_inc(vec_loaded, 16)
                sp.dma_start(stage[V1_CONV:V1_CONV + 96, 0, :],
                             of_layer("dn_conv_w", l).rearrange("o j (r n) -> (o j r) n", n=P)).then_inc(vec_loaded, 16)
                sp.dma_start(hcol[:, 0:1], of_layer("dn_dt_bias", l).rearrange("o (h u) -> (o h) u", u=1)).then_inc(vec_loaded, 16)
                sp.dma_start(hcol[:, 1:2], of_layer("dn_a_log", l).rearrange("o (h u) -> (o h) u", u=1)).then_inc(vec_loaded, 16)
                b = LAYER1_TURNS * l
                ffn("ffn1_w_in", "ffn1_w_out", l, b)
                for r in range(MIX1_UNITS):
                    kind, _, c0, n = mix1_unit(r)
                    w = {"wa": "w_branch_a", "wb": "w_branch_b", "wo": "w_out"}.get(kind, "w_in")
                    load(b + NCH, r, cols(w, l, c0, n), 8, n)
                ffn("ffn2_w_in", "ffn2_w_out", l, b + (FFN_UNITS + MIX1_UNITS) // RING)

            with sp.Fori(0, DEPTH) as l:
                sp.wait_ge(x_ready, 3 * l + (3 * DEPTH - 1))
                sp.sem_inc(loads_begun, 1)
                sp.wait_ge(vec_taken, l + DEPTH)
                sp.wait_ge(zeroed, 1)
                sp.dma_start(attn[:].rearrange("p (g q) -> p g q", g=4),
                             of_layer("gmlp_w_s_2", l).rearrange("o g p q -> p (o g) q")).then_inc(vec_loaded, 16)
                sp.dma_start(lmat[:, 0:S], of_layer("gmlp_v_norm_2", l).partition_broadcast(P).rearrange("p o n -> p (o n)")).then_inc(vec_loaded, 16)
                for at, name, n in ((V2_MIX, "mix_norm_2", 8), (V2_CQ, "mla_q_norm_2", 2), (V2_CKV, "mla_kv_norm_2", 1),
                                    (V2_ON, "out_norm_2", 8), (V2_MEMX, "mem_x_norm_2", 8), (V2_MEMKV, "mem_kv_norm_2", 8),
                                    (V2_FFN, "ffn_norm_2", 8), (V2_CB, "ffn_conv_b_2", 44)):
                    sp.dma_start(stage[at:at + n, 0, :], of_layer(name, l).rearrange("o (r n) -> (o r) n", n=P)).then_inc(vec_loaded, 16)
                for at, name in ((V2_GQ, "gqa_q_norm_2"), (V2_GK, "gqa_k_norm_2")):
                    for half in range(2):
                        sp.dma_start(stage[at:at + 1, 0, 64 * half:64 * half + 64], of_layer(name, l)).then_inc(vec_loaded, 16)
                sp.dma_start(stage[V2_BS:V2_BS + 4, 0, :], of_layer("gmlp_b_s_2", l).rearrange("o g p -> (o g) p")).then_inc(vec_loaded, 16)
                taps = of_layer("ffn_conv_w_2", l).rearrange("o j (r n) -> (o j) r n", n=P)
                for j in range(3):
                    dst = stage[44 * (j % 2):44 * (j % 2) + 44, 1 + j // 2, :]
                    sp.dma_start(dst, taps[j]).then_inc(vec_loaded, 16)
                b = LAYER2_TURNS * l + DEPTH * LAYER1_TURNS
                for r, (c0, n) in enumerate(W2_COLS):
                    if r in (2, 3):
                        load_heads(b, r, of_layer("w_in_2", l)[:, 512 * (r - 2):512 * (r - 1), c0:c0 + n])
                    else:
                        load(b, r, cols("w_in_2", l, c0, n), 8, n)
                load(b, 7, rows("mla_w_uq_2", l, 0, 256), 2, 576)
                load(b, 8, rows("mla_w_ukv_2", l, 0, 128), 1, 768)
                for m in range(4):
                    load(b, 9 + m, cols("w_out_2", l, 256 * m, 256), 8, 256)
                for m in range(3):
                    load(b, 13 + m, cols("mem_w_kv_2", l, 256 * m, 256), 8, 256)
                sp.wait_ge(x_ready, 3 * l + (3 * DEPTH + 1))
                sp.dma_start(memx, a["mem_2"].rearrange("o (t p) d -> p (o t) d", p=P)).then_inc(mem_loaded, 16)
                load(b, 16, cols("mem_w_kv_2", l, 768, 256), 8, 256)
                for m in range(2):
                    load(b, 17 + m, cols("mem_w_q_2", l, 256 * m, 256), 8, 256)
                for m in range(2):
                    load(b, 19 + m, cols("mem_w_o_2", l, 512 * m, 512), 4, 512)
                ffn("ffn_w_up_2", "ffn_w_down_2", l, b + MIX2_UNITS // RING)

            sp.wait_ge(x_ready, 6 * DEPTH - 1)
            sp.dma_start(gain_row, a["final_norm_2"].partition_broadcast(P)).then_inc(start_loaded, 16)
            for t in range(ST):
                sp.wait_ge(out_ready, t + 1)
                sp.dma_start(out.rearrange("o (t p) d -> p (o t) d", p=P)[:, t, :], result[:, t, :]).then_inc(out_stored, 16)
            sp.wait_ge(out_stored, 16 * ST)

        @block.gpsimd
        def _(pool):
            pool.sem_inc(lo_ready, RING)
            with pool.Fori(0, DEPTH * (LAYER1_TURNS + LAYER2_TURNS)) as turn:
                for slot in range(RING):
                    pool.wait_ge(hi_ready, RING * turn + (slot + 1))
                    nc.gpsimd.tensor_tensor(lo[:, slot, :], raw[:, slot, :], hi[:, slot, :].bitcast(F32),
                                            ALU.subtract).then_inc(lo_ready, 1)

        @block.tensor
        def _(pe):
            pe.sem_inc(unit_done, RING)
            pe.wait_ge(start_loaded, 32)
            mm = nc.tensor.matmul

            def weights(k, kk, n):
                slot = k % RING
                return [w[:, slot, 0:kk * n].rearrange("p (k n) -> p k n", k=kk) for w in (hi, lo)]

            def arrived(b, k):
                pe.wait_ge(lo_ready, RING * b + (k + RING + 1))

            def product(dst, pairs, first=True, last=True):
                n = 0
                for (ah, al), (bh, bl) in pairs:
                    for s, m in ((ah, bh), (al, bh), (ah, bl)):
                        ins = mm(dst, s, m, start=first and n == 0, stop=last and n == 3 * len(pairs) - 1)
                        n += 1
                return ins

            def feature_major(b, k, src, bank, n=256, kk=8, at=0):
                arrived(b, k)
                wh, wl = weights(k, kk, n)
                for i in range(n // P):
                    ins = product(ps[:, bank, at + i * S:at + (i + 1) * S],
                                  [((wh[:, c, i * P:(i + 1) * P], wl[:, c, i * P:(i + 1) * P]), (src[0][:, c, :], src[1][:, c, :])) for c in range(kk)])
                return ins

            def token_major(b, k, src, dst, n=256, kk=8, c0=0, w=256):
                arrived(b, k)
                wh, wl = weights(k, kk, n)
                for t in range(ST):
                    tt = slice(t * P, (t + 1) * P)
                    ins = product(dst(t), [((src[0][:, c, tt], src[1][:, c, tt]), (wh[:, c, c0:c0 + w], wl[:, c, c0:c0 + w])) for c in range(kk)])
                return ins

            hT, oT = (hT_h, hT_l), (o_h, o_l)

            def transposes(q):
                pe.wait_ge(xn_ready, ST * q + ST)
                for g in range(4):
                    for i in range(2):
                        for t in range(ST):
                            k = 2 * g + i
                            ins = nc.tensor.transpose(ps[:, g, i * S + t * P:i * S + (t + 1) * P], tok[:, t, k * P:(k + 1) * P], ident)
                    ins.then_inc(tr_ready, 1)

            def ffn(f, b, q, gate_read, G0):
                pe.wait_ge(h_ready, 4 * q + 4)
                F0 = NCH * f

                def up(bb, k, bank):
                    feature_major(bb, k, hT, bank).then_inc(unit_done, 1)

                def down(bb, k, first, last):
                    arrived(bb, k)
                    wh, wl = weights(k, 2, D)
                    for t in range(ST):
                        for n in range(2):
                            pairs = []
                            for i in range(2):
                                c = slice(i * S + t * P, i * S + (t + 1) * P)
                                e = slice(n * 512, (n + 1) * 512)
                                pairs.append(((act_h[:, c], act_l[:, c]), (wh[:, i, e], wl[:, i, e])))
                            ins = product(ps[:, 4 + 2 * t + n, :], pairs, first, last)
                    ins.then_inc(unit_done, 1)

                up(b, 0, 0)
                up(b, 1, 1)
                pe.wait_ge(gate_read, G0 + 1)
                up(b, 2, 0)
                pe.wait_ge(up_used, F0 + 1)
                up(b, 3, 1)
                pe.wait_ge(act_ready, F0 + 1)
                down(b, 4, True, False)
                with pe.Fori(1, NCH - 1) as j:
                    pe.wait_ge(gate_read, G0 + j + 1)
                    up(b + j, 2, 0)
                    pe.wait_ge(up_used, F0 + j + 1)
                    up(b + j, 3, 1)
                    pe.wait_ge(act_ready, F0 + j + 1)
                    down(b + j, 4, False, False)
                pe.wait_ge(act_ready, F0 + NCH)
                down(b + (NCH - 1), 2, False, True)

            def columns(n, loads, tiles):
                pe.wait_ge(vec_loaded, loads)
                pe.wait_ge(x_ready, 3 * n)
                for i in range(tiles):
                    ins = nc.tensor.transpose(ps[:, 7, i * P:(i + 1) * P], stage[:, i, :], ident)
                ins.then_inc(vec_taken, 1)

            def unit1(l, b, r):
                kind, c, _, n = mix1_unit(r)
                bank = r % 2
                if r >= 2:
                    pe.wait_ge(bank_free[bank], (26, 25)[bank] * l + r // 2)
                if kind == "wo":
                    pe.wait_ge(merged_ready, 4 * l + 4)
                if kind in ("wo", "sv"):
                    ins = token_major(b, r, hT, lambda t: ps[:, bank, t * S:(t + 1) * S])
                else:
                    ins = feature_major(b, r, oT if kind in ("wa", "wb") else hT, bank, n)
                ins.then_inc(unit_done, 1)

            def delta(l, c):
                g = NPAIR * l + c
                wa = lambda name: pe.wait_ge(dl_act, DELTA_ACT.at(g, name))
                wv = lambda name: pe.wait_ge(dl_dve, DELTA_DVE.at(g, name))
                heads = (2 * c, 2 * c + 1)
                probs = [(i, t) for i in range(2) for t in range(ST)]
                blk = lambda bank, p: ps[:, bank, p * P:(p + 1) * P]
                of = lambda buf, p: buf[:, p * P:(p + 1) * P]
                tile = lambda buf, p: buf[:, heads[probs[p][0]], probs[p][1] * P:(probs[p][1] + 1) * P]
                wa("sq")
                for i in range(2):
                    ins = mm(ps[:, 2 + i, :], cc("ones"), sq[:, i, :], start=True, stop=True)
                ins.then_inc(dl_pe, 1)
                for n, row in enumerate((g_r, beta_r, eg_r)):
                    for i, h in enumerate(heads):
                        ins = mm(ps[:, 4 + n, i * S:(i + 1) * S], ident[0:HEADS, h:h + 1].to_broadcast([HEADS, P]), row[:, :], start=True, stop=True)
                ins.then_inc(dl_pe, 1)
                yield
                wv("qkn")
                for p in range(4):
                    mm(blk(2, p), tile(kT, p), tile(kT, p), start=True, stop=True)
                    ins = mm(blk(3, p), tile(kT, p), tile(qT, p), start=True, stop=True)
                ins.then_inc(dl_pe, 1)
                for p in range(4):
                    nc.tensor.transpose(blk(7, p), tile(kT, p), ident)
                    ins = nc.tensor.transpose(blk(4, p), tile(vT, p), ident)
                ins.then_inc(dl_pe, 1)
                yield
                wv("lt")
                for p in range(4):
                    ins = nc.tensor.transpose(blk(2, p), of(yinv, p), ident)
                ins.then_inc(dl_pe, 1)
                yield
                for i in range(LEVELS):
                    wv(f"m{i}")
                    if i == 0:
                        wa("x")
                    else:
                        wv(f"t{i - 1}")
                    for p in range(4):
                        ins = mm(blk(3, p), of(mlev, p), of(xinv, p), start=True, stop=True)
                    ins.then_inc(dl_pe, 1)
                    yield
                    wa(f"p{i}")
                    for p in range(4):
                        ins = mm(blk(2, p), of(plev, p), of(yinv, p), start=True, stop=True)
                        if i < LEVELS - 1:
                            ins = mm(blk(5, p), of(yinv, p), of(plev, p), start=True, stop=True)
                    ins.then_inc(dl_pe, 1)
                    yield
                wv(f"t{LEVELS - 1}")
                wv("tok")
                for p in range(4):
                    mm(blk(2, p), of(yinv, p), of(u_v, p), start=True, stop=True)
                    ins = mm(blk(3, p), of(w_k, p), of(yinv, p), start=True, stop=True)
                ins.then_inc(dl_pe, 1)
                yield

                def push(ch):
                    t, half = divmod(ch, 2)
                    rr = slice(64 * half, 64 * half + 64)
                    for i in range(2):
                        p = 2 * i + t
                        ins = mm(ps[:, 4, i * P:(i + 1) * P], of(k_dec, p)[rr, :], of(u_v, p)[rr, :], start=True, stop=True)
                    ins.then_inc(dl_pe, 1)

                wa("uw")
                push(0)
                yield
                for ch in range(1, 4):
                    t, half = divmod(ch, 2)
                    rr = slice(64 * half, 64 * half + 64)
                    wv(f"s{ch - 1}")
                    for i in range(2):
                        ins = mm(ps[rr, 5, i * P:(i + 1) * P], of(w_k, 2 * i + t)[:, rr], state[:, ch - 1, i, :], start=True, stop=True)
                    ins.then_inc(dl_pe, 1)
                    yield
                    wv(f"v{ch}")
                    if ch < 3:
                        push(ch)
                        yield
                for p, (i, t) in enumerate(probs):
                    dst = ps[:, 6 + i, t * P:(t + 1) * P]
                    mm(dst, of(u_v, p), of(attn, p), start=True, stop=False)
                    for ch in (2 * t, 2 * t + 1):
                        if ch > 0:
                            c0 = (ch % 2) * CHUNK
                            ins = mm(ps[:, 6 + i, t * P + c0:t * P + c0 + CHUNK], state[:, ch - 1, i, :], of(q_dec, p)[:, c0:c0 + CHUNK],
                                     start=False, stop=ch % 2 == 1)
                ins.then_inc(dl_pe, 1)
                yield
                wa("osq")
                mm(ps[:, 2, :], cc("ones"), sq[:, 0, :], start=True, stop=True).then_inc(dl_pe, 1)

            def stick(l, c):
                g = NPAIR * l + c
                wa = lambda name: pe.wait_ge(sb_act, SB_ACT.at(g, name))
                wv = lambda name: pe.wait_ge(sb_dve, SB_DVE.at(g, name))
                heads = (2 * c, 2 * c + 1)
                wa("sq")
                for i in range(2):
                    ins = mm(ps[:, 2 + i, :], cc("ones"), sq[:, i, :], start=True, stop=True)
                ins.then_inc(sb_pe, 1)
                yield
                wv("qkn")
                for i, h in enumerate(heads):
                    mm(ps[:, 4 + i, 0:S], kT[:, h, 0:P], qT[:, h, :], start=True, stop=False, skip_group_check=True)
                    ins = mm(ps[:, 4 + i, S:S + P], kT[:, h, P:S], qT[:, h, P:S], start=False, stop=False, skip_group_check=True)
                ins.then_inc(sb_pe, 1)
                yield
                wv("nsp")
                for i in range(2):
                    n0 = rsf[:, 384 * i:384 * i + S]
                    n1 = rsf[:, 384 * i + S:384 * (i + 1)]
                    mm(ps[:, 4 + i, 0:S], cc("tri"), n0, start=False, stop=False, skip_group_check=True)
                    mm(ps[:, 4 + i, P:S], cc("ones"), n1, start=False, stop=False, skip_group_check=True)
                    ins = mm(ps[:, 4 + i, S:S + P], cc("tri"), n1, start=False, stop=True, skip_group_check=True)
                ins.then_inc(sb_pe, 1)
                yield
                wa("w")
                for i, h in enumerate(heads):
                    w0 = sqf[:, 384 * i:384 * i + S]
                    w1 = sqf[:, 384 * i + S:384 * (i + 1)]
                    hh = slice(h * P, (h + 1) * P)
                    mm(ps[:, 6, i * S:(i + 1) * S], tok[:, 0, hh], w0, start=True, stop=False, skip_group_check=True)
                    ins = mm(ps[:, 6, i * S + P:(i + 1) * S], tok[:, 1, hh], w1, start=False, stop=True, skip_group_check=True)
                ins.then_inc(sb_pe, 1)
                yield

            def with_units(steps, units, l, b, n):
                for at, _ in enumerate(steps):
                    for r in spread(units, n)[at] if at < n else ():
                        unit1(l, b, r)

            def mixer1(l, b, q):
                pe.wait_ge(h_ready, 4 * q + 4)
                unit1(l, b, 0)
                unit1(l, b, 1)
                pe.wait_ge(rows_dve, ROWS_DVE.at(l, "beg"))
                for n, row in enumerate((beta_r[:, :], g_r[:, :], sq[0:HEADS, 0, 0:S], sq[0:HEADS, 1, S:2 * S])):
                    for t in range(ST):
                        at = (n * ST + t) * HEADS
                        ins = mm(ps[:, 7, at:at + HEADS], row[:, t * P:(t + 1) * P], ident[0:HEADS, 0:HEADS], start=True, stop=True)
                ins.then_inc(rows_pe, 1)
                for r in range(2, 6):
                    unit1(l, b, r)
                for c in range(NPAIR):
                    with_units(delta(l, c), DELTA_BG[c], l, b, 20)
                for r in (27, 28, 29):
                    unit1(l, b, r)
                for c in range(NPAIR):
                    with_units(stick(l, c), SB_BG[c], l, b, 3)
                pe.wait_ge(sb_dve, SB_DVE.at(NPAIR * l + NPAIR - 1, "o"))
                for r in range(43, 51):
                    unit1(l, b, r)

            with pe.Fori(0, DEPTH) as l:
                b = LAYER1_TURNS * l
                columns(l, 16 * V1_LOADS * l + 16 * V1_LOADS, 1)
                transposes(3 * l)
                ffn(2 * l, b, 3 * l, sil_ready, 2 * NCH * l)
                transposes(3 * l + 1)
                mixer1(l, b + NCH, 3 * l + 1)
                transposes(3 * l + 2)
                ffn(2 * l + 1, b + (FFN_UNITS + MIX1_UNITS) // RING, 3 * l + 2, sil_ready, 2 * NCH * l + NCH)

            def scores_order(n):
                return ["s0"] + sum([([f"s{i + 1}"] if i + 1 < n else []) + [f"t{i}", f"v{i}"] for i in range(n)], [])

            def weights_out(pbuf, beta):
                for i in range(2):
                    for kt in range(ST):
                        for t in range(ST):
                            ins = nc.tensor.transpose(ps[:, (4, 6)[beta % 2] + i, kt * S + t * P:kt * S + (t + 1) * P],
                                                      pbuf[:, (i * ST + t) * S + kt * P:(i * ST + t) * S + (kt + 1) * P], ident)
                return ins

            def mixer2(l, b, q):
                wa = lambda name: pe.wait_ge(m2_act, M2_ACT.at(l, name))
                wv = lambda name: pe.wait_ge(m2_dve, M2_DVE.at(l, name))
                col = lambda v, k, c0, n: tuple(w[:, k, c0:c0 + n] for w in v)
                pe.wait_ge(h_ready, 4 * q + 4)
                feature_major(b, 0, hT, 0).then_inc(unit_done, 1)
                arrived(b, 1)
                w = weights(1, 8, 160)
                hb = lambda c: (hT_h[:, c, :], hT_l[:, c, :])
                product(ps[:, 1, 0:S], [(col(w, c, 0, P), hb(c)) for c in range(KB)])
                product(ps[0:96, 1, S:2 * S], [(col(w, c, 64, 96), hb(c)) for c in range(KB)]).then_inc(unit_done, 1)
                for u in (2, 3):
                    arrived(b, u)
                    w = weights(u, 4, 384)
                    for j in range(3):
                        pairs = []
                        for c in range(4):
                            pairs.append((col(w, c, P * j, P), hb(4 * (u - 2) + c)))
                        ins = product(ps[:, 2 + j, 0:S], pairs, u == 2, u == 3)
                    ins.then_inc(unit_done, 1)
                arrived(b, 4)
                w = weights(4, 8, 256)
                product(ps[:, 5, 0:S], [(col(w, c, 0, P), hb(c)) for c in range(KB)])
                for t in range(ST):
                    tt_ = slice(t * P, (t + 1) * P)
                    ins = product(ps[:, 5, S + t * P:S + (t + 1) * P],
                                  [((hT_h[:, c, tt_], hT_l[:, c, tt_]), col(w, c, P, P)) for c in range(KB)])
                ins.then_inc(unit_done, 1)
                for u in (5, 6):
                    token_major(b, u, hT, lambda t: ps[:, u + 1, t * S:(t + 1) * S]).then_inc(unit_done, 1)
                wa("sq")
                flat = lambda v: v.rearrange("p k n -> p (k n)")
                mm(ps[:, 0, 0:S], cc("ones"), kT[:, 0, :], start=True, stop=False)
                mm(ps[:, 0, 0:S], cc("ones"), kT[:, 1, :], start=False, stop=True)
                mm(ps[:, 0, S:2 * S], cc("ones"), kT[:, 2, :], start=True, stop=True)
                mm(ps[:, 2, :], cc("halves"), flat(kT[:, 3:5, :]), start=True, stop=True)
                mm(ps[:, 3, :], cc("halves"), flat(kT[:, 5:7, :]), start=True, stop=True).then_inc(m2_pe, 1)
                wv("gn")
                mm(ps[:, 2, :], cc("rot"), flat(qT[:, 0:2, :]), start=True, stop=True)
                mm(ps[:, 3, :], cc("rot"), flat(qT[:, 2:4, :]), start=True, stop=True)
                mm(ps[0:96, 4, 0:S], cc("rot")[64:96, 0:96], zT[64:96, 3, :], start=True, stop=True).then_inc(m2_pe, 1)
                wa("gv")
                arrived(b, 7)
                w = weights(7, 2, 576)
                QB, KBANK = (0, 1, 5), (4, 6, 7)
                for h in range(MLA_H):
                    ins = product(ps[0:96, QB[h // 2], (h % 2) * S:(h % 2 + 1) * S], [(col(w, c, 96 * h, 96), (o_h[:, c, :], o_l[:, c, :])) for c in range(2)])
                ins.then_inc(unit_done, 1)
                wa("gelu")
                wv("gr")
                arrived(b, 8)
                w = weights(8, 1, 768)
                for h in range(MLA_H):
                    product(ps[:, KBANK[h // 2], (h % 2) * S:(h % 2 + 1) * S], [(col(w, 0, P * h, P), (o_h[:, 2, :], o_l[:, 2, :]))])
                for t in range(ST):
                    tt_ = slice(t * P, (t + 1) * P)
                    vals = tuple(v[:, 0, :].rearrange("p (h e) -> p h e", h=MLA_H)[:, :, NOPE:P] for v in w)
                    ins = product(ps[:, 2 + t, 0:384], [((o_h[:, 2, tt_], o_l[:, 2, tt_]), vals)])
                ins.then_inc(unit_done, 1)
                wa("qa")
                for j in range(3):
                    ins = mm(ps[0:96, QB[j], :], cc("rot")[0:96, 0:96], flat(kT[0:96, 2 * j:2 * j + 2, :]), start=True, stop=True)
                ins.then_inc(m2_pe, 1)
                wa("kv")
                for g in range(4):
                    ins = nc.tensor.transpose(ps[:, 4, g * P:(g + 1) * P], attn[:, g * P:(g + 1) * P], ident)
                ins.then_inc(m2_pe, 1)
                wa("wst")
                wv("vn")
                for t in range(ST):
                    for g in range(4):
                        c0 = t * S + g * 64
                        ins = mm(ps[:, 6, c0:c0 + 64], plev[:, g * P:(g + 1) * P], yinv[:, c0:c0 + 64], start=True, stop=True)
                ins.then_inc(m2_pe, 1)
                for step in scores_order(M2_BATCHES):
                    kind, beta = step[0], int(step[1:])
                    bank = 2 * (beta % 2)
                    if kind == "s":
                        wv("qr" if beta < 2 else f"o{beta - 2}")
                        for i in range(2):
                            for t in range(ST):
                                tt_ = slice(t * P, (t + 1) * P)
                                if beta < 3:
                                    left, right = kT[0:96, 2 * beta + i, tt_], vT[0:96, 2 * beta + i, :]
                                else:
                                    r = slice(64 * i, 64 * i + 64)
                                    left, right = qT[r, beta - 3, tt_], qT[r, 3, :]
                                ins = mm(ps[:, bank + i, t * S:(t + 1) * S], left, right, start=True, stop=True)
                        ins.then_inc(m2_pe, 1)
                    elif kind == "t":
                        wa(f"e{beta}")
                        if beta == 1:
                            wv("mix")
                        weights_out((sqf, rsf)[beta % 2], beta).then_inc(m2_pe, 1)
                    else:
                        wa(f"pt{beta}")
                        buf = (qT[:, 4:8, :], zT[:, 0:4, :])[beta % 2]
                        for i in range(2):
                            for t in range(ST):
                                dst = ps[:, bank, (i * ST + t) * 64:(i * ST + t + 1) * 64]
                                for kt in range(ST):
                                    if beta < 3:
                                        c0 = kt * 384 + 64 * (2 * beta + i)
                                        val = flat(zT[:, 4:7, :])[:, c0:c0 + 64]
                                    else:
                                        val = decay[:, kt * P + 64 * i:kt * P + 64 * i + 64]
                                    ins = mm(dst, buf[:, i * ST + kt, t * P:(t + 1) * P], val, start=kt == 0, stop=kt == ST - 1)
                        ins.then_inc(m2_pe, 1)
                transposes(q + 1)
                pe.wait_ge(h_ready, 4 * q + 8)
                for m in range(4):
                    if m >= 2:
                        pe.wait_ge(added, 3 * l + m - 1)
                    token_major(b, 9 + m, hT, lambda t: ps[:, 4 + m % 2, t * S:(t + 1) * S]).then_inc(unit_done, 1)

            def memory(l, b, q):
                wa = lambda name: pe.wait_ge(me_act, ME_ACT.at(l, name))
                wv = lambda name: pe.wait_ge(me_dve, ME_DVE.at(l, name))
                transposes(q + 2)
                pe.wait_ge(h_ready, 4 * q + 12)
                for m in range(2):
                    feature_major(b, 13 + m, oT, 4 + m).then_inc(unit_done, 1)
                for m in range(2):
                    token_major(b, 15 + m, oT, lambda t: ps[:, 6 + m, t * S:(t + 1) * S]).then_inc(unit_done, 1)
                transposes(q + 3)
                pe.wait_ge(h_ready, 4 * q + 16)
                wa("kv1")
                for m in range(2):
                    feature_major(b, 17 + m, hT, 4 + m).then_inc(unit_done, 1)
                for step in scores_order(ME_BATCHES):
                    kind, beta = step[0], int(step[1:])
                    bank = 2 * (beta % 2)
                    if kind == "s":
                        wa("q1")
                        for i in range(2):
                            h = 2 * beta + i
                            for t in range(ST):
                                ins = mm(ps[:, bank + i, t * S:(t + 1) * S], qT[:, h, t * P:(t + 1) * P], kT[:, h, :], start=True, stop=True)
                        ins.then_inc(me_pe, 1)
                    elif kind == "t":
                        wv(f"pn{beta}")
                        weights_out((sqf, rsf)[beta % 2], beta).then_inc(me_pe, 1)
                    else:
                        wa(f"pt{beta}")
                        buf = (kT[:, 4:8, :], zT[:, 0:4, :])[beta % 2]
                        for i in range(2):
                            h = 2 * beta + i
                            for kt in range(ST):
                                val = mem_v[:, kt, h * P:(h + 1) * P]
                                ins = mm(ps[:, bank, i * S:(i + 1) * S], val, buf[:, i * ST + kt, :], start=kt == 0, stop=kt == ST - 1)
                        ins.then_inc(me_pe, 1)
                wv(f"ol{ME_BATCHES - 1}")
                for m in range(2):
                    token_major(b, 19 + m, hT, lambda t: ps[:, 4 + 2 * m + t, :], n=512, kk=4, w=512).then_inc(unit_done, 1)

            with pe.Fori(0, DEPTH) as l:
                b = LAYER2_TURNS * l + DEPTH * LAYER1_TURNS
                q = 5 * l + 3 * DEPTH
                columns(l + DEPTH, 16 * V2_LOADS * l + 16 * (V1_LOADS * DEPTH + V2_LOADS), 3)
                transposes(q)
                mixer2(l, b, q)
                memory(l, b, q)
                transposes(q + 4)
                ffn(l + 2 * DEPTH, b + MIX2_UNITS // RING, q + 4, gate_used, NCH * l)

        @block.scalar
        def _(act):
            own = Own(act, act_own)
            fn = nc.scalar.activation
            LOGS = "natural_log_exp_and_others"

            def split(b, k):
                slot = k % RING
                act.wait_ge(raw_loaded[slot], 16 * b + 16 * (k // RING + 1))
                act.wait_ge(unit_done, RING * b + (k + 1))
                fn(hi[:, slot, :], raw[:, slot, :], ACT.Copy).then_inc(hi_ready, 1)

            def rsqrt(dst, src, scale, to=None):
                own.link(fn(dst, src, ACT.Ln, bias=eps_t[:, 0:1], scale=scale))
                return fn(dst, dst, ACT.Exp, scale=-0.5)

            def stats(n, src, x_updates, junk=junk):
                act.wait_ge(x_ready, x_updates)
                for t in range(ST):
                    ins = fn(junk[:, t, :], src[:, t, :], ACT.Square, accum_out=ss[:, t:t + 1])
                own.link(ins)
                rsqrt(rstd[:, 0:ST], ss[:, 0:ST], 1.0 / D).then_inc(rstd_ready, 1)

            def high(q, gain, dst):
                for g in range(4):
                    act.wait_ge(tr_ready, 4 * q + (g + 1))
                    for i in range(2):
                        k = 2 * g + i
                        ins = fn(dst[:, k, :], ps[:, g, i * S:(i + 1) * S], ACT.Copy, scale=gain(k))
                    ins.then_inc(hh_ready, 1)

            def ffn(f, b):
                F0 = NCH * f

                def silu(bb, k, j):
                    act.wait_ge(unit_done, RING * bb + (k + RING + 1))
                    if j is not None:
                        act.wait_ge(up_used, F0 + j)
                    fn(sil[:], ps[:, 0, :], ACT.Silu).then_inc(sil_ready, 1)

                split(b, 2)
                split(b, 3)
                silu(b, 0, None)
                split(b, 4)
                split(b, 5)
                silu(b, 2, 1)
                split(b, 6)
                with act.Fori(1, NCH - 2) as j:
                    split(b + j, 4)
                    split(b + j, 5)
                    silu(b + j, 2, j + 1)
                    split(b + j, 6)
                split(b + (NCH - 2), 4)
                split(b + (NCH - 2), 5)
                silu(b + (NCH - 2), 2, NCH - 1)

            def evac1(l, r):
                kind, c, _, n = mix1_unit(r)
                bank = r % 2
                src = ps[:, bank, 0:2 * n]
                two = src.rearrange("p (k n) -> p k n", n=S)
                sl = slice(2 * c, 2 * c + 2)
                if kind == "z":
                    dst, v = zT[:, sl, :], two
                elif kind in ("sq", "sk"):
                    dst, v = (qT if kind == "sq" else kT)[:, sl, :], two
                elif kind == "sv":
                    dst, v = tok[:, :, S * c:S * (c + 1)], two
                elif kind == "wa":
                    dst, v = vT[:, sl, :], two
                elif kind in ("ga", "gb"):
                    k0 = 2 * c + (1 if r == 42 else 0)
                    dst, v = zT[:, k0:k0 + n // P, :], two
                else:
                    return
                if kind == "gb":
                    act.wait_ge(gated_a, l + 1)
                act.wait_ge(unit_done, RING * b_of(l) + (r + RING + 1))
                fn(dst, v, ACT.Copy).then_inc(bank_free[bank], 1)

            def b_of(l):
                return LAYER1_TURNS * l + NCH

            def freed(l, r):
                act.wait_ge(bank_free[r % 2], (26, 25)[r % 2] * l + (r // 2 + 1))

            def delta(l, c):
                g = NPAIR * l + c
                wp = lambda name: act.wait_ge(dl_pe, DELTA_PE.at(g, name))
                wv = lambda name: act.wait_ge(dl_dve, DELTA_DVE.at(g, name))
                sl = slice(2 * c, 2 * c + 2)
                for r in range(2 + 4 * c, 6 + 4 * c):
                    freed(l, r)
                for buf in (qT, kT, vT, zT):
                    ins = fn(buf[:, sl, :], buf[:, sl, :], ACT.Silu)
                ins.then_inc(dl_act, 1)
                act.preload_act_table_set(LOGS)
                act.wait_ge(dl_act, DELTA_ACT.at(g, "silu"))
                act.wait_ge(dl_dve, DELTA_DVE.count * g)
                act.wait_ge(rows_dve, ROWS_DVE.at(l, "cols"))
                fn(sq[:, 0, :].rearrange("p (k n) -> p k n", n=S), qT[:, sl, :], ACT.Square)
                fn(sq[:, 1, :].rearrange("p (k n) -> p k n", n=S), kT[:, sl, :], ACT.Square).then_inc(dl_act, 1)
                wp("sums")
                rsqrt(rs[:], ps[:, 2:4, :], 1.0).then_inc(dl_act, 1)
                wv("diff")
                fn(decay[:], decay[:], ACT.Exp).then_inc(dl_act, 1)
                yield
                yield
                wp("xt")
                fn(xinv[:], ps[:, 2, :], ACT.Copy).then_inc(dl_act, 1)
                yield
                for i in range(LEVELS):
                    wp(f"p{i}")
                    fn(plev[:], ps[:, 3, :], ACT.Copy).then_inc(dl_act, 1)
                    yield
                    yield
                wp("uw")
                fn(u_v[:], ps[:, 2, :], ACT.Copy)
                fn(w_k[:], ps[:, 3, :], ACT.Copy).then_inc(dl_act, 1)
                yield
                for _ in range(6):
                    yield
                wp("o")
                fn(sq[:, 0, :].rearrange("p (k n) -> p k n", n=S), ps[:, 6:8, 0:S], ACT.Square).then_inc(dl_act, 1)
                wp("osum")
                rsqrt(rs[:, 0, :], ps[:, 2, :], 1.0 / P).then_inc(dl_act, 1)
                yield

            def stick(l, c):
                g = NPAIR * l + c
                wp = lambda name: act.wait_ge(sb_pe, SB_PE.at(g, name))
                wv = lambda name: act.wait_ge(sb_dve, SB_DVE.at(g, name))
                sl = slice(2 * c, 2 * c + 2)
                soft = sqf[:, 0:768]
                for r in range(18 + 3 * c, 21 + 3 * c):
                    freed(l, r)
                act.wait_ge(sb_dve, SB_DVE.count * g)
                fn(sq[:, 0, :].rearrange("p (k n) -> p k n", n=S), qT[:, sl, :], ACT.Square)
                fn(sq[:, 1, :].rearrange("p (k n) -> p k n", n=S), kT[:, sl, :], ACT.Square).then_inc(sb_act, 1)
                wp("sums")
                rsqrt(rs[:], ps[:, 2:4, :], 1.0 / P).then_inc(sb_act, 1)
                yield
                wp("z")
                own.link(fn(soft.rearrange("p (i n) -> p i n", i=2), ps[:, 4:6, 0:384], ACT.Abs))
                own.link(fn(soft, soft, ACT.Exp, scale=-1.0))
                fn(soft, soft, ACT.Ln, bias=1.0).then_inc(sb_act, 1)
                yield
                wv("ex")
                fn(soft, soft, ACT.Exp).then_inc(sb_act, 1)
                yield
                wp("pv")
                fn(o_h[:, sl, :], ps[:, 6, :].rearrange("p (k n) -> p k n", n=S), ACT.Copy).then_inc(sb_act, 1)
                yield

            def with_units(steps, units, l, b, n):
                late = []
                for at, _ in enumerate(steps):
                    for r in late:
                        evac1(l, r)
                    late = spread(units, n)[at] if at < n else []
                    for r in late:
                        if r + 2 < MIX1_UNITS:
                            split(b, r + 2)
                for r in late:
                    evac1(l, r)

            def plain(l, b, units):
                for r in units:
                    if r + 2 < MIX1_UNITS:
                        split(b, r + 2)
                    evac1(l, r)

            def mixer1(l, b):
                split(b, 2)
                act.wait_ge(unit_done, RING * b + (0 + RING + 1))
                fn(beta_r[:, :], ps[0:HEADS, 0, 0:S], ACT.Exp, scale=-1.0).then_inc(bank_free[0], 1)
                split(b, 3)
                freed(l, 1)
                y, e = sq[0:HEADS, 0, 0:S], sq[0:HEADS, 0, S:2 * S]
                own.link(fn(e, y, ACT.Abs))
                own.link(fn(e, e, ACT.Exp, scale=-1.0))
                fn(hcol[:, 2:3], hcol[:, 1:2], ACT.Exp)
                fn(e, e, ACT.Ln, bias=1.0).then_inc(rows_act, 1)
                act.wait_ge(rows_dve, ROWS_DVE.at(l, "g"))
                fn(eg_r[:, :], g_r[:, :], ACT.Exp)
                d = sq[0:HEADS, 1, S:2 * S]
                fn(d, d, ACT.Exp).then_inc(rows_act, 1)
                plain(l, b, range(2, 6))
                for c in range(NPAIR):
                    with_units(delta(l, c), DELTA_BG[c], l, b, 20)
                act.wait_ge(dl_dve, DELTA_DVE.count * (NPAIR * l) + DELTA_DVE.count * NPAIR)
                plain(l, b, (27, 28, 29))
                for c in range(NPAIR):
                    with_units(stick(l, c), SB_BG[c], l, b, 3)
                    if c == 1:
                        freed(l, 36)
                        freed(l, 37)
                        fn(zT[:], zT[:], ACT.Sigmoid).then_inc(gate_a, 1)
                        act.preload_act_table_set(LOGS)
                freed(l, 41)
                freed(l, 42)
                fn(zT[:], zT[:], ACT.Sigmoid).then_inc(gate_b, 1)
                act.preload_act_table_set(LOGS)
                plain(l, b, range(43, 51))

            act.wait_ge(start_loaded, 32)
            act.wait_ge(eps_ready, 1)
            with act.Fori(0, DEPTH) as l:
                own.restart()
                b = LAYER1_TURNS * l
                act.preload_act_table_set(LOGS)
                stats(3 * l, x, 3 * l)
                split(b, 0)
                split(b, 1)
                act.wait_ge(vec_ready, l + 1)
                high(3 * l, lambda k: vec1[:, V1_FFN1 + k:V1_FFN1 + k + 1], hT_h)
                ffn(2 * l, b)
                act.preload_act_table_set(LOGS)
                stats(3 * l + 1, x, 3 * l + 1)
                split(b + NCH, 0)
                split(b + NCH, 1)
                high(3 * l + 1, lambda k: vec1[:, V1_MIX + k:V1_MIX + k + 1], hT_h)
                mixer1(l, b + NCH)
                stats(3 * l + 2, x, 3 * l + 2)
                b2 = b + (FFN_UNITS + MIX1_UNITS) // RING
                split(b2, 0)
                split(b2, 1)
                high(3 * l + 2, lambda k: vec1[:, V1_FFN2 + k:V1_FFN2 + k + 1], hT_h)
                ffn(2 * l + 1, b2)

            def done(b, r):
                act.wait_ge(unit_done, RING * b + (r + RING + 1))

            def two_next(b, r):
                if r + 2 < MIX2_UNITS:
                    split(b, r + 2)

            def mixer2(l, b):
                wp = lambda name: act.wait_ge(m2_pe, M2_PE.at(l, name))
                wv = lambda name: act.wait_ge(m2_dve, M2_DVE.at(l, name))
                sig = lambda ins: ins.then_inc(m2_act, 1)
                two = lambda v: v.rearrange("p (k n) -> p k n", n=S)
                act.wait_ge(heads_loaded[0], 80 * l + 80)
                two_next(b, 0)
                done(b, 0)
                fn(zT[:, 0:2, :], two(ps[:, 0, :]), ACT.Copy)
                fn(kT[:, 0:2, :], two(ps[:, 0, :]), ACT.Square)
                act.wait_ge(heads_loaded[1], 80 * l + 80)
                two_next(b, 1)
                done(b, 1)
                fn(zT[:, 2, :], ps[:, 1, 0:S], ACT.Copy)
                fn(kT[:, 2, :], ps[:, 1, 0:S], ACT.Square)
                fn(zT[64:96, 3, :], ps[64:96, 1, S:2 * S], ACT.Copy)
                two_next(b, 2)
                two_next(b, 3)
                done(b, 3)
                fn(qT[:, 0:3, :], ps[:, 2:5, 0:S], ACT.Copy)
                fn(kT[:, 3:6, :], ps[:, 2:5, 0:S], ACT.Square)
                two_next(b, 4)
                done(b, 4)
                fn(qT[:, 3, :], ps[:, 5, 0:S], ACT.Copy)
                sig(fn(kT[:, 6, :], ps[:, 5, 0:S], ACT.Square))
                sig(fn(decay[:, 0:S], ps[:, 5, S:2 * S], ACT.Copy))
                two_next(b, 5)
                two_next(b, 6)
                wp("sums")
                e1 = eps_t[:, 0:1]
                fn(vT[:, 0, :], ps[:, 0, 0:S], ACT.Ln, bias=e1, scale=1.0 / 256)
                fn(vT[:, 1, :], ps[:, 0, S:2 * S], ACT.Ln, bias=e1, scale=1.0 / 128)
                own.link(fn(vT[:, 2:6, :], ps[:, 2:4, :].rearrange("p b (k n) -> p (b k) n", n=S), ACT.Ln, bias=e1, scale=1.0 / 64))
                sig(fn(vT[:, 0:6, :], vT[:, 0:6, :], ACT.Exp, scale=-0.5))
                done(b, 6)
                fn(xinv[:], ps[:, 6, :], ACT.Gelu_apprx_tanh)
                sig(fn(yinv[:], ps[:, 7, :], ACT.Gelu_apprx_tanh))
                act.preload_act_table_set(LOGS)
                act.wait_ge(m2_act, M2_ACT.at(l, "gelu"))
                for t in range(ST):
                    ins = fn(mlev[:, t * S:(t + 1) * S], yinv[:, t * S:(t + 1) * S], ACT.Square, accum_out=ss[:, t:t + 1])
                own.link(ins)
                sig(rsqrt(rstd[:, 0:ST], ss[:, 0:ST], 1.0 / 256))
                two_next(b, 7)
                done(b, 7)
                fn(kT[0:96, 0:4, :], ps[0:96, 0:2, :].rearrange("p b (k n) -> p (b k) n", n=S), ACT.Copy)
                sig(fn(kT[0:96, 4:6, :], two(ps[0:96, 5, :]), ACT.Copy))
                two_next(b, 8)
                done(b, 8)
                fn(vT[0:64, 0:2, :], two(ps[0:64, 4, :]), ACT.Copy)
                fn(vT[0:64, 2:6, :], ps[0:64, 6:8, :].rearrange("p b (k n) -> p (b k) n", n=S), ACT.Copy)
                vals = zT[:, 4:7, :].rearrange("p k n -> p (k n)").rearrange("p (t n) -> p t n", t=ST)
                sig(fn(vals, ps[:, 2:4, 0:384], ACT.Copy))
                wp("wst")
                sig(fn(plev[:], ps[:, 4, :], ACT.Copy))
                attention(l, M2_BATCHES, wp, wv, sig, lambda n: (MLA_DK if n < 3 else 64) ** -0.5, (qT[:, 4:8, :], zT[:, 0:4, :]))
                wv(f"o{M2_BATCHES - 1}")
                segs = ((0, 384), (384, 768), (768, D))
                for i, (c0, c1) in enumerate(segs):
                    for t in range(ST):
                        ins = fn(junk[:, t, c0:c1], tok[:, t, c0:c1], ACT.Square, accum_out=ss[:, 2 * i + t:2 * i + t + 1])
                own.link(ins)
                for i, (c0, c1) in enumerate(segs):
                    ins = fn(rstd[:, 2 * i:2 * i + 2], ss[:, 2 * i:2 * i + 2], ACT.Ln, bias=e1, scale=1.0 / (c1 - c0))
                own.link(ins)
                sig(fn(rstd[:, 0:6], rstd[:, 0:6], ACT.Exp, scale=-0.5))

            def attention(l, n, wp, wv, sig, scale, pts, after=None):
                def weigh(beta):
                    wv(f"mx{beta}")
                    pbuf = (sqf, rsf)[beta % 2]
                    for i in range(2 * ST):
                        ins = fn(pbuf[:, i * S:(i + 1) * S], ps[:, 2 * (beta % 2) + i // ST, (i % ST) * S:(i % ST + 1) * S], ACT.Exp,
                                 bias=negmax[:, beta % 2, i:i + 1], scale=scale(beta), accum_out=psum_p[:, beta % 2, i:i + 1])
                    sig(ins)

                weigh(0)
                for beta in range(n):
                    if beta + 1 < n:
                        weigh(beta + 1)
                    wp(f"t{beta}")
                    bank = (4, 6)[beta % 2]
                    sig(fn(pts[beta % 2], ps[:, bank:bank + 2, :].rearrange("p b (k n) -> p (b k) n", n=S), ACT.Copy))
                    if after:
                        after(beta)

            def memory(l, b, n, q):
                wp = lambda name: act.wait_ge(me_pe, ME_PE.at(l, name))
                wv = lambda name: act.wait_ge(me_dve, ME_DVE.at(l, name))
                sig = lambda ins: ins.then_inc(me_act, 1)
                two = lambda v: v.rearrange("p (k n) -> p k n", n=S)
                for m in range(2):
                    two_next(b, 13 + m)
                    done(b, 13 + m)
                    sig(fn(kT[:, 2 * m:2 * m + 2, :], two(ps[:, 4 + m, :]), ACT.Copy))
                for m in range(2):
                    two_next(b, 15 + m)
                    done(b, 15 + m)
                    sig(fn(mem_v[:, :, S * m:S * (m + 1)], two(ps[:, 6 + m, :]), ACT.Copy))
                stats(n, x, 3 * l + (3 * DEPTH + 1), memx)
                high(q + 3, gain2(V2_MEMX), hT_h)
                for m in range(2):
                    two_next(b, 17 + m)
                    done(b, 17 + m)
                    sig(fn(qT[:, 2 * m:2 * m + 2, :], two(ps[:, 4 + m, :]), ACT.Copy))

                def out_high(beta):
                    wp(f"v{beta}")
                    sig(fn(hT_h[:, 2 * beta:2 * beta + 2, :], two(ps[:, 2 * beta, :]), ACT.Copy))

                attention(l, ME_BATCHES, wp, wv, sig, lambda n: P ** -0.5, (kT[:, 4:8, :], zT[:, 0:4, :]), out_high)

            def conv_ffn(l, b):
                F0, G0 = NCH * l + 2 * NCH * DEPTH, NCH * l

                def silu(j):
                    act.wait_ge(gate_used, G0 + j + 1)
                    act.wait_ge(act_ready, F0 + j)
                    fn(sil[:], decay[:], ACT.Silu).then_inc(sil_ready, 1)

                split(b, 2)
                split(b, 3)
                silu(0)
                split(b, 4)
                split(b, 5)
                silu(1)
                split(b, 6)
                with act.Fori(1, NCH - 2) as j:
                    split(b + j, 4)
                    split(b + j, 5)
                    silu(j + 1)
                    split(b + j, 6)
                split(b + (NCH - 2), 4)
                split(b + (NCH - 2), 5)
                silu(NCH - 1)

            def gain2(at):
                return lambda k: vec2[:, at + k:at + k + 1]

            with act.Fori(0, DEPTH) as l:
                own.restart()
                b = LAYER2_TURNS * l + DEPTH * LAYER1_TURNS
                n, q = 4 * l + 3 * DEPTH, 5 * l + 3 * DEPTH
                act.preload_act_table_set(LOGS)
                stats(n, x, 3 * l + 3 * DEPTH)
                split(b, 0)
                split(b, 1)
                act.wait_ge(vec_ready, l + (DEPTH + 1))
                high(q, gain2(V2_MIX), hT_h)
                mixer2(l, b)
                high(q + 1, gain2(V2_ON), hT_h)
                for r in range(9, 13):
                    two_next(b, r)
                act.wait_ge(mem_loaded, 16 * l + 16)
                stats(n + 1, memx, 3 * l + (3 * DEPTH + 1))
                high(q + 2, gain2(V2_MEMKV), o_h)
                memory(l, b, n + 2, q)
                stats(n + 3, x, 3 * l + (3 * DEPTH + 2))
                bf = b + MIX2_UNITS // RING
                split(bf, 0)
                split(bf, 1)
                high(q + 4, gain2(V2_FFN), hT_h)
                conv_ffn(l, bf)
            stats(7 * DEPTH, x, 6 * DEPTH)

        @block.vector
        def _(dve):
            own = Own(dve, dve_own)
            V = nc.vector
            tt, stt, ts = V.tensor_tensor, V.scalar_tensor_tensor, V.tensor_scalar

            def scaled(src, n):
                dve.wait_ge(rstd_ready, n + 1)
                for t in range(ST):
                    ts(tok[:, t, :], src[:, t, :], rstd[:, t:t + 1], None, ALU.mult).then_inc(xn_ready, 1)

            def low(q, gain, dst_h, dst_l):
                for g in range(4):
                    dve.wait_ge(hh_ready, 4 * q + (g + 1))
                    for i in range(2):
                        k = 2 * g + i
                        ins = stt(out=dst_l[:, k, :], in0=ps[:, g, i * S:(i + 1) * S], scalar=gain(k), in1=dst_h[:, k, :].bitcast(F32),
                                  op0=ALU.mult, op1=ALU.subtract)
                    ins.then_inc(h_ready, 1)

            def halve(h, l_, src):
                own.link(V.tensor_copy(h, src))
                return tt(l_, src, h.bitcast(F32), ALU.subtract)

            def columns(n, dst, tiles):
                dve.wait_ge(vec_taken, n + 1)
                V.tensor_copy(dst, ps[:, 7, 0:tiles * P]).then_inc(vec_ready, 1)

            def add_half_ffn(b, half):
                dve.wait_ge(unit_done, RING * b + (FFN_UNITS + RING))
                for t in range(ST):
                    for n in range(2):
                        c = slice(n * 512, (n + 1) * 512)
                        ins = stt(out=x[:, t, c], in0=ps[:, 4 + 2 * t + n, :], scalar=half, in1=x[:, t, c], op0=ALU.mult, op1=ALU.add)
                ins.then_inc(x_ready, 1)

            def ffn(f, b):
                F0 = NCH * f

                def chunk(bb, ku, kd, j):
                    dve.wait_ge(act_ready, F0 + j)
                    dve.wait_ge(sil_ready, F0 + j + 1)
                    dve.wait_ge(unit_done, RING * bb + (ku + RING + 1))
                    tt(prod[:], sil[:], ps[:, 1, :], ALU.mult).then_inc(up_used, 1)
                    dve.wait_ge(up_used, F0 + j + 1)
                    if kd is not None:
                        dve.wait_ge(unit_done, RING * bb + (kd + RING + 1))
                    own.link(V.tensor_copy(act_h, prod[:]))
                    tt(act_l, prod[:], act_h.bitcast(F32), ALU.subtract).then_inc(act_ready, 1)

                chunk(b, 1, None, 0)
                chunk(b, 3, 4, 1)
                with dve.Fori(1, NCH - 1) as j:
                    own.restart()
                    chunk(b + j, 3, 4, j + 1)
                own.restart()
                add_half_ffn(b, 0.5)

            def freed(l, r):
                dve.wait_ge(bank_free[r % 2], (26, 25)[r % 2] * l + (r // 2 + 1))

            def evac1(l, b, r):
                kind, c, _, n = mix1_unit(r)
                bank = r % 2
                sl = slice(2 * c, 2 * c + 2)
                if kind in ("z", "sq", "sk", "sv", "wa", "ga", "gb", "b"):
                    return
                dve.wait_ge(unit_done, RING * b + (r + RING + 1))
                src = ps[:, bank, :].rearrange("p (k n) -> p k n", n=S)
                if kind in ("q", "k", "v"):
                    dst = {"q": qT, "k": kT, "v": vT}[kind]
                    w = lambda j, i: vec1[:, V1_CONV + 24 * j + 8 * "qkv".index(kind) + 2 * c + i:][:, 0:1]
                    for i in range(2):
                        ins = ts(dst[:, 2 * c + i, :], src[:, i, :], w(3, i), None, ALU.mult)
                    own.link(ins)
                    for j in (2, 1, 0):
                        d = 3 - j
                        for i in range(2):
                            o = dst[:, 2 * c + i, d:S]
                            ins = stt(out=o, in0=src[:, i, 0:S - d], scalar=w(j, i), in1=o, op0=ALU.mult, op1=ALU.add)
                        if j:
                            own.link(ins)
                    ins.then_inc(bank_free[bank], 1)
                elif kind == "wb":
                    if r == 43:
                        dve.wait_ge(gate_b, l + 1)
                    t1 = sqf[:, 0:512]
                    t2 = rsf[:, 0:512]
                    k2 = lambda v: v.rearrange("p (k n) -> p k n", n=S)
                    tt(k2(t1), zT[:, sl, :], src, ALU.mult).then_inc(bank_free[bank], 1)
                    freed(l, r)
                    own.link(tt(k2(t2), k2(t1), vT[:, sl, :], ALU.add))
                    halve(hT_h[:, sl, :], hT_l[:, sl, :], k2(t2)).then_inc(merged_ready, 1)
                else:
                    cc_ = slice(S * c, S * (c + 1))
                    if r < MIX1_UNITS - 1:
                        tt(x[:, :, cc_], x[:, :, cc_], src, ALU.add).then_inc(bank_free[bank], 1)
                    else:
                        tt(x[:, 0, cc_], x[:, 0, cc_], src[:, 0, :], ALU.add).then_inc(bank_free[bank], 1)
                        tt(x[:, 1, cc_], x[:, 1, cc_], src[:, 1, :], ALU.add).then_inc(x_ready, 1)

            def delta(l, c):
                g = NPAIR * l + c
                wp = lambda name: dve.wait_ge(dl_pe, DELTA_PE.at(g, name))
                wa = lambda name: dve.wait_ge(dl_act, DELTA_ACT.at(g, name))
                me = lambda name: dve.wait_ge(dl_dve, DELTA_DVE.at(g, name))
                heads = (2 * c, 2 * c + 1)
                sl = slice(2 * c, 2 * c + 2)
                probs = [(i, t) for i in range(2) for t in range(ST)]
                of = lambda buf, p: buf[:, p * P:(p + 1) * P]
                col = lambda kind, p: tcol[:, kind, probs[p][1], heads[probs[p][0]]:heads[probs[p][0]] + 1]
                four = lambda v: v.rearrange("p (k n) -> p k n", n=P)
                two = lambda v: v.rearrange("p (k n) -> p k n", n=S)
                q, k = qT[:, sl, :], kT[:, sl, :]
                wp("rows")
                V.tensor_copy(egl[:], ps[:, 6, :].rearrange("p (i c n) -> p i c n", i=2, c=4)[:, :, :, CHUNK - 1])
                for p in range(4):
                    ins = ts(of(decay, p), ps[:, 4, p * P:(p + 1) * P], col(1, p), 0.0, ALU.subtract, ALU.min)
                ins.then_inc(dl_dve, 1)
                wa("rs")
                stt(out=q, in0=q, scalar=float(P) ** -0.5, in1=two(rs[:, 0, :]), op0=ALU.mult, op1=ALU.mult)
                tt(k, k, two(rs[:, 1, :]), ALU.mult).then_inc(dl_dve, 1)
                yield
                wa("decay")
                own.link(tt(four(decay[:]), four(decay[:]), over(cc("chunk"), 4), ALU.mult))
                wp("gram")
                tt(lmat[:], decay[:], ps[:, 2, :], ALU.mult)
                own.link(tt(attn[:], decay[:], ps[:, 3, :], ALU.mult))
                own.link(tt(lmat[:], lmat[:], ps[:, 5, :], ALU.mult))
                own.link(tt(four(mlev[:]), four(lmat[:]), over(cc("inv0"), 4), ALU.mult))
                tt(four(yinv[:]), over(ident, 4), four(mlev[:]), ALU.subtract).then_inc(dl_dve, 1)
                me("lt")
                tt(four(mlev[:]), four(lmat[:]), over(cc("inv1"), 4), ALU.mult).then_inc(dl_dve, 1)
                yield
                wp("tok")
                for p in range(4):
                    ts(of(u_v, p), ps[:, 4, p * P:(p + 1) * P], col(0, p), None, ALU.mult)
                    ts(of(w_k, p), ps[:, 7, p * P:(p + 1) * P], col(2, p), None, ALU.mult)
                    ts(of(k_dec, p), ps[:, 7, p * P:(p + 1) * P], col(3, p), None, ALU.mult)
                tt(two(q_dec[:]), q, two(ps[:, 6, :]), ALU.mult).then_inc(dl_dve, 1)
                yield
                for i in range(LEVELS):
                    if i + 1 < LEVELS:
                        wp(f"p{i}")
                        tt(four(mlev[:]), four(lmat[:]), over(cc(f"inv{i + 2}"), 4), ALU.mult).then_inc(dl_dve, 1)
                    yield
                    wp(f"q{i}")
                    if i + 1 < LEVELS:
                        tt(xinv[:], xinv[:], ps[:, 5, :], ALU.subtract)
                    tt(yinv[:], yinv[:], ps[:, 2, :], ALU.subtract).then_inc(dl_dve, 1)
                    yield
                yield
                pair = lambda buf, rr, t: buf[rr, :].rearrange("p (i t n) -> p i t n", i=2, t=2)[:, :, t, :]
                wp("kv0")
                V.tensor_copy(state[:, 0, :, :], ps[:, 4, 0:S].rearrange("p (i n) -> p i n", i=2)).then_inc(dl_dve, 1)
                yield
                for ch in range(1, 4):
                    t, half = divmod(ch, 2)
                    rr = slice(64 * half, 64 * half + 64)
                    wp(f"ws{ch}")
                    u = pair(u_v, rr, t)
                    tt(u, u, ps[rr, 5, 0:S].rearrange("p (i n) -> p i n", i=2), ALU.subtract).then_inc(dl_dve, 1)
                    yield
                    if ch < 3:
                        wp(f"kv{ch}")
                        me(f"s{ch - 1}")
                        for i in range(2):
                            ins = stt(out=state[:, ch, i, :], in0=state[:, ch - 1, i, :], scalar=egl[:, i, ch:ch + 1],
                                      in1=ps[:, 4, i * P:(i + 1) * P], op0=ALU.mult, op1=ALU.add)
                        ins.then_inc(dl_dve, 1)
                        yield
                wa("ors")
                t1 = sq[:, 1, :]
                for i in range(2):
                    ins = stt(out=t1[:, i * S:(i + 1) * S], in0=ps[:, 6 + i, 0:S], scalar=vec1[:, V1_ON:V1_ON + 1], in1=rs[:, 0, i * S:(i + 1) * S],
                              op0=ALU.mult, op1=ALU.mult)
                own.link(ins)
                own.link(tt(two(t1), two(t1), zT[:, sl, :], ALU.mult))
                halve(o_h[:, sl, :], o_l[:, sl, :], two(t1)).then_inc(dl_dve, 1)
                yield

            def stick(l, c):
                g = NPAIR * l + c
                wp = lambda name: dve.wait_ge(sb_pe, SB_PE.at(g, name))
                wa = lambda name: dve.wait_ge(sb_act, SB_ACT.at(g, name))
                sl = slice(2 * c, 2 * c + 2)
                two = lambda v: v.rearrange("p (k n) -> p k n", n=S)
                pair = lambda v: v.rearrange("p (i n) -> p i n", i=2)
                soft, neg = sqf[:, 0:768], rsf[:, 0:768]
                wa("rs")
                stt(out=qT[:, sl, :], in0=qT[:, sl, :], scalar=gcol[:, 0:1], in1=two(rs[:, 0, :]), op0=ALU.mult, op1=ALU.mult)
                stt(out=kT[:, sl, :], in0=kT[:, sl, :], scalar=vec1[:, V1_SBK:V1_SBK + 1], in1=two(rs[:, 1, :]),
                    op0=ALU.mult, op1=ALU.mult).then_inc(sb_dve, 1)
                yield
                wa("soft")
                own.link(stt(out=pair(neg), in0=ps[:, 4:6, 0:384], scalar=0.0, in1=pair(soft), op0=ALU.max, op1=ALU.add))
                tt(pair(neg), pair(neg), over(cc("sbneg"), 2), ALU.mult).then_inc(sb_dve, 1)
                yield
                wp("tri")
                stt(out=pair(soft), in0=ps[:, 4:6, 0:384], scalar=0.0, in1=over(cc("sbadd"), 2), op0=ALU.min, op1=ALU.add).then_inc(sb_dve, 1)
                yield
                wa("o")
                tt(o_l[:, sl, :], two(ps[:, 6, :]), o_h[:, sl, :].bitcast(F32), ALU.subtract).then_inc(sb_dve, 1)
                yield

            def with_units(steps, units, l, b, n):
                late = []
                for at, _ in enumerate(steps):
                    for r in late:
                        evac1(l, b, r)
                    late = spread(units, n)[at] if at < n else []
                for r in late:
                    evac1(l, b, r)

            def mixer1(l, b):
                h8 = slice(0, HEADS)
                y, e = sq[h8, 0, 0:S], sq[h8, 0, S:2 * S]
                dve.wait_ge(unit_done, RING * b + (1 + RING + 1))
                ts(y, ps[h8, 1, 0:S], hcol[:, 0:1], None, ALU.add).then_inc(bank_free[1], 1)
                freed(l, 0)
                own.link(ts(beta_r[:, :], beta_r[:, :], 1.0, None, ALU.add))
                own.link(V.reciprocal(beta_r[:, :], beta_r[:, :]))
                dve.wait_ge(rows_act, ROWS_ACT.at(l, "ln"))
                freed(l, 1)
                g0, d = sq[h8, 1, 0:S], sq[h8, 1, S:2 * S]
                own.link(stt(out=g0, in0=y, scalar=0.0, in1=e, op0=ALU.max, op1=ALU.add))
                own.link(ts(g0, g0, hcol[:, 2:3], -1.0, ALU.mult, ALU.mult))
                own.link(V.tensor_tensor_scan(out=g_r[:, :], data0=cc("scan")[h8, :], data1=g0, initial=0.0, op0=ALU.mult, op1=ALU.add))
                gc = g_r[:, :].rearrange("h (c n) -> h c n", n=CHUNK)
                tt(d.rearrange("h (c n) -> h c n", n=CHUNK), gc[:, :, CHUNK - 1:CHUNK].to_broadcast([HEADS, 4, CHUNK]), gc,
                   ALU.subtract).then_inc(rows_dve, 1)
                dve.wait_ge(rows_act, ROWS_ACT.at(l, "eg"))
                tt(y, beta_r[:, :], eg_r[:, :], ALU.mult).then_inc(rows_dve, 1)
                dve.wait_ge(rows_pe, l + 1)
                V.tensor_copy(tcol[:].rearrange("p a t h -> p (a t h)"), ps[:, 7, 0:4 * ST * HEADS]).then_inc(rows_dve, 1)
                dve.wait_ge(rows_dve, ROWS_DVE.at(l, "cols"))
                for r in range(2, 6):
                    evac1(l, b, r)
                for c in range(NPAIR):
                    with_units(delta(l, c), DELTA_BG[c], l, b, 20)
                for c in range(NPAIR):
                    with_units(stick(l, c), SB_BG[c], l, b, 3)
                    if c == 1:
                        dve.wait_ge(gate_a, l + 1)
                        tt(vT[:], vT[:], zT[:], ALU.mult).then_inc(gated_a, 1)
                        dve.wait_ge(gated_a, l + 1)
                for r in range(43, 51):
                    evac1(l, b, r)

            V.memset(stage[:], 0.0).then_inc(zeroed, 1)
            V.memset(eps_t[:], EPS).then_inc(eps_ready, 1)
            dve.wait_ge(start_loaded, 32)
            with dve.Fori(0, DEPTH) as l:
                own.restart()
                b = LAYER1_TURNS * l
                columns(l, vec1[:, :], 1)
                dve.wait_ge(vec_ready, l + 1)
                ts(gcol[:, 0:1], vec1[:, V1_SBQ:V1_SBQ + 1], float(P) ** -0.5, None, ALU.mult)
                scaled(x, 3 * l)
                low(3 * l, lambda k: vec1[:, V1_FFN1 + k:V1_FFN1 + k + 1], hT_h, hT_l)
                ffn(2 * l, b)
                dve.wait_ge(x_ready, 3 * l + 1)
                scaled(x, 3 * l + 1)
                low(3 * l + 1, lambda k: vec1[:, V1_MIX + k:V1_MIX + k + 1], hT_h, hT_l)
                mixer1(l, b + NCH)
                dve.wait_ge(x_ready, 3 * l + 2)
                scaled(x, 3 * l + 2)
                low(3 * l + 2, lambda k: vec1[:, V1_FFN2 + k:V1_FFN2 + k + 1], hT_h, hT_l)
                ffn(2 * l + 1, b + (FFN_UNITS + MIX1_UNITS) // RING)
                dve.wait_ge(x_ready, 3 * l + 3)

            def mixer2(l, b, q):
                wp = lambda name: dve.wait_ge(m2_pe, M2_PE.at(l, name))
                wa = lambda name: dve.wait_ge(m2_act, M2_ACT.at(l, name))
                me = lambda name: dve.wait_ge(m2_dve, M2_DVE.at(l, name))
                sig = lambda ins: ins.then_inc(m2_dve, 1)
                v2 = lambda c: vec2[:, c:c + 1]
                wa("rs")
                for k in range(3):
                    ins = stt(out=zT[:, k, :], in0=zT[:, k, :], scalar=v2(V2_CQ + k), in1=vT[:, (0, 0, 1)[k], :], op0=ALU.mult, op1=ALU.mult)
                own.link(ins)
                sig(halve(o_h[:, 0:3, :], o_l[:, 0:3, :], zT[:, 0:3, :]))
                for j in range(4):
                    ins = stt(out=qT[:, j, :], in0=qT[:, j, :], scalar=v2(V2_GK if j == 3 else V2_GQ), in1=vT[:, 2 + j, :], op0=ALU.mult, op1=ALU.mult)
                sig(ins)
                wp("rope")
                me("gn")
                r = slice(64, 96)
                t1 = rs[r, 0, 0:S]
                tt(t1, ps[r, 4, 0:S], cc("sina")[r, :], ALU.mult)
                own.link(tt(zT[r, 3, :], zT[r, 3, :], cc("cosa")[r, :], ALU.mult))
                own.link(tt(zT[r, 3, :], zT[r, 3, :], t1, ALU.add))
                sig(V.tensor_copy(vT[r, 0:6, :], over(zT[r, 3, :], 6)))
                turned = sqf.rearrange("p (k n) -> p k n", n=S)
                tt(turned, ps[:, 2:4, :].rearrange("p b (k n) -> p (b k) n", n=S), over(cc("sinb"), 4), ALU.mult)
                own.link(tt(qT[:, 0:4, :], qT[:, 0:4, :], over(cc("cosb"), 4), ALU.mult))
                sig(tt(qT[:, 0:4, :], qT[:, 0:4, :], turned, ALU.add))
                wp("qrope")
                h = slice(0, 96)
                turned = tok[h].rearrange("p t (k n) -> p (t k) n", n=S)[:, 0:6, :]
                tt(turned[:, 0:4, :], ps[h, 0:2, :].rearrange("p b (k n) -> p (b k) n", n=S), over(cc("sina")[h, :], 4), ALU.mult)
                tt(turned[:, 4:6, :], ps[h, 5, :].rearrange("p (k n) -> p k n", n=S), over(cc("sina")[h, :], 2), ALU.mult)
                own.link(tt(kT[h, 0:6, :], kT[h, 0:6, :], over(cc("cosa")[h, :], 6), ALU.mult))
                sig(tt(kT[h, 0:6, :], kT[h, 0:6, :], turned, ALU.add))
                wa("vrs")
                for t in range(ST):
                    c = slice(t * S, (t + 1) * S)
                    ins = stt(out=yinv[:, c], in0=yinv[:, c], scalar=rstd[:, t:t + 1], in1=lmat[:, 0:S], op0=ALU.mult, op1=ALU.mult)
                sig(ins)
                wp("mix")
                me("qr")
                for t in range(ST):
                    for g in range(4):
                        c = slice(t * S + 64 * g, t * S + 64 * g + 64)
                        ins = stt(out=tok[:, t, 768 + 64 * g:832 + 64 * g], in0=ps[:, 6, c], scalar=v2(V2_BS + g), in1=xinv[:, c], op0=ALU.add, op1=ALU.mult)
                sig(ins)

                def top(beta):
                    maxima(beta, wp, sig, MLA_DK if beta < 3 else 64)

                top(0)
                for beta in range(M2_BATCHES):
                    if beta + 1 < M2_BATCHES:
                        top(beta + 1)
                    wp(f"v{beta}")
                    w = beta % 2
                    own.link(V.reciprocal(rinv[:, w, :], psum_p[:, w, :]))
                    for i in range(2):
                        c0 = 64 * (2 * beta + i) if beta < 3 else 384 + 64 * (beta - 3 + 3 * i)
                        ins = tt(tok[:, :, c0:c0 + 64], ps[:, 2 * w, 128 * i:128 * (i + 1)].rearrange("p (t e) -> p t e", t=ST),
                                 rinv[:, w, 2 * i:2 * i + 2].unsqueeze(2).to_broadcast([P, ST, 64]), ALU.mult)
                    sig(ins)
                wa("seg")
                me(f"o{M2_BATCHES - 1}")
                for t in range(ST):
                    for i, (c0, c1) in enumerate(((0, 384), (384, 768), (768, D))):
                        ins = ts(tok[:, t, c0:c1], tok[:, t, c0:c1], rstd[:, 2 * i + t:2 * i + t + 1], None, ALU.mult)
                    ins.then_inc(xn_ready, 1)
                low(q + 1, gain2(V2_ON), hT_h, hT_l)
                for m in range(4):
                    dve.wait_ge(unit_done, RING * b + (9 + m + RING + 1))
                    c = slice(S * m, S * (m + 1))
                    src = ps[:, 4 + m % 2, :].rearrange("p (t n) -> p t n", n=S)
                    tt(x[:, :, c], x[:, :, c], src, ALU.add).then_inc(added if m < 3 else x_ready, 1)

            def maxima(beta, wp, sig, dk):
                wp(f"s{beta}")
                w = beta % 2
                own.link(V.tensor_reduce(negmax[:, w, :], ps[:, 2 * w:2 * w + 2, :].rearrange("p b (t n) -> p (b t) n", n=S), AX_X, ALU.max))
                sig(ts(negmax[:, w, :], negmax[:, w, :], -float(dk) ** -0.5, None, ALU.mult))

            def memory(l, b, n, q):
                wp = lambda name: dve.wait_ge(me_pe, ME_PE.at(l, name))
                wa = lambda name: dve.wait_ge(me_act, ME_ACT.at(l, name))
                sig = lambda ins: ins.then_inc(me_dve, 1)
                scaled(memx, n + 1)
                low(q + 2, gain2(V2_MEMKV), o_h, o_l)
                scaled(x, n + 2)
                low(q + 3, gain2(V2_MEMX), hT_h, hT_l)
                maxima(0, wp, sig, P)
                for beta in range(ME_BATCHES):
                    if beta + 1 < ME_BATCHES:
                        maxima(beta + 1, wp, sig, P)
                    w = beta % 2
                    pbuf = (sqf, rsf)[w]
                    wa(f"e{beta}")
                    own.link(V.reciprocal(rinv[:, w, :], psum_p[:, w, :]))
                    for i in range(2 * ST):
                        ins = ts(pbuf[:, i * S:(i + 1) * S], pbuf[:, i * S:(i + 1) * S], rinv[:, w, i:i + 1], None, ALU.mult)
                    sig(ins)
                    wa(f"oh{beta}")
                    sl = slice(2 * beta, 2 * beta + 2)
                    sig(tt(hT_l[:, sl, :], ps[:, 2 * beta, :].rearrange("p (k n) -> p k n", n=S), hT_h[:, sl, :].bitcast(F32), ALU.subtract))
                dve.wait_ge(unit_done, RING * b + (20 + RING + 1))
                for m in range(2):
                    c = slice(512 * m, 512 * (m + 1))
                    ins = tt(x[:, :, c], x[:, :, c], ps[:, 4 + 2 * m:6 + 2 * m, :], ALU.add)
                ins.then_inc(x_ready, 1)

            def conv_ffn(l, b):
                F0, G0 = NCH * l + 2 * NCH * DEPTH, NCH * l

                def convolve(dst, bank, blk):
                    for i in range(2):
                        c0, src = i * S, ps[:, bank, i * S:(i + 1) * S]
                        ins = ts(dst[:, c0:c0 + S], src, vcol(V2_TAP[1], blk, i), vcol(V2_CB, blk, i), ALU.mult, ALU.add)
                    own.link(ins)
                    for i in range(2):
                        c0 = i * S
                        o = dst[:, c0 + 1:c0 + S]
                        ins = stt(out=o, in0=ps[:, bank, c0:c0 + S - 1], scalar=vcol(V2_TAP[0], blk, i), in1=o, op0=ALU.mult, op1=ALU.add)
                    own.link(ins)
                    for i in range(2):
                        c0 = i * S
                        o = dst[:, c0:c0 + S - 1]
                        ins = stt(out=o, in0=ps[:, bank, c0 + 1:c0 + S], scalar=vcol(V2_TAP[2], blk, i), in1=o, op0=ALU.mult, op1=ALU.add)
                    return ins

                def vcol(at, blk, i):
                    return vec2[:, bass.ds(blk + (at + i), 1)]

                def chunk(bb, kg, ku, kd, j):
                    dve.wait_ge(unit_done, RING * bb + (kg + RING + 1))
                    dve.wait_ge(sil_ready, F0 + j)
                    dve.wait_ge(act_ready, F0 + j)
                    convolve(decay, 0, 2 * j).then_inc(gate_used, 1)
                    dve.wait_ge(unit_done, RING * bb + (ku + RING + 1))
                    convolve(mlev, 1, 2 * j + FB).then_inc(up_used, 1)
                    dve.wait_ge(sil_ready, F0 + j + 1)
                    dve.wait_ge(up_used, F0 + j + 1)
                    own.link(tt(prod[:], sil[:], mlev[:], ALU.mult))
                    if kd is not None:
                        dve.wait_ge(unit_done, RING * bb + (kd + RING + 1))
                    own.link(V.tensor_copy(act_h, prod[:]))
                    tt(act_l, prod[:], act_h.bitcast(F32), ALU.subtract).then_inc(act_ready, 1)

                chunk(b, 0, 1, None, 0)
                chunk(b, 2, 3, 4, 1)
                with dve.Fori(1, NCH - 1) as j:
                    own.restart()
                    chunk(b + j, 2, 3, 4, j + 1)
                own.restart()
                add_half_ffn(b, 1.0)

            def gain2(at):
                return lambda k: vec2[:, at + k:at + k + 1]

            with dve.Fori(0, DEPTH) as l:
                own.restart()
                b = LAYER2_TURNS * l + DEPTH * LAYER1_TURNS
                n, q = 4 * l + 3 * DEPTH, 5 * l + 3 * DEPTH
                columns(l + DEPTH, vec2[:, :], 3)
                scaled(x, n)
                dve.wait_ge(vec_ready, l + (DEPTH + 1))
                low(q, gain2(V2_MIX), hT_h, hT_l)
                mixer2(l, b, q)
                memory(l, b, n, q)
                scaled(x, n + 3)
                low(q + 4, gain2(V2_FFN), hT_h, hT_l)
                conv_ffn(l, b + MIX2_UNITS // RING)
                dve.wait_ge(x_ready, 3 * l + (3 * DEPTH + 3))
            dve.wait_ge(rstd_ready, 7 * DEPTH + 1)
            dve.wait_ge(start_loaded, 48)
            for t in range(ST):
                stt(out=result[:, t, :], in0=x[:, t, :], scalar=rstd[:, t:t + 1], in1=gain_row, op0=ALU.mult, op1=ALU.mult).then_inc(out_ready, 1)


def kernel(**inputs):
    import numpy as _np
    import concourse.bacc as _bacc
    from concourse import mybir as _mybir
    from concourse.bass_utils import run_bass_kernel_spmd as _run

    nc = _bacc.Bacc("TRN2", target_bir_lowering=False, num_devices=1)
    arrays, args = {}, {}

    def give(name, value):
        arrays[name] = value
        return nc.dram_tensor(name, value.shape, _mybir.dt.from_np(value.dtype), kind="ExternalInput").ap()

    for name, value in inputs.items():
        args[name] = give(f"in_{name}", _np.ascontiguousarray(value))
    const = give("const", constants())
    out = nc.dram_tensor("out", (1, S, D), F32, kind="ExternalOutput").ap()
    build_program(nc, args, const, out)
    r = _run(nc, [arrays], core_ids=[0])
    return r.results[0]["out"]
```

```python
from contextlib import ExitStack
from itertools import chain

import numpy as np

import concourse.bass as bass
from concourse import mybir

F32 = mybir.dt.float32
F32R = mybir.dt.float32r
ALU = mybir.AluOpType
ACT = mybir.ActivationFunctionType
AX_X = mybir.AxisListType.X

P = 128
D = 1024
S = 256
ST = S // P
KB = D // P
DFF = 2816
FB = DFF // P
NCH = FB // 2
DEPTH = 2
RING = 3
UNIT = 2048
EPS = 1e-6

HEADS = 8
CHUNK = 64
NPAIR = HEADS // 2
B_COL = 4 * D
A_COL = B_COL + HEADS
SB_COL = A_COL + HEADS
GA_COL = SB_COL + 3 * D
GB_COL = GA_COL + D
FFN_UNITS = 3 * NCH
V1_FFN1, V1_MIX, V1_FFN2, V1_CONV, V1_ON, V1_SBQ, V1_SBK = 0, 8, 16, 24, 120, 121, 122
V1_LOADS = 9

MLA_H, GQA_H = 6, 6
MLA_DK, NOPE, ROPE = 96, 64, 32
MIX2_UNITS = 9 + 4 + 4 + 2 + 2
LAYER2_TURNS = (MIX2_UNITS + FFN_UNITS) // RING
V2_MIX, V2_CQ, V2_CKV, V2_GQ, V2_GK, V2_ON, V2_MEMX, V2_MEMKV, V2_FFN, V2_CB, V2_BS = 0, 8, 10, 11, 12, 13, 21, 29, 37, 45, 89
V2_TAP = (128, 128 + 44, 256)
V2_LOADS = 18
W2_COLS = [(0, 256), (256, 160), (416, 384), (416, 384), (800, 256), (1056, 256), (1312, 256)]

CONSTS = ["ident", "ones", "halves", "tri", "rot", "chunk", "inv0", "inv1", "inv2", "inv3", "inv4", "inv5",
          "sbneg", "sbadd", "cosa", "sina", "cosb", "sinb", "scan"]
CONST_W = {"sbneg": 384, "sbadd": 384, "cosa": 256, "sina": 256, "cosb": 256, "sinb": 256, "scan": 256}
CONST_AT, _w = {}, 0
for _name in CONSTS:
    CONST_AT[_name] = (_w, CONST_W.get(_name, 128))
    _w += CONST_W.get(_name, 128)
CONST_TOTAL = _w


def constants():
    c = np.zeros((P, CONST_TOTAL), np.float32)

    def put(name, value):
        at, w = CONST_AT[name]
        c[:value.shape[0], at:at + value.shape[1]] = value

    j, i = np.arange(P)[:, None], np.arange(P)[None, :]
    put("ident", (j == i).astype(np.float32))
    put("ones", np.ones((P, P), np.float32))
    put("halves", (j // 64 == i // 64).astype(np.float32))
    put("tri", (j >= i).astype(np.float32))
    rot = np.zeros((P, P), np.float32)
    rot[np.arange(1, P, 2), np.arange(0, P, 2)] = -1.0
    rot[np.arange(0, P, 2), np.arange(1, P, 2)] = 1.0
    put("rot", rot)
    put("chunk", ((j // CHUNK == i // CHUNK) & (j <= i)).astype(np.float32))
    for n in range(6):
        s = 1 << n
        put(f"inv{n}", ((j // (2 * s) == i // (2 * s)) & ((i // s) % 2 == 1) & ((j // s) % 2 == 0)).astype(np.float32))
    before = (j < i).astype(np.float32)
    full = np.concatenate([before, np.ones((P, P), np.float32), before], axis=1)
    put("sbneg", -full)
    put("sbadd", np.where(full > 0, 0.0, -1e30).astype(np.float32))

    def table(d_rot):
        t = np.arange(S, dtype=np.float32)
        row, col = np.floor(t / 64), t % 64
        n = d_rot // 4
        inv = (np.float32(10000.0) ** (-np.arange(n, dtype=np.float32) / np.float32(n))).astype(np.float32)
        ang = np.concatenate([row[:, None] * inv, col[:, None] * inv], axis=-1).astype(np.float32)
        return np.repeat(np.cos(ang), 2, axis=1).T.astype(np.float32), np.repeat(np.sin(ang), 2, axis=1).T.astype(np.float32)

    ca, sa = table(ROPE)
    put("cosa", np.concatenate([np.ones((NOPE, S), np.float32), ca]))
    put("sina", np.concatenate([np.zeros((NOPE, S), np.float32), sa]))
    cb, sbb = table(64)
    put("cosb", np.concatenate([cb, cb]))
    put("sinb", np.concatenate([sbb, sbb]))
    put("scan", np.broadcast_to((np.arange(S) % CHUNK != 0).astype(np.float32), (P, S)))
    return c


class Steps:

    def __init__(self, names):
        self.names = list(names)
        assert len(set(self.names)) == len(self.names)
        self.count = len(self.names)

    def at(self, stage, name):
        return self.count * stage + (self.names.index(name) + 1)


class Own:

    def __init__(self, eng, sem):
        self.eng, self.sem, self.n = eng, sem, 0

    def restart(self):
        self.eng.sem_clear(self.sem)
        self.n = 0

    def link(self, ins):
        self.n += 1
        ins.then_inc(self.sem, 1)
        self.eng.wait_ge(self.sem, self.n)


LEVELS = 5
DELTA_PE = Steps(["rows", "eg", "gram", "tok", "xt"] + [f"{a}{i}" for i in range(LEVELS) for a in "pq"]
                 + ["uw", "kv0", "ws1", "kv1", "ws2", "kv2", "ws3", "o", "osum"])
PRE_ACT = Steps(["sq", "rs"])
HALVES = 2 * NPAIR
DELTA_ACT = Steps(["decay", "x"] + [f"p{i}" for i in range(LEVELS)] + ["uw", "osq", "ors"])
DELTA_DVE = Steps(["diff", "lt", "m0"]
                  + sum([[f"m{i + 1}" if i + 1 < LEVELS else "tok", f"t{i}"] for i in range(LEVELS)], [])
                  + ["s0", "v1", "s1", "v2", "s2", "v3", "o"])
SB_PE = Steps(["z", "tri", "pv"])
SB_ACT = Steps(["soft", "w", "o"])
SB_DVE = Steps(["nsp", "ex", "o"])
ROWS_ACT = Steps(["ln", "eg"])
ROWS_DVE = Steps(["g", "beg", "cols"])


def scores_order(n):
    return ["s0"] + sum([[f"t{i}"] + ([f"s{i + 1}"] if i + 1 < n else []) + [f"v{i}"] for i in range(n)], [])


M2_BATCHES = 6
M2_SEG_AFTER = 3
M2_PE = Steps(["sums", "wst", "rope", "qrope", "s0", "mix"] + scores_order(M2_BATCHES)[1:])
M2_ACT = Steps(["sq", "gv", "rs", "wst", "gelu", "vrs", "qa", "kv", "e0"]
               + sum([[f"pt{b}"] + ([f"e{b + 1}"] if b + 1 < M2_BATCHES else []) + (["seg2", "seg0"] if b == M2_SEG_AFTER else [])
                      for b in range(M2_BATCHES)], []) + ["seg1"])
M2_DVE = Steps(["gn", "cn", "kpe", "gr", "qr", "vn", "mix", "mx0"]
               + sum([([f"mx{b + 1}"] if b + 1 < M2_BATCHES else []) + [f"o{b}"] for b in range(M2_BATCHES)], []))
ME_BATCHES = 2
ME_ORDER = [f"{kind}{b}" for kind in "stv" for b in range(ME_BATCHES)]
ME_PE = Steps(ME_ORDER)
ME_ACT = Steps(["q0", "q1"] + [f"{kind}{b}" for kind in ("e", "pt", "oh") for b in range(ME_BATCHES)])
ME_DVE = Steps([f"{kind}{b}" for kind in ("mx", "pn", "ol") for b in range(ME_BATCHES)])

def pair_units(c):
    return [(kind, c) for kind in ("q", "k", "v", "z")]


FIRST = [("b", 0), ("a", 0), ("sv", 0)] + pair_units(0) + [("sv", 1)]
DELTA_BG = [pair_units(1) + [("sv", 2), ("sv", 3)], pair_units(2) + [("sq", 0), ("sk", 0)],
            pair_units(3) + [("sq", 1), ("sk", 1), ("ga", 0)],
            [("sq", 2), ("sk", 2), ("ga", 1), ("ga", 2), ("gb", 0), ("gb", 1), ("gb", 2)]]
SB_BG = [[("sq", 3), ("sk", 3), ("ga", 3), ("gb", 3), ("gb", 3.5)], [("wa", c) for c in range(4)]]
LAST = [("wb", c) for c in range(4)] + [("wo", c) for c in range(4)]
MIX1_ORDER = FIRST + sum(DELTA_BG, []) + sum(SB_BG, []) + LAST
MIX1_UNITS = len(MIX1_ORDER)
BANK_UNITS = ((MIX1_UNITS + 1) // 2, MIX1_UNITS // 2)
PARTS = 4
WARM = 20
DELTA_WEIGHT = [2, 3, 2] + [1] * 10 + [1.3, 1, 1, 1, 1, 1, 1, 1.5, 2]
SB_WEIGHT = [4, 3, 0]


def plan(units, weights):
    parts = [(u, i) for u in units for i in range(PARTS)]
    ends = [round(len(parts) * sum(weights[:i + 1]) / sum(weights)) for i in range(len(weights))]
    return [parts[a:b] for a, b in zip([0] + ends, ends)]


numbers = lambda units: [MIX1_ORDER.index(u) for u in units]
DELTA_PLAN = sum((plan(numbers(units), DELTA_WEIGHT) for units in DELTA_BG), [])
SB_PLAN = plan(numbers(SB_BG[0]), SB_WEIGHT) + plan(numbers(SB_BG[1]), 3 * SB_WEIGHT)
MEM_PLAN = plan(range(9, 13), [4] + [{"s": 1.5, "t": 0.3, "v": 1.5}[step[0]] for step in scores_order(M2_BATCHES)])
LAYER1_TURNS = (2 * FFN_UNITS + MIX1_UNITS) // RING


def mix1_unit(r):
    kind, c = MIX1_ORDER[r]
    n = 128 if kind in "ba" or (kind, int(c)) == ("gb", 3) else 256
    start = {"q": 0, "k": D, "v": 2 * D, "z": 3 * D, "b": B_COL, "a": A_COL, "sq": SB_COL, "sk": SB_COL + D,
             "sv": SB_COL + 2 * D, "ga": GA_COL, "gb": GB_COL, "wa": 0, "wb": 0, "wo": 0}[kind]
    return kind, c, start + int(256 * c), n


def build_program(nc, a, const, out):
    ctx = ExitStack()
    with ctx:
        def sb(name, shape, dt=F32):
            return ctx.enter_context(nc.sbuf_tensor("sb_" + name, shape, dt))

        def sem(name):
            return ctx.enter_context(nc.semaphore(name))

        ps = ctx.enter_context(nc.psum_tensor("ps", [P, 8, 512], F32))
        raw = sb("raw", [P, RING, UNIT])
        hi = sb("hi", [P, RING, UNIT], F32R)
        lo = sb("lo", [P, RING, UNIT], F32R)
        x = sb("x", [P, ST, D])
        hT_h = sb("hT_h", [P, KB, S], F32R)
        hT_l = sb("hT_l", [P, KB, S], F32R)
        o_h = sb("o_h", [P, KB, S], F32R)
        o_l = sb("o_l", [P, KB, S], F32R)
        qT = sb("qT", [P, KB, S])
        kT = sb("kT", [P, KB, S])
        vT = sb("vT", [P, KB, S])
        zT = sb("zT", [P, KB, S])
        tok = sb("tok", [P, ST, D])
        sq = sb("sq", [P, 2, 512])
        rs = sb("rs", [P, 2, 512])
        decay, attn, yinv = (sb(n, [P, 512]) for n in ("decay", "attn", "yinv"))
        quad = sb("quad", [P, 4, 512])
        u_v, w_k, k_dec, q_dec = (quad[:, i, :] for i in range(4))
        levels = sb("levels", [P, 4, 512])
        xinv, plev, mlev, lmat = (levels[:, i, :] for i in range(4))
        state = sb("state", [P, 3, 2, P])
        cst = sb("const", [P, CONST_TOTAL])
        stage = sb("stage", [P, 3, P])
        vec1 = sb("vec1", [P, P])
        vec2 = sb("vec2", [P, 3 * P])
        beta_r, g_r, eg_r = (sb(n, [HEADS, S]) for n in ("beta_r", "g_r", "eg_r"))
        tcol = sb("tcol", [P, 4, ST, HEADS])
        egl = sb("egl", [P, 2, 4])
        hcol = sb("hcol", [HEADS, 4])
        gcol = sb("gcol", [P, 4])
        eps_t = sb("eps", [P, 1])
        ss = sb("ss", [P, 8])
        rstd = sb("rstd", [P, 8])
        negmax = sb("negmax", [P, 2, 4])
        psum_p = sb("psum_p", [P, 2, 4])
        rinv = sb("rinv", [P, 2, 4])
        sqf = sq[:].rearrange("p a n -> p (a n)")
        rsf = rs[:].rearrange("p a n -> p (a n)")
        act_parts, last_act = ([o[:, i:i + 2, :].rearrange("p a n -> p (a n)") for o in (o_h, o_l)] for i in (0, 2))
        sil, prod = xinv, yinv
        junk = kT[:].rearrange("p (t k) n -> p t (k n)", t=ST)
        memx = quad[:].rearrange("p (t k) n -> p t (k n)", t=ST)
        mem_k = quad[:, 0:2, :].rearrange("p a (k n) -> p (a k) n", n=S)
        mem_v = quad[:, 2:4, :]

        def cc(name):
            at, w = CONST_AT[name]
            return cst[:, at:at + w]

        def over(ap, n, axis=1):
            v = ap.unsqueeze(axis)
            shape = list(v.shape)
            shape[axis] = n
            return v.to_broadcast(shape)

        gain_row = vT[:, 0:4, :].rearrange("p k n -> p (k n)")
        result = qT[:].rearrange("p (t k) n -> p t (k n)", t=ST)
        ident = cc("ident")
        cn_h, cn_l = hT_h[:, 0:3, :], hT_l[:, 0:3, :]

        start_loaded = sem("start_loaded")
        loads_begun = sem("loads_begun")
        raw_loaded = [sem(f"raw_loaded{i}") for i in range(RING)]
        heads_loaded = [sem("heads_loaded0"), sem("heads_loaded1")]
        hi_ready, lo_ready, unit_done = sem("hi_ready"), sem("lo_ready"), sem("unit_done")
        vec_loaded, vec_taken, vec_ready = sem("vec_loaded"), sem("vec_taken"), sem("vec_ready")
        zeroed, eps_ready = sem("zeroed"), sem("eps_ready")
        rstd_ready, xn_ready, tr_ready, hh_ready, h_ready = (sem(n) for n in ("rstd_ready", "xn_ready", "tr_ready", "hh_ready", "h_ready"))
        x_ready, added = sem("x_ready"), sem("added")
        half_done = sem("half_done")
        sil_ready, gate_used, up_used, act_ready = (sem(n) for n in ("sil_ready", "gate_used", "up_used", "act_ready"))
        bank_free = [sem("bank_free0"), sem("bank_free1")]
        rows_act, rows_dve, rows_pe = sem("rows_act"), sem("rows_dve"), sem("rows_pe")
        pre_pe, pre_act, pre_dve = sem("pre_pe"), sem("pre_act"), sem("pre_dve")
        dl_pe, dl_act, dl_dve = sem("delta_pe"), sem("delta_act"), sem("delta_dve")
        sb_pe, sb_act, sb_dve = sem("sb_pe"), sem("sb_act"), sem("sb_dve")
        gates_ready = sem("gates_ready")
        merged_ready = sem("merged_ready")
        m2_pe, m2_act, m2_dve = sem("m2_pe"), sem("m2_act"), sem("m2_dve")
        me_pe, me_act, me_dve = sem("me_pe"), sem("me_act"), sem("me_dve")
        mem_loaded, mem_rstd, mem_kv = sem("mem_loaded"), sem("mem_rstd"), sem("mem_kv")
        out_ready, out_stored = sem("out_ready"), sem("out_stored")
        act_own, dve_own = sem("act_own"), sem("dve_own")

        block = ctx.enter_context(nc.Block())

        def updates(n):
            return ST * n + ST

        def of_layer(name, l):
            return a[name][bass.ds(l, 1)]

        @block.sync
        def _(sp):
            def load(b, k, src, kk, n):
                slot = k % RING
                sp.wait_ge(lo_ready, RING * b + (k + 1))
                sp.sem_inc(loads_begun, 1)
                dst = raw[:, slot, 0:kk * n].rearrange("p (k n) -> p k n", k=kk)
                sp.dma_start(dst, src).then_inc(raw_loaded[slot], 16)

            def load_heads(b, k, src):
                slot = k % RING
                sp.wait_ge(lo_ready, RING * b + (k + 1))
                sp.sem_inc(loads_begun, 1)
                dst = raw[:, slot, 0:4 * 384].rearrange("p (k j h e) -> p k j h e", k=4, j=3, h=2)
                src = src.rearrange("o (k p) (h j e) -> p (o k) h j e", p=P, h=2, j=3)
                for h in range(2):
                    for j in range(3):
                        done = heads_loaded[k % 2] if h + j else raw_loaded[slot]
                        sp.dma_start(dst[:, :, j, h, :], src[:, :, h, j, :]).then_inc(done, 16)

            def cols(w, l, c0, n):
                return of_layer(w, l)[:, :, bass.ds(c0, n)].rearrange("o (k p) n -> p (o k) n", p=P)

            def rows(w, l, r0, n):
                return of_layer(w, l)[:, bass.ds(r0, n), :].rearrange("o (k p) n -> p (o k) n", p=P)

            def ffn(w_in, w_out, l, b):
                gate = lambda k, c, bb=0: load(b + bb, k, cols(w_in, l, 256 * c, 256), 8, 256)
                up = lambda k, c, bb=0: load(b + bb, k, cols(w_in, l, DFF + 256 * c, 256), 8, 256)
                down = lambda k, c, bb=0: load(b + bb, k, rows(w_out, l, 256 * c, 256), 2, D)
                gate(0, 0), up(1, 0), gate(2, 1), up(3, 1), down(4, 0)
                with sp.Fori(1, NCH - 1) as j:
                    gate(2, j + 1, j), up(3, j + 1, j), down(4, j, j)
                down(2, NCH - 1, NCH - 1)

            sp.dma_start(cst[:], const).then_inc(start_loaded, 16)
            sp.dma_start(x[:], a["x"].rearrange("o (t p) d -> p (o t) d", p=P)).then_inc(start_loaded, 16)

            with sp.Fori(0, DEPTH) as l:
                sp.wait_ge(zeroed, 1)
                for at, name, n in ((V1_FFN1, "ffn1_norm", 8), (V1_MIX, "mix_norm", 8), (V1_FFN2, "ffn2_norm", 8),
                                    (V1_ON, "dn_out_norm", 1), (V1_SBQ, "sb_q_norm", 1), (V1_SBK, "sb_k_norm", 1)):
                    sp.dma_start(stage[at:at + n, 0, :], of_layer(name, l).rearrange("o (r n) -> (o r) n", n=P)).then_inc(vec_loaded, 16)
                sp.dma_start(stage[V1_CONV:V1_CONV + 96, 0, :],
                             of_layer("dn_conv_w", l).rearrange("o j (r n) -> (o j r) n", n=P)).then_inc(vec_loaded, 16)
                sp.dma_start(hcol[:, 0:1], of_layer("dn_dt_bias", l).rearrange("o (h u) -> (o h) u", u=1)).then_inc(vec_loaded, 16)
                sp.dma_start(hcol[:, 1:2], of_layer("dn_a_log", l).rearrange("o (h u) -> (o h) u", u=1)).then_inc(vec_loaded, 16)
                b = LAYER1_TURNS * l
                ffn("ffn1_w_in", "ffn1_w_out", l, b)
                for r in range(MIX1_UNITS):
                    kind, _, c0, n = mix1_unit(r)
                    w = {"wa": "w_branch_a", "wb": "w_branch_b", "wo": "w_out"}.get(kind, "w_in")
                    load(b + NCH, r, cols(w, l, c0, n), 8, n)
                ffn("ffn2_w_in", "ffn2_w_out", l, b + (FFN_UNITS + MIX1_UNITS) // RING)

            with sp.Fori(0, DEPTH) as l:
                sp.wait_ge(x_ready, updates(3 * l + (3 * DEPTH - 1)))
                sp.sem_inc(loads_begun, 1)
                sp.wait_ge(vec_taken, l + DEPTH)
                sp.wait_ge(zeroed, 1)
                sp.dma_start(memx, a["mem_2"].rearrange("o (t p) d -> p (o t) d", p=P)).then_inc(mem_loaded, 16)
                sp.dma_start(attn[:].rearrange("p (g q) -> p g q", g=4),
                             of_layer("gmlp_w_s_2", l).rearrange("o g p q -> p (o g) q")).then_inc(vec_loaded, 16)
                sp.dma_start(lmat[:, 0:S], of_layer("gmlp_v_norm_2", l).partition_broadcast(P).rearrange("p o n -> p (o n)")).then_inc(vec_loaded, 16)
                for at, name, n in ((V2_MIX, "mix_norm_2", 8), (V2_CQ, "mla_q_norm_2", 2), (V2_CKV, "mla_kv_norm_2", 1),
                                    (V2_ON, "out_norm_2", 8), (V2_MEMX, "mem_x_norm_2", 8), (V2_MEMKV, "mem_kv_norm_2", 8),
                                    (V2_FFN, "ffn_norm_2", 8), (V2_CB, "ffn_conv_b_2", 44)):
                    sp.dma_start(stage[at:at + n, 0, :], of_layer(name, l).rearrange("o (r n) -> (o r) n", n=P)).then_inc(vec_loaded, 16)
                for at, name in ((V2_GQ, "gqa_q_norm_2"), (V2_GK, "gqa_k_norm_2")):
                    for half in range(2):
                        sp.dma_start(stage[at:at + 1, 0, 64 * half:64 * half + 64], of_layer(name, l)).then_inc(vec_loaded, 16)
                sp.dma_start(stage[V2_BS:V2_BS + 4, 0, :], of_layer("gmlp_b_s_2", l).rearrange("o g p -> (o g) p")).then_inc(vec_loaded, 16)
                taps = of_layer("ffn_conv_w_2", l).rearrange("o j (r n) -> (o j) r n", n=P)
                for j in range(3):
                    dst = stage[44 * (j % 2):44 * (j % 2) + 44, 1 + j // 2, :]
                    sp.dma_start(dst, taps[j]).then_inc(vec_loaded, 16)
                b = LAYER2_TURNS * l + DEPTH * LAYER1_TURNS
                for r, (c0, n) in enumerate(W2_COLS):
                    if r in (2, 3):
                        load_heads(b, r, of_layer("w_in_2", l)[:, 512 * (r - 2):512 * (r - 1), c0:c0 + n])
                    else:
                        load(b, r, cols("w_in_2", l, c0, n), 8, n)
                load(b, 7, rows("mla_w_uq_2", l, 0, 256), 2, 576)
                load(b, 8, rows("mla_w_ukv_2", l, 0, 128), 1, 768)
                for m in range(4):
                    load(b, 9 + m, cols("mem_w_kv_2", l, 256 * m, 256), 8, 256)
                for m in range(4):
                    load(b, 13 + m, cols("w_out_2", l, 256 * m, 256), 8, 256)
                for m in range(2):
                    load(b, 17 + m, cols("mem_w_q_2", l, 256 * m, 256), 8, 256)
                for m in range(2):
                    load(b, 19 + m, cols("mem_w_o_2", l, 512 * m, 512), 4, 512)
                ffn("ffn_w_up_2", "ffn_w_down_2", l, b + MIX2_UNITS // RING)

            sp.wait_ge(x_ready, updates(6 * DEPTH - 1))
            sp.dma_start(gain_row, a["final_norm_2"].partition_broadcast(P)).then_inc(start_loaded, 16)
            for t in range(ST):
                sp.wait_ge(out_ready, t + 1)
                sp.dma_start(out.rearrange("o (t p) d -> p (o t) d", p=P)[:, t, :], result[:, t, :]).then_inc(out_stored, 16)
            sp.wait_ge(out_stored, 16 * ST)

        @block.gpsimd
        def _(pool):
            pool.sem_inc(lo_ready, RING)
            with pool.Fori(0, DEPTH * (LAYER1_TURNS + LAYER2_TURNS)) as turn:
                for slot in range(RING):
                    pool.wait_ge(hi_ready, RING * turn + (slot + 1))
                    nc.gpsimd.tensor_tensor(lo[:, slot, :], raw[:, slot, :], hi[:, slot, :].bitcast(F32),
                                            ALU.subtract).then_inc(lo_ready, 1)

        @block.tensor
        def _(pe):
            pe.sem_inc(unit_done, RING)
            pe.wait_ge(start_loaded, 32)
            mm = nc.tensor.matmul

            def weights(k, kk, n):
                slot = k % RING
                return [w[:, slot, 0:kk * n].rearrange("p (k n) -> p k n", k=kk) for w in (hi, lo)]

            def arrived(b, k):
                pe.wait_ge(lo_ready, RING * b + (k + RING + 1))

            def product(dst, pairs, first=True, last=True):
                n = 0
                for (ah, al), (bh, bl) in pairs:
                    for s, m in ((ah, bh), (al, bh), (ah, bl)):
                        ins = mm(dst, s, m, start=first and n == 0, stop=last and n == 3 * len(pairs) - 1)
                        n += 1
                return ins

            def feature_major(b, k, src, bank, q=None):
                arrived(b, k)
                wh, wl = weights(k, KB, 256)
                for i in range(2):
                    for c in range(KB):
                        if q is not None and i == 0 and c % 2 == 0:
                            pe.wait_ge(h_ready, 4 * q + (c // 2 + 1))
                        ins = product(ps[:, bank, i * S:(i + 1) * S],
                                      [((wh[:, c, i * P:(i + 1) * P], wl[:, c, i * P:(i + 1) * P]), (src[0][:, c, :], src[1][:, c, :]))],
                                      c == 0, c == KB - 1)
                return ins

            def token_major(b, k, src, dst, n=256, kk=8, c0=0, w=256):
                arrived(b, k)
                wh, wl = weights(k, kk, n)
                for t in range(ST):
                    tt = slice(t * P, (t + 1) * P)
                    ins = product(dst(t), [((src[0][:, c, tt], src[1][:, c, tt]), (wh[:, c, c0:c0 + w], wl[:, c, c0:c0 + w])) for c in range(kk)])
                return ins

            hT, oT = (hT_h, hT_l), (o_h, o_l)

            def warm(bank):
                for _ in range(WARM):
                    nc.tensor.transpose(ps[:, bank, 0:P], ident, ident)

            def transposes(q, src=tok, bank=0):
                if bank == 0:
                    warm(3)
                for t in range(ST):
                    pe.wait_ge(xn_ready, ST * q + (t + 1))
                    for g in range(4):
                        for i in range(2):
                            k = 2 * g + i
                            ins = nc.tensor.transpose(ps[:, bank + g, i * S + t * P:i * S + (t + 1) * P], src[:, t, k * P:(k + 1) * P], ident)
                        if t == ST - 1:
                            ins.then_inc(tr_ready, 1)

            def ffn(f, b, q, gate_read, G0):
                F0 = NCH * f

                def up(bb, k, bank, q=None):
                    feature_major(bb, k, hT, bank, q).then_inc(unit_done, 1)

                def down(bb, k, first, last):
                    arrived(bb, k)
                    wh, wl = weights(k, 2, D)
                    act_h, act_l = last_act if last else act_parts
                    for t in range(ST):
                        if last and t > 0:
                            ins.then_inc(half_done, 1)
                        for n in range(2):
                            pairs = []
                            for i in range(2):
                                c = slice(i * S + t * P, i * S + (t + 1) * P)
                                e = slice(n * 512, (n + 1) * 512)
                                pairs.append(((act_h[:, c], act_l[:, c]), (wh[:, i, e], wl[:, i, e])))
                            ins = product(ps[:, 4 + 2 * t + n, :], pairs, first, last)
                    ins.then_inc(unit_done, 1)

                up(b, 0, 0, q)
                up(b, 1, 1)
                pe.wait_ge(gate_read, G0 + 1)
                up(b, 2, 0)
                pe.wait_ge(up_used, F0 + 1)
                up(b, 3, 1)
                pe.wait_ge(act_ready, F0 + 2)
                down(b, 4, True, False)
                with pe.Fori(1, NCH - 1) as j:
                    pe.wait_ge(gate_read, G0 + j + 1)
                    up(b + j, 2, 0)
                    pe.wait_ge(up_used, F0 + j + 1)
                    up(b + j, 3, 1)
                    pe.wait_ge(act_ready, F0 + j + 2)
                    down(b + j, 4, False, False)
                pe.wait_ge(act_ready, F0 + NCH + 1)
                down(b + (NCH - 1), 2, False, True)

            def columns(n, loads, tiles):
                pe.wait_ge(vec_loaded, loads)
                pe.wait_ge(x_ready, updates(3 * n))
                for i in range(tiles):
                    ins = nc.tensor.transpose(ps[:, 7, i * P:(i + 1) * P], stage[:, i, :], ident)
                ins.then_inc(vec_taken, 1)

            def quarters(b, r, src, bank, n=256, by_token=False, q=None):
                arrived(b, r)
                w = weights(r, KB, n)
                work = []
                for i in range(ST if by_token else n // P):
                    blk = slice(i * P, (i + 1) * P)
                    for k in range(KB):
                        if by_token:
                            pair = tuple(v[:, k, blk] for v in src), tuple(v[:, k, :] for v in w)
                        else:
                            pair = tuple(v[:, k, blk] for v in w), tuple(v[:, k, :] for v in src)
                        work.append((ps[:, bank, i * S:(i + 1) * S], pair, k))
                for part in range(PARTS):
                    for dst, pair, k in work[len(work) * part // PARTS:len(work) * (part + 1) // PARTS]:
                        if q is not None and k % 2 == 0:
                            pe.wait_ge(h_ready, 4 * q + (k // 2 + 1))
                        ins = product(dst, [pair], k == 0, k == KB - 1)
                    if part == PARTS - 1:
                        ins.then_inc(unit_done, 1)
                    yield

            def unit1_parts(l, b, r, q=None):
                kind, c, _, n = mix1_unit(r)
                bank = r % 2
                if r >= 2:
                    pe.wait_ge(bank_free[bank], BANK_UNITS[bank] * l + r // 2)
                if kind == "wo":
                    pe.wait_ge(merged_ready, 4 * l + 4)
                return quarters(b, r, oT if kind in ("wa", "wo") else hT, bank, n, kind in ("wo", "sv"), q)

            def unit1(l, b, r, q=None):
                for _ in unit1_parts(l, b, r, q):
                    pass

            def pre(l, half):
                pe.wait_ge(pre_act, PRE_ACT.at(HALVES * l + half, "sq"))
                for i in range(2):
                    ins = mm(ps[:, 2 + i, :], cc("ones"), levels[:, i, :], start=True, stop=True)
                ins.then_inc(pre_pe, 1)

            def delta(l, c):
                g = NPAIR * l + c
                wa = lambda name: pe.wait_ge(dl_act, DELTA_ACT.at(g, name))
                wv = lambda name: pe.wait_ge(dl_dve, DELTA_DVE.at(g, name))
                heads = (2 * c, 2 * c + 1)
                probs = [(i, t) for i in range(2) for t in range(ST)]
                blk = lambda bank, p: ps[:, bank, p * P:(p + 1) * P]
                of = lambda buf, p: buf[:, p * P:(p + 1) * P]
                tile = lambda buf, p: buf[:, heads[probs[p][0]], probs[p][1] * P:(probs[p][1] + 1) * P]
                pe.wait_ge(rows_dve, ROWS_DVE.at(l, "cols"))
                if c:
                    pe.wait_ge(dl_dve, DELTA_DVE.at(g - 1, "v3"))
                for n, row in enumerate((g_r, beta_r, eg_r)):
                    if n == 2:
                        ins.then_inc(dl_pe, 1)
                        yield
                        if c:
                            pe.wait_ge(dl_dve, DELTA_DVE.at(g - 1, "o"))
                    for i, h in enumerate(heads):
                        ins = mm(ps[:, 4 + n, i * S:(i + 1) * S], ident[0:HEADS, h:h + 1].to_broadcast([HEADS, P]), row[:, :], start=True, stop=True)
                ins.then_inc(dl_pe, 1)
                pe.wait_ge(pre_dve, HALVES * l + c + 1)
                for p in range(4):
                    mm(blk(2, p), tile(kT, p), tile(kT, p), start=True, stop=True)
                    ins = mm(blk(3, p), tile(kT, p), tile(qT, p), start=True, stop=True)
                ins.then_inc(dl_pe, 1)
                wv("diff")
                for p in range(4):
                    nc.tensor.transpose(blk(7, p), tile(kT, p), ident)
                    ins = nc.tensor.transpose(blk(4, p), tile(vT, p), ident)
                ins.then_inc(dl_pe, 1)
                yield
                wv("lt")
                for p in range(4):
                    ins = nc.tensor.transpose(blk(2, p), of(yinv, p), ident)
                ins.then_inc(dl_pe, 1)
                yield
                for i in range(LEVELS):
                    wv(f"m{i}")
                    if i == 0:
                        wa("x")
                    else:
                        wv(f"t{i - 1}")
                    for p in range(4):
                        ins = mm(blk(3, p), of(mlev, p), of(xinv, p), start=True, stop=True)
                    ins.then_inc(dl_pe, 1)
                    yield
                    wa(f"p{i}")
                    for p in range(4):
                        ins = mm(blk(2, p), of(plev, p), of(yinv, p), start=True, stop=True)
                        if i < LEVELS - 1:
                            ins = mm(blk(5, p), of(yinv, p), of(plev, p), start=True, stop=True)
                    ins.then_inc(dl_pe, 1)
                    yield
                wv(f"t{LEVELS - 1}")
                wv("tok")
                for p in range(4):
                    mm(blk(2, p), of(yinv, p), of(u_v, p), start=True, stop=True)
                    ins = mm(blk(3, p), of(w_k, p), of(yinv, p), start=True, stop=True)
                ins.then_inc(dl_pe, 1)
                yield

                def push(ch):
                    t, half = divmod(ch, 2)
                    rr = slice(64 * half, 64 * half + 64)
                    for i in range(2):
                        p = 2 * i + t
                        ins = mm(ps[:, 4, i * P:(i + 1) * P], of(k_dec, p)[rr, :], of(u_v, p)[rr, :], start=True, stop=True)
                    ins.then_inc(dl_pe, 1)

                wa("uw")
                push(0)
                yield
                for ch in range(1, 4):
                    t, half = divmod(ch, 2)
                    rr = slice(64 * half, 64 * half + 64)
                    if ch == 3:
                        pre(l, c + 1)
                    wv(f"s{ch - 1}")
                    for i in range(2):
                        ins = mm(ps[rr, 5, i * P:(i + 1) * P], of(w_k, 2 * i + t)[:, rr], state[:, ch - 1, i, :], start=True, stop=True)
                    ins.then_inc(dl_pe, 1)
                    yield
                    wv(f"v{ch}")
                    if ch < 3:
                        push(ch)
                        yield
                for p, (i, t) in enumerate(probs):
                    dst = ps[:, 6 + i, t * P:(t + 1) * P]
                    mm(dst, of(u_v, p), of(attn, p), start=True, stop=False)
                    for ch in (2 * t, 2 * t + 1):
                        if ch > 0:
                            c0 = (ch % 2) * CHUNK
                            ins = mm(ps[:, 6 + i, t * P + c0:t * P + c0 + CHUNK], state[:, ch - 1, i, :], of(q_dec, p)[:, c0:c0 + CHUNK],
                                     start=False, stop=ch % 2 == 1)
                ins.then_inc(dl_pe, 1)
                yield
                wa("osq")
                mm(ps[:, 2, :], cc("ones"), sq[:, 0, :], start=True, stop=True).then_inc(dl_pe, 1)
                yield

            def stick(l, c):
                g = NPAIR * l + c
                wa = lambda name: pe.wait_ge(sb_act, SB_ACT.at(g, name))
                wv = lambda name: pe.wait_ge(sb_dve, SB_DVE.at(g, name))
                heads = (2 * c, 2 * c + 1)
                pe.wait_ge(pre_dve, HALVES * l + NPAIR + c + 1)
                if c:
                    pe.wait_ge(sb_dve, SB_DVE.at(g - 1, "ex"))
                for i, h in enumerate(heads):
                    mm(ps[:, 4 + i, 0:S], kT[:, h, 0:P], qT[:, h, :], start=True, stop=False, skip_group_check=True)
                    ins = mm(ps[:, 4 + i, S:S + P], kT[:, h, P:S], qT[:, h, P:S], start=False, stop=False, skip_group_check=True)
                ins.then_inc(sb_pe, 1)
                yield
                if c + 1 < NPAIR:
                    pre(l, NPAIR + c + 1)
                wv("nsp")
                for i in range(2):
                    n0 = rsf[:, 384 * i:384 * i + S]
                    n1 = rsf[:, 384 * i + S:384 * (i + 1)]
                    mm(ps[:, 4 + i, 0:S], cc("tri"), n0, start=False, stop=False, skip_group_check=True)
                    mm(ps[:, 4 + i, P:S], cc("ones"), n1, start=False, stop=False, skip_group_check=True)
                    ins = mm(ps[:, 4 + i, S:S + P], cc("tri"), n1, start=False, stop=True, skip_group_check=True)
                ins.then_inc(sb_pe, 1)
                yield
                wa("w")
                for i, h in enumerate(heads):
                    w0 = sqf[:, 384 * i:384 * i + S]
                    w1 = sqf[:, 384 * i + S:384 * (i + 1)]
                    hh = slice(h * P, (h + 1) * P)
                    mm(ps[:, 6, i * S:(i + 1) * S], tok[:, 0, hh], w0, start=True, stop=False, skip_group_check=True)
                    ins = mm(ps[:, 6, i * S + P:(i + 1) * S], tok[:, 1, hh], w1, start=False, stop=True, skip_group_check=True)
                ins.then_inc(sb_pe, 1)
                yield

            def with_units(steps, todo, parts):
                unit = None
                for at, _ in enumerate(steps):
                    for r, part in todo[at] if at < len(todo) else ():
                        if part == 0:
                            unit = parts(r)
                        next(unit)

            def mixer1(l, b, q):
                for r in range(4):
                    unit1(l, b, r, None if r else q)
                pe.wait_ge(rows_dve, ROWS_DVE.at(l, "beg"))
                for n, row in enumerate((beta_r[:, :], g_r[:, :], sq[0:HEADS, 0, 0:S], sq[0:HEADS, 1, S:2 * S])):
                    for t in range(ST):
                        at = (n * ST + t) * HEADS
                        ins = mm(ps[:, 7, at:at + HEADS], row[:, t * P:(t + 1) * P], ident[0:HEADS, 0:HEADS], start=True, stop=True)
                ins.then_inc(rows_pe, 1)
                for r in range(4, len(FIRST)):
                    unit1(l, b, r)
                warm(2)
                pre(l, 0)
                with_units(chain(*(delta(l, c) for c in range(NPAIR))), DELTA_PLAN, lambda r: unit1_parts(l, b, r))
                with_units(chain(*(stick(l, c) for c in range(NPAIR))), SB_PLAN, lambda r: unit1_parts(l, b, r))
                pe.wait_ge(sb_dve, SB_DVE.at(NPAIR * l + NPAIR - 1, "o"))
                for r in range(MIX1_UNITS - len(LAST), MIX1_UNITS):
                    unit1(l, b, r)

            with pe.Fori(0, DEPTH) as l:
                b = LAYER1_TURNS * l
                columns(l, 16 * V1_LOADS * l + 16 * V1_LOADS, 1)
                transposes(3 * l)
                ffn(2 * l, b, 3 * l, sil_ready, 2 * NCH * l)
                transposes(3 * l + 1)
                mixer1(l, b + NCH, 3 * l + 1)
                transposes(3 * l + 2)
                ffn(2 * l + 1, b + (FFN_UNITS + MIX1_UNITS) // RING, 3 * l + 2, sil_ready, 2 * NCH * l + NCH)

            def weights_out(pbuf, bank):
                for i in range(2):
                    for kt in range(ST):
                        for t in range(ST):
                            ins = nc.tensor.transpose(ps[:, bank + i, kt * S + t * P:kt * S + (t + 1) * P],
                                                      pbuf[:, (i * ST + t) * S + kt * P:(i * ST + t) * S + (kt + 1) * P], ident)
                return ins

            def mixer2(l, b, q):
                wa = lambda name: pe.wait_ge(m2_act, M2_ACT.at(l, name))
                wv = lambda name: pe.wait_ge(m2_dve, M2_DVE.at(l, name))
                col = lambda v, k, c0, n: tuple(w[:, k, c0:c0 + n] for w in v)
                feature_major(b, 0, hT, 0, q).then_inc(unit_done, 1)
                arrived(b, 1)
                w = weights(1, 8, 160)
                hb = lambda c: (hT_h[:, c, :], hT_l[:, c, :])
                product(ps[:, 1, 0:S], [(col(w, c, 0, P), hb(c)) for c in range(KB)])
                product(ps[0:96, 1, S:2 * S], [(col(w, c, 64, 96), hb(c)) for c in range(KB)]).then_inc(unit_done, 1)
                pe.wait_ge(h_ready, 4 * q + 8)
                for u in (2, 3):
                    arrived(b, u)
                    w = weights(u, 4, 384)
                    for j in range(3):
                        pairs = []
                        for c in range(4):
                            pairs.append((col(w, c, P * j, P), hb(4 * (u - 2) + c)))
                        ins = product(ps[:, 2 + j, 0:S], pairs, u == 2, u == 3)
                    ins.then_inc(unit_done, 1)
                arrived(b, 4)
                w = weights(4, 8, 256)
                product(ps[:, 5, 0:S], [(col(w, c, 0, P), hb(c)) for c in range(KB)])
                for t in range(ST):
                    tt_ = slice(t * P, (t + 1) * P)
                    ins = product(ps[:, 5, S + t * P:S + (t + 1) * P],
                                  [((hT_h[:, c, tt_], hT_l[:, c, tt_]), col(w, c, P, P)) for c in range(KB)])
                ins.then_inc(unit_done, 1)
                gmlp = lambda u: token_major(b, u, hT, lambda t: ps[:, u + 1, t * S:(t + 1) * S]).then_inc(unit_done, 1)
                gmlp(5)
                wa("sq")
                flat = lambda v: v.rearrange("p k n -> p (k n)")
                mm(ps[:, 0, 0:S], cc("ones"), kT[:, 0, :], start=True, stop=False)
                mm(ps[:, 0, 0:S], cc("ones"), kT[:, 1, :], start=False, stop=True)
                mm(ps[:, 0, S:2 * S], cc("ones"), kT[:, 2, :], start=True, stop=True)
                mm(ps[:, 2, :], cc("halves"), flat(kT[:, 3:5, :]), start=True, stop=True)
                mm(ps[:, 3, :], cc("halves"), flat(kT[:, 5:7, :]), start=True, stop=True).then_inc(m2_pe, 1)
                for g in range(4):
                    ins = nc.tensor.transpose(ps[:, 1, g * P:(g + 1) * P], attn[:, g * P:(g + 1) * P], ident)
                ins.then_inc(m2_pe, 1)
                gmlp(6)
                wv("gn")
                mm(ps[:, 2, :], cc("rot"), flat(qT[:, 0:2, :]), start=True, stop=True)
                mm(ps[:, 3, :], cc("rot"), flat(qT[:, 2:4, :]), start=True, stop=True)
                mm(ps[0:96, 4, 0:S], cc("rot")[64:96, 0:96], zT[64:96, 3, :], start=True, stop=True).then_inc(m2_pe, 1)
                wa("wst")
                wv("cn")
                arrived(b, 7)
                w = weights(7, 2, 576)
                QB, KBANK = (0, 1, 5), (4, 6, 7)
                for h in range(MLA_H):
                    ins = product(ps[0:96, QB[h // 2], (h % 2) * S:(h % 2 + 1) * S], [(col(w, c, 96 * h, 96), (cn_h[:, c, :], cn_l[:, c, :])) for c in range(2)])
                ins.then_inc(unit_done, 1)
                wa("gelu")
                wv("gr")
                arrived(b, 8)
                w = weights(8, 1, 768)
                for h in range(MLA_H):
                    product(ps[:, KBANK[h // 2], (h % 2) * S:(h % 2 + 1) * S], [(col(w, 0, P * h, P), (cn_h[:, 2, :], cn_l[:, 2, :]))])
                for t in range(ST):
                    tt_ = slice(t * P, (t + 1) * P)
                    vals = tuple(v[:, 0, :].rearrange("p (h e) -> p h e", h=MLA_H)[:, :, NOPE:P] for v in w)
                    ins = product(ps[:, 2 + t, 0:384], [((cn_h[:, 2, tt_], cn_l[:, 2, tt_]), vals)])
                ins.then_inc(unit_done, 1)
                wa("qa")
                for j in range(3):
                    ins = mm(ps[0:96, QB[j], :], cc("rot")[0:96, 0:96], flat(kT[0:96, 2 * j:2 * j + 2, :]), start=True, stop=True)
                ins.then_inc(m2_pe, 1)
                wa("kv")
                def attention():
                    yield
                    for step in scores_order(M2_BATCHES):
                        kind, beta = step[0], int(step[1:])
                        bank = 2 * (beta % 2)
                        if kind == "s":
                            wv("qr" if beta < 2 else f"o{beta - 2}")
                            for i in range(2):
                                for t in range(ST):
                                    tt_ = slice(t * P, (t + 1) * P)
                                    if beta < 3:
                                        left, right = kT[0:96, 2 * beta + i, tt_], vT[0:96, 2 * beta + i, :]
                                    else:
                                        r = slice(64 * i, 64 * i + 64)
                                        left, right = qT[r, beta - 3, tt_], qT[r, 3, :]
                                    ins = mm(ps[:, bank + i, t * S:(t + 1) * S], left, right, start=True, stop=True)
                            ins.then_inc(m2_pe, 1)
                            if beta == 0:
                                wv("vn")
                                for t in range(ST):
                                    for g in range(4):
                                        c0 = t * S + g * 64
                                        ins = mm(ps[:, 6, c0:c0 + 64], plev[:, g * P:(g + 1) * P], yinv[:, c0:c0 + 64], start=True, stop=True)
                                ins.then_inc(m2_pe, 1)
                        elif kind == "t":
                            wa(f"e{beta}")
                            weights_out((sqf, rsf)[beta % 2], 4).then_inc(m2_pe, 1)
                        else:
                            wa(f"pt{beta}")
                            buf = (qT[:, 4:8, :], zT[:, 0:4, :])[beta % 2]
                            for i in range(2):
                                for t in range(ST):
                                    dst = ps[:, bank, (i * ST + t) * 64:(i * ST + t + 1) * 64]
                                    for kt in range(ST):
                                        if beta < 3:
                                            c0 = kt * 384 + 64 * (2 * beta + i)
                                            val = flat(zT[:, 4:7, :])[:, c0:c0 + 64]
                                        else:
                                            val = decay[:, kt * P + 64 * i:kt * P + 64 * i + 64]
                                        ins = mm(dst, buf[:, i * ST + kt, t * P:(t + 1) * P], val, start=kt == 0, stop=kt == ST - 1)
                            ins.then_inc(m2_pe, 1)
                        yield

                def mem_parts(r):
                    if r == 10:
                        wv("mix")
                    if r >= 11:
                        pe.wait_ge(mem_kv, 4 * l + (r - 10))
                    return quarters(b, r, oT, 7 - (r - 9) % 2, by_token=r >= 11)

                with_units(attention(), MEM_PLAN, mem_parts)
                transposes(q + 2)
                for m in range(4):
                    if m >= 2:
                        pe.wait_ge(added, 3 * l + m - 1)
                    for _ in quarters(b, 13 + m, hT, 4 + m % 2, by_token=True, q=None if m else q + 2):
                        pass

            def memory(l, b, q):
                wa = lambda name: pe.wait_ge(me_act, ME_ACT.at(l, name))
                wv = lambda name: pe.wait_ge(me_dve, ME_DVE.at(l, name))
                transposes(q + 3)
                for m in range(2):
                    feature_major(b, 17 + m, hT, 4 + m, None if m else q + 3).then_inc(unit_done, 1)
                for step in ME_ORDER:
                    kind, beta = step[0], int(step[1:])
                    bank = 2 * (beta % 2)
                    if kind == "s":
                        wa("q1")
                        pe.wait_ge(mem_kv, 4 * l + 4)
                        for i in range(2):
                            h = 2 * beta + i
                            for t in range(ST):
                                ins = mm(ps[:, bank + i, t * S:(t + 1) * S], qT[:, h, t * P:(t + 1) * P], mem_k[:, h, :], start=True, stop=True)
                        ins.then_inc(me_pe, 1)
                    elif kind == "t":
                        if beta == 0:
                            warm(6)
                        wv(f"pn{beta}")
                        weights_out((sqf, rsf)[beta % 2], 4 + bank).then_inc(me_pe, 1)
                    else:
                        wa(f"pt{beta}")
                        buf = (kT[:, 4:8, :], zT[:, 0:4, :])[beta % 2]
                        for i in range(2):
                            h = 2 * beta + i
                            for kt in range(ST):
                                val = mem_v[:, kt, h * P:(h + 1) * P]
                                ins = mm(ps[:, bank, i * S:(i + 1) * S], val, buf[:, i * ST + kt, :], start=kt == 0, stop=kt == ST - 1)
                        ins.then_inc(me_pe, 1)
                wv(f"ol{ME_BATCHES - 1}")
                for m in range(2):
                    token_major(b, 19 + m, hT, lambda t: ps[:, 4 + 2 * m + t, :], n=512, kk=4, w=512).then_inc(unit_done, 1)

            with pe.Fori(0, DEPTH) as l:
                b = LAYER2_TURNS * l + DEPTH * LAYER1_TURNS
                q = 5 * l + 3 * DEPTH
                columns(l + DEPTH, 16 * V2_LOADS * l + 16 * (V1_LOADS * DEPTH + V2_LOADS), 3)
                transposes(q)
                transposes(q + 1, memx, 4)
                mixer2(l, b, q)
                memory(l, b, q)
                transposes(q + 4)
                ffn(l + 2 * DEPTH, b + MIX2_UNITS // RING, q + 4, gate_used, NCH * l)

        @block.scalar
        def _(act):
            own = Own(act, act_own)
            fn = nc.scalar.activation
            LOGS = "natural_log_exp_and_others"

            def split(b, k):
                slot = k % RING
                act.wait_ge(raw_loaded[slot], 16 * b + 16 * (k // RING + 1))
                act.wait_ge(unit_done, RING * b + (k + 1))
                fn(hi[:, slot, :], raw[:, slot, :], ACT.Copy).then_inc(hi_ready, 1)

            def rsqrt(dst, src, scale, to=None):
                own.link(fn(dst, src, ACT.Ln, bias=eps_t[:, 0:1], scale=scale))
                return fn(dst, dst, ACT.Exp, scale=-0.5)

            def stats(n, src, x_updates, junk=junk):
                for t in range(ST):
                    act.wait_ge(x_ready, ST * x_updates + (t + 1))
                    own.link(fn(junk[:, t, :], src[:, t, :], ACT.Square, accum_out=ss[:, t:t + 1]))
                    rsqrt(rstd[:, t:t + 1], ss[:, t:t + 1], 1.0 / D).then_inc(rstd_ready, 1)

            def high(q, gain, dst, bank=0):
                for g in range(4):
                    act.wait_ge(tr_ready, 4 * q + (g + 1))
                    for i in range(2):
                        k = 2 * g + i
                        ins = fn(dst[:, k, :], ps[:, bank + g, i * S:(i + 1) * S], ACT.Copy, scale=gain(k))
                    ins.then_inc(hh_ready, 1)

            def ffn(f, b):
                F0 = NCH * f

                def silu(bb, k, j):
                    act.wait_ge(unit_done, RING * bb + (k + RING + 1))
                    if j is not None:
                        act.wait_ge(up_used, F0 + j)
                    fn(sil[:], ps[:, 0, :], ACT.Silu).then_inc(sil_ready, 1)

                split(b, 2)
                split(b, 3)
                silu(b, 0, None)
                split(b, 4)
                split(b, 5)
                silu(b, 2, 1)
                split(b, 6)
                with act.Fori(1, NCH - 2) as j:
                    split(b + j, 4)
                    split(b + j, 5)
                    silu(b + j, 2, j + 1)
                    split(b + j, 6)
                split(b + (NCH - 2), 4)
                split(b + (NCH - 2), 5)
                silu(b + (NCH - 2), 2, NCH - 1)

            def evac1(l, r):
                kind, c, _, n = mix1_unit(r)
                bank = r % 2
                v = ps[:, bank, 0:2 * n].rearrange("p (k n) -> p k n", n=S)
                arena = {"z": zT, "sq": qT, "sk": kT, "ga": zT, "gb": vT}
                if kind == "sv":
                    dst = tok[:, :, S * c:S * (c + 1)]
                elif kind in arena:
                    dst = arena[kind][:, int(2 * c):int(2 * c) + n // P, :]
                else:
                    return
                act.wait_ge(unit_done, RING * b_of(l) + (r + RING + 1))
                fn(dst, v, ACT.Copy).then_inc(bank_free[bank], 1)

            def b_of(l):
                return LAYER1_TURNS * l + NCH

            def freed(l, r):
                act.wait_ge(bank_free[r % 2], BANK_UNITS[r % 2] * l + (r // 2 + 1))

            def pre_squares(l, half):
                c = half % NPAIR
                sl = slice(2 * c, 2 * c + 2)
                if half < NPAIR:
                    for u in pair_units(c):
                        freed(l, MIX1_ORDER.index(u))
                    for buf in (qT, kT, vT, zT):
                        ins = fn(buf[:, sl, :], buf[:, sl, :], ACT.Silu)
                    own.link(ins)
                    act.preload_act_table_set(LOGS)
                else:
                    for kind in ("sq", "sk"):
                        freed(l, MIX1_ORDER.index((kind, c)))
                fn(levels[:, 0, :].rearrange("p (k n) -> p k n", n=S), qT[:, sl, :], ACT.Square)
                fn(levels[:, 1, :].rearrange("p (k n) -> p k n", n=S), kT[:, sl, :], ACT.Square).then_inc(pre_act, 1)

            def pre_roots(l, half):
                act.wait_ge(pre_pe, HALVES * l + half + 1)
                rsqrt(levels[:, 2:4, :], ps[:, 2:4, :], 1.0 if half < NPAIR else 1.0 / P).then_inc(pre_act, 1)

            def delta(l, c):
                g = NPAIR * l + c
                wp = lambda name: act.wait_ge(dl_pe, DELTA_PE.at(g, name))
                wv = lambda name: act.wait_ge(dl_dve, DELTA_DVE.at(g, name))
                wv("diff")
                fn(decay[:], decay[:], ACT.Exp).then_inc(dl_act, 1)
                yield
                yield
                wp("xt")
                fn(xinv[:], ps[:, 2, :], ACT.Copy).then_inc(dl_act, 1)
                yield
                for i in range(LEVELS):
                    wp(f"p{i}")
                    fn(plev[:], ps[:, 3, :], ACT.Copy).then_inc(dl_act, 1)
                    yield
                    yield
                wp("uw")
                fn(u_v[:], ps[:, 2, :], ACT.Copy)
                fn(w_k[:], ps[:, 3, :], ACT.Copy).then_inc(dl_act, 1)
                yield
                yield
                pre_squares(l, c + 1)
                for _ in range(4):
                    yield
                pre_roots(l, c + 1)
                yield
                wp("o")
                fn(sq[:, 0, :].rearrange("p (k n) -> p k n", n=S), ps[:, 6:8, 0:S], ACT.Square).then_inc(dl_act, 1)
                wp("osum")
                rsqrt(rs[:, 0, :], ps[:, 2, :], 1.0 / P).then_inc(dl_act, 1)
                yield
                yield

            def stick(l, c):
                g = NPAIR * l + c
                wp = lambda name: act.wait_ge(sb_pe, SB_PE.at(g, name))
                wv = lambda name: act.wait_ge(sb_dve, SB_DVE.at(g, name))
                sl = slice(2 * c, 2 * c + 2)
                soft = sqf[:, 0:768]
                if c == 0:
                    act.wait_ge(dl_dve, DELTA_DVE.at(NPAIR * l + NPAIR - 1, "o"))
                else:
                    act.wait_ge(sb_pe, SB_PE.at(g - 1, "pv"))
                wp("z")
                own.link(fn(soft.rearrange("p (i n) -> p i n", i=2), ps[:, 4:6, 0:384], ACT.Abs))
                own.link(fn(soft, soft, ACT.Exp, scale=-1.0))
                fn(soft, soft, ACT.Ln, bias=1.0).then_inc(sb_act, 1)
                if c + 1 < NPAIR:
                    pre_squares(l, NPAIR + c + 1)
                if c == 1:
                    for chunk in (3, 3.5):
                        freed(l, MIX1_ORDER.index(("gb", chunk)))
                    fn(zT[:], zT[:], ACT.Sigmoid)
                    fn(vT[:], vT[:], ACT.Sigmoid).then_inc(gates_ready, 1)
                    act.preload_act_table_set(LOGS)
                yield
                wv("ex")
                fn(soft, soft, ACT.Exp).then_inc(sb_act, 1)
                if c + 1 < NPAIR:
                    pre_roots(l, NPAIR + c + 1)
                yield
                wp("pv")
                if c == 0:
                    act.wait_ge(unit_done, RING * b_of(l) + (MIX1_ORDER.index(("gb", 3.5)) + RING + 1))
                fn(hT_h[:, sl, :], ps[:, 6, :].rearrange("p (k n) -> p k n", n=S), ACT.Copy).then_inc(sb_act, 1)
                yield

            def with_units(steps, todo, b, evac):
                late = []
                for at, _ in enumerate(steps):
                    for r in late:
                        evac(r)
                    late = []
                    for r, part in todo[at] if at < len(todo) else ():
                        if part == 0:
                            if r - 2 in late:
                                late.remove(r - 2)
                                evac(r - 2)
                            split(b, r + 2)
                        if part == PARTS - 1:
                            late.append(r)
                for r in late:
                    evac(r)

            def plain(l, b, units):
                for r in units:
                    if r + 2 < MIX1_UNITS:
                        split(b, r + 2)
                    evac1(l, r)

            def mixer1(l, b):
                split(b, 2)
                act.wait_ge(unit_done, RING * b + (0 + RING + 1))
                fn(beta_r[:, :], ps[0:HEADS, 0, 0:S], ACT.Exp, scale=-1.0).then_inc(bank_free[0], 1)
                split(b, 3)
                freed(l, 1)
                y, e = sq[0:HEADS, 0, 0:S], sq[0:HEADS, 0, S:2 * S]
                own.link(fn(e, y, ACT.Abs))
                own.link(fn(e, e, ACT.Exp, scale=-1.0))
                fn(hcol[:, 2:3], hcol[:, 1:2], ACT.Exp)
                fn(e, e, ACT.Ln, bias=1.0).then_inc(rows_act, 1)
                act.wait_ge(rows_dve, ROWS_DVE.at(l, "g"))
                fn(eg_r[:, :], g_r[:, :], ACT.Exp)
                d = sq[0:HEADS, 1, S:2 * S]
                fn(d, d, ACT.Exp).then_inc(rows_act, 1)
                plain(l, b, range(2, len(FIRST) - 1))
                split(b, len(FIRST) + 1)
                pre_squares(l, 0)
                evac1(l, len(FIRST) - 1)
                pre_roots(l, 0)
                with_units(chain(*(delta(l, c) for c in range(NPAIR))), DELTA_PLAN, b, lambda r: evac1(l, r))
                act.wait_ge(dl_dve, DELTA_DVE.count * (NPAIR * l) + DELTA_DVE.count * NPAIR)
                with_units(chain(*(stick(l, c) for c in range(NPAIR))), SB_PLAN, b, lambda r: evac1(l, r))
                plain(l, b, range(MIX1_UNITS - len(LAST), MIX1_UNITS))

            act.wait_ge(start_loaded, 32)
            act.wait_ge(eps_ready, 1)
            with act.Fori(0, DEPTH) as l:
                own.restart()
                b = LAYER1_TURNS * l
                act.preload_act_table_set(LOGS)
                split(b, 0)
                split(b, 1)
                stats(3 * l, x, 3 * l)
                act.wait_ge(vec_ready, l + 1)
                high(3 * l, lambda k: vec1[:, V1_FFN1 + k:V1_FFN1 + k + 1], hT_h)
                ffn(2 * l, b)
                act.preload_act_table_set(LOGS)
                split(b + NCH, 0)
                split(b + NCH, 1)
                stats(3 * l + 1, x, 3 * l + 1)
                high(3 * l + 1, lambda k: vec1[:, V1_MIX + k:V1_MIX + k + 1], hT_h)
                mixer1(l, b + NCH)
                b2 = b + (FFN_UNITS + MIX1_UNITS) // RING
                split(b2, 0)
                split(b2, 1)
                stats(3 * l + 2, x, 3 * l + 2)
                high(3 * l + 2, lambda k: vec1[:, V1_FFN2 + k:V1_FFN2 + k + 1], hT_h)
                ffn(2 * l + 1, b2)

            def done(b, r):
                act.wait_ge(unit_done, RING * b + (r + RING + 1))

            def two_next(b, r):
                if r + 2 < MIX2_UNITS:
                    split(b, r + 2)

            def mixer2(l, b):
                wp = lambda name: act.wait_ge(m2_pe, M2_PE.at(l, name))
                wv = lambda name: act.wait_ge(m2_dve, M2_DVE.at(l, name))
                sig = lambda ins: ins.then_inc(m2_act, 1)
                two = lambda v: v.rearrange("p (k n) -> p k n", n=S)
                act.wait_ge(heads_loaded[0], 80 * l + 80)
                two_next(b, 0)
                done(b, 0)
                fn(zT[:, 0:2, :], two(ps[:, 0, :]), ACT.Copy)
                fn(kT[:, 0:2, :], two(ps[:, 0, :]), ACT.Square)
                act.wait_ge(heads_loaded[1], 80 * l + 80)
                two_next(b, 1)
                done(b, 1)
                fn(zT[:, 2, :], ps[:, 1, 0:S], ACT.Copy)
                fn(kT[:, 2, :], ps[:, 1, 0:S], ACT.Square)
                fn(zT[64:96, 3, :], ps[64:96, 1, S:2 * S], ACT.Copy)
                two_next(b, 2)
                two_next(b, 3)
                done(b, 3)
                fn(qT[:, 0:3, :], ps[:, 2:5, 0:S], ACT.Copy)
                fn(kT[:, 3:6, :], ps[:, 2:5, 0:S], ACT.Square)
                two_next(b, 4)
                done(b, 4)
                fn(qT[:, 3, :], ps[:, 5, 0:S], ACT.Copy)
                sig(fn(kT[:, 6, :], ps[:, 5, 0:S], ACT.Square))
                sig(fn(decay[:, 0:S], ps[:, 5, S:2 * S], ACT.Copy))
                two_next(b, 5)
                wp("sums")
                e1 = eps_t[:, 0:1]
                fn(vT[:, 0, :], ps[:, 0, 0:S], ACT.Ln, bias=e1, scale=1.0 / 256)
                fn(vT[:, 1, :], ps[:, 0, S:2 * S], ACT.Ln, bias=e1, scale=1.0 / 128)
                own.link(fn(vT[:, 2:6, :], ps[:, 2:4, :].rearrange("p b (k n) -> p (b k) n", n=S), ACT.Ln, bias=e1, scale=1.0 / 64))
                sig(fn(vT[:, 0:6, :], vT[:, 0:6, :], ACT.Exp, scale=-0.5))
                wp("wst")
                sig(fn(plev[:], ps[:, 1, :], ACT.Copy))
                two_next(b, 6)
                done(b, 6)
                fn(xinv[:], ps[:, 6, :], ACT.Gelu_apprx_tanh)
                sig(fn(yinv[:], ps[:, 7, :], ACT.Gelu_apprx_tanh))
                act.preload_act_table_set(LOGS)
                act.wait_ge(m2_act, M2_ACT.at(l, "gelu"))
                for t in range(ST):
                    ins = fn(mlev[:, t * S:(t + 1) * S], yinv[:, t * S:(t + 1) * S], ACT.Square, accum_out=ss[:, t:t + 1])
                own.link(ins)
                sig(rsqrt(rstd[:, 0:ST], ss[:, 0:ST], 1.0 / 256))
                two_next(b, 7)
                done(b, 7)
                fn(kT[0:96, 0:4, :], ps[0:96, 0:2, :].rearrange("p b (k n) -> p (b k) n", n=S), ACT.Copy)
                sig(fn(kT[0:96, 4:6, :], two(ps[0:96, 5, :]), ACT.Copy))
                two_next(b, 8)
                done(b, 8)
                fn(vT[0:64, 0:2, :], two(ps[0:64, 4, :]), ACT.Copy)
                fn(vT[0:64, 2:6, :], ps[0:64, 6:8, :].rearrange("p b (k n) -> p (b k) n", n=S), ACT.Copy)
                vals = zT[:, 4:7, :].rearrange("p k n -> p (k n)").rearrange("p (t n) -> p t n", t=ST)
                sig(fn(vals, ps[:, 2:4, 0:384], ACT.Copy))

                def mem_out(r):
                    m = (r - 9) % 2
                    done(b, r)
                    dst = mem_k[:, 2 * m:2 * m + 2, :] if r < 11 else mem_v[:, :, S * m:S * (m + 1)]
                    fn(dst, two(ps[:, 7 - m, :]), ACT.Copy).then_inc(mem_kv, 1)

                segs = ((0, 384), (384, 768), (768, D))
                spare = levels[:].rearrange("p (t k) n -> p t (k n)", t=ST)

                def segment(i):
                    c0, c1 = segs[i]
                    for t in range(ST):
                        ins = fn(spare[:, t, c0:c1], tok[:, t, c0:c1], ACT.Square, accum_out=ss[:, 2 * i + t:2 * i + t + 1])
                    own.link(ins)
                    own.link(fn(rstd[:, 2 * i:2 * i + 2], ss[:, 2 * i:2 * i + 2], ACT.Ln, bias=e1, scale=1.0 / (c1 - c0)))
                    sig(fn(rstd[:, 2 * i:2 * i + 2], rstd[:, 2 * i:2 * i + 2], ACT.Exp, scale=-0.5))

                def early(beta):
                    if beta == M2_SEG_AFTER:
                        wv(f"o{beta - 1}")
                        segment(2)
                        segment(0)

                softmaxes = attention(scores_order(M2_BATCHES), wp, wv, sig, lambda n: (MLA_DK if n < 3 else 64) ** -0.5,
                                      (qT[:, 4:8, :], zT[:, 0:4, :]), (4, 4), early)
                with_units(chain((None,), softmaxes), MEM_PLAN, b, mem_out)
                wv(f"o{M2_BATCHES - 1}")
                segment(1)

            def attention(order, wp, wv, sig, scale, pts, bank, after):
                for step in order:
                    kind, beta = step[0], int(step[1:])
                    w = beta % 2
                    if kind == "s":
                        wv(f"mx{beta}")
                        pbuf = (sqf, rsf)[w]
                        for i in range(2 * ST):
                            ins = fn(pbuf[:, i * S:(i + 1) * S], ps[:, 2 * w + i // ST, (i % ST) * S:(i % ST + 1) * S], ACT.Exp,
                                     bias=negmax[:, w, i:i + 1], scale=scale(beta), accum_out=psum_p[:, w, i:i + 1])
                        sig(ins)
                    elif kind == "t":
                        wp(step)
                        sig(fn(pts[w], ps[:, bank[w]:bank[w] + 2, :].rearrange("p b (k n) -> p (b k) n", n=S), ACT.Copy))
                    else:
                        after(beta)
                    yield

            def memory(l, b, n, q):
                wp = lambda name: act.wait_ge(me_pe, ME_PE.at(l, name))
                wv = lambda name: act.wait_ge(me_dve, ME_DVE.at(l, name))
                sig = lambda ins: ins.then_inc(me_act, 1)
                two = lambda v: v.rearrange("p (k n) -> p k n", n=S)
                stats(n, x, 3 * l + (3 * DEPTH + 1))
                high(q + 3, gain2(V2_MEMX), hT_h)
                for m in range(2):
                    two_next(b, 17 + m)
                    done(b, 17 + m)
                    sig(fn(qT[:, 2 * m:2 * m + 2, :], two(ps[:, 4 + m, :]), ACT.Copy))

                def out_high(beta):
                    wp(f"v{beta}")
                    sig(fn(hT_h[:, 2 * beta:2 * beta + 2, :], two(ps[:, 2 * beta, :]), ACT.Copy))

                for _ in attention(ME_ORDER, wp, wv, sig, lambda n: P ** -0.5, (kT[:, 4:8, :], zT[:, 0:4, :]), (4, 6), out_high):
                    pass

            def conv_ffn(l, b):
                F0, G0 = NCH * l + 2 * NCH * DEPTH, NCH * l

                def silu(j):
                    act.wait_ge(gate_used, G0 + j + 1)
                    act.wait_ge(act_ready, F0 + j + 1)
                    fn(sil[:], decay[:], ACT.Silu).then_inc(sil_ready, 1)

                split(b, 2)
                split(b, 3)
                silu(0)
                split(b, 4)
                split(b, 5)
                silu(1)
                split(b, 6)
                with act.Fori(1, NCH - 2) as j:
                    split(b + j, 4)
                    split(b + j, 5)
                    silu(j + 1)
                    split(b + j, 6)
                split(b + (NCH - 2), 4)
                split(b + (NCH - 2), 5)
                silu(NCH - 1)

            def gain2(at):
                return lambda k: vec2[:, at + k:at + k + 1]

            with act.Fori(0, DEPTH) as l:
                own.restart()
                b = LAYER2_TURNS * l + DEPTH * LAYER1_TURNS
                n, q = 3 * l + 3 * DEPTH, 5 * l + 3 * DEPTH
                act.preload_act_table_set(LOGS)
                act.wait_ge(mem_loaded, 16 * l + 16)
                for t in range(ST):
                    own.link(fn((sqf, rsf)[t], memx[:, t, :], ACT.Square, accum_out=ss[:, 6 + t:7 + t]))
                    rsqrt(rstd[:, 6 + t:7 + t], ss[:, 6 + t:7 + t], 1.0 / D).then_inc(mem_rstd, 1)
                split(b, 0)
                split(b, 1)
                stats(n, x, 3 * l + 3 * DEPTH)
                act.wait_ge(vec_ready, l + (DEPTH + 1))
                high(q, gain2(V2_MIX), hT_h)
                high(q + 1, gain2(V2_MEMKV), o_h, 4)
                mixer2(l, b)
                high(q + 2, gain2(V2_ON), hT_h)
                for r in range(13, 17):
                    two_next(b, r)
                memory(l, b, n + 1, q)
                bf = b + MIX2_UNITS // RING
                split(bf, 0)
                split(bf, 1)
                stats(n + 2, x, 3 * l + (3 * DEPTH + 2))
                high(q + 4, gain2(V2_FFN), hT_h)
                conv_ffn(l, bf)
            stats(6 * DEPTH, x, 6 * DEPTH)

        @block.vector
        def _(dve):
            own = Own(dve, dve_own)
            V = nc.vector
            tt, stt, ts = V.tensor_tensor, V.scalar_tensor_tensor, V.tensor_scalar

            def scaled(src, n):
                for t in range(ST):
                    dve.wait_ge(rstd_ready, ST * n + (t + 1))
                    ts(tok[:, t, :], src[:, t, :], rstd[:, t:t + 1], None, ALU.mult).then_inc(xn_ready, 1)

            def low(q, gain, dst_h, dst_l, bank=0):
                for g in range(4):
                    dve.wait_ge(hh_ready, 4 * q + (g + 1))
                    for i in range(2):
                        k = 2 * g + i
                        ins = stt(out=dst_l[:, k, :], in0=ps[:, bank + g, i * S:(i + 1) * S], scalar=gain(k), in1=dst_h[:, k, :].bitcast(F32),
                                  op0=ALU.mult, op1=ALU.subtract)
                    ins.then_inc(h_ready, 1)

            def halve(h, l_, src):
                own.link(V.tensor_copy(h, src))
                return tt(l_, src, h.bitcast(F32), ALU.subtract)

            def columns(n, dst, tiles):
                dve.wait_ge(vec_taken, n + 1)
                V.tensor_copy(dst, ps[:, 7, 0:tiles * P]).then_inc(vec_ready, 1)

            def add_ffn(f, b, scale):
                for t in range(ST):
                    if t < ST - 1:
                        dve.wait_ge(half_done, f + 1)
                    else:
                        dve.wait_ge(unit_done, RING * b + (FFN_UNITS + RING))
                    stt(out=x[:, t, :], in0=ps[:, 4 + 2 * t:6 + 2 * t, :].rearrange("p a n -> p (a n)"), scalar=scale, in1=x[:, t, :],
                        op0=ALU.mult, op1=ALU.add).then_inc(x_ready, 1)

            def ffn(f, b):
                F0 = NCH * f

                def chunk(bb, ku, kd, j, parts=act_parts):
                    dve.wait_ge(act_ready, F0 + j + 1)
                    dve.wait_ge(sil_ready, F0 + j + 1)
                    dve.wait_ge(unit_done, RING * bb + (ku + RING + 1))
                    tt(prod[:], sil[:], ps[:, 1, :], ALU.mult).then_inc(up_used, 1)
                    dve.wait_ge(up_used, F0 + j + 1)
                    if kd is not None:
                        dve.wait_ge(unit_done, RING * bb + (kd + RING + 1))
                    own.link(V.tensor_copy(parts[0], prod[:]))
                    tt(parts[1], prod[:], parts[0].bitcast(F32), ALU.subtract).then_inc(act_ready, 1)

                chunk(b, 1, None, 0)
                chunk(b, 3, 4, 1)
                with dve.Fori(1, NCH - 2) as j:
                    own.restart()
                    chunk(b + j, 3, 4, j + 1)
                own.restart()
                chunk(b + (NCH - 2), 3, None, NCH - 1, last_act)
                add_ffn(f, b, 0.5)

            def freed(l, r):
                dve.wait_ge(bank_free[r % 2], BANK_UNITS[r % 2] * l + (r // 2 + 1))

            def evac1(l, b, r, blocks=(0, 1)):
                kind, c, _, n = mix1_unit(r)
                bank = r % 2
                sl = slice(int(2 * c), int(2 * c) + 2)
                if kind in ("z", "sq", "sk", "sv", "ga", "gb", "b"):
                    return
                dve.wait_ge(unit_done, RING * b + (r + RING + 1))
                src = ps[:, bank, :].rearrange("p (k n) -> p k n", n=S)
                if kind in ("q", "k", "v"):
                    dst = {"q": qT, "k": kT, "v": vT}[kind]
                    w = lambda j, i: vec1[:, V1_CONV + 24 * j + 8 * "qkv".index(kind) + 2 * c + i:][:, 0:1]
                    for i in blocks:
                        ins = ts(dst[:, 2 * c + i, :], src[:, i, :], w(3, i), None, ALU.mult)
                    own.link(ins)
                    for j in (2, 1, 0):
                        d = 3 - j
                        for i in blocks:
                            o = dst[:, 2 * c + i, d:S]
                            ins = stt(out=o, in0=src[:, i, 0:S - d], scalar=w(j, i), in1=o, op0=ALU.mult, op1=ALU.add)
                        if j:
                            own.link(ins)
                    if 1 in blocks:
                        ins.then_inc(bank_free[bank], 1)
                elif kind == "wa":
                    dve.wait_ge(gates_ready, l + 1)
                    tt(zT[:, sl, :], zT[:, sl, :], src, ALU.mult).then_inc(bank_free[bank], 1)
                elif kind == "wb":
                    t1 = sqf[:, 0:512]
                    t2 = rsf[:, 0:512]
                    k2 = lambda v: v.rearrange("p (k n) -> p k n", n=S)
                    tt(k2(t1), vT[:, sl, :], src, ALU.mult).then_inc(bank_free[bank], 1)
                    freed(l, r)
                    own.link(tt(k2(t2), k2(t1), zT[:, sl, :], ALU.add))
                    halve(o_h[:, sl, :], o_l[:, sl, :], k2(t2)).then_inc(merged_ready, 1)
                else:
                    cc_ = slice(S * c, S * (c + 1))
                    if r < MIX1_UNITS - 1:
                        tt(x[:, :, cc_], x[:, :, cc_], src, ALU.add).then_inc(bank_free[bank], 1)
                    else:
                        for t in range(ST):
                            tt(x[:, t, cc_], x[:, t, cc_], src[:, t, :], ALU.add).then_inc(x_ready, 1)
                        dve.wait_ge(x_ready, updates(3 * l + 2))
                        dve.sem_inc(bank_free[bank], 1)

            def pre_norm(l, half):
                dve.wait_ge(pre_act, PRE_ACT.at(HALVES * l + half, "rs"))
                c = half % NPAIR
                q, k = qT[:, 2 * c:2 * c + 2, :], kT[:, 2 * c:2 * c + 2, :]
                rq, rk = (v.rearrange("p (k n) -> p k n", n=S) for v in (mlev, lmat))
                if half < NPAIR:
                    stt(out=q, in0=q, scalar=float(P) ** -0.5, in1=rq, op0=ALU.mult, op1=ALU.mult)
                    tt(k, k, rk, ALU.mult).then_inc(pre_dve, 1)
                else:
                    stt(out=q, in0=q, scalar=gcol[:, 0:1], in1=rq, op0=ALU.mult, op1=ALU.mult)
                    stt(out=k, in0=k, scalar=vec1[:, V1_SBK:V1_SBK + 1], in1=rk, op0=ALU.mult, op1=ALU.mult).then_inc(pre_dve, 1)

            def delta(l, c):
                g = NPAIR * l + c
                wp = lambda name: dve.wait_ge(dl_pe, DELTA_PE.at(g, name))
                wa = lambda name: dve.wait_ge(dl_act, DELTA_ACT.at(g, name))
                me = lambda name: dve.wait_ge(dl_dve, DELTA_DVE.at(g, name))
                heads = (2 * c, 2 * c + 1)
                sl = slice(2 * c, 2 * c + 2)
                probs = [(i, t) for i in range(2) for t in range(ST)]
                of = lambda buf, p: buf[:, p * P:(p + 1) * P]
                col = lambda kind, p: tcol[:, kind, probs[p][1], heads[probs[p][0]]:heads[probs[p][0]] + 1]
                four = lambda v: v.rearrange("p (k n) -> p k n", n=P)
                two = lambda v: v.rearrange("p (k n) -> p k n", n=S)
                wp("rows")
                for p in range(4):
                    ins = ts(of(decay, p), ps[:, 4, p * P:(p + 1) * P], col(1, p), 0.0, ALU.subtract, ALU.min)
                ins.then_inc(dl_dve, 1)
                yield
                wa("decay")
                own.link(tt(four(decay[:]), four(decay[:]), over(cc("chunk"), 4), ALU.mult))
                wp("gram")
                tt(lmat[:], decay[:], ps[:, 2, :], ALU.mult)
                own.link(tt(attn[:], decay[:], ps[:, 3, :], ALU.mult))
                own.link(tt(lmat[:], lmat[:], ps[:, 5, :], ALU.mult))
                own.link(tt(four(mlev[:]), four(lmat[:]), over(cc("inv0"), 4), ALU.mult))
                tt(four(yinv[:]), over(ident, 4), four(mlev[:]), ALU.subtract).then_inc(dl_dve, 1)
                me("lt")
                tt(four(mlev[:]), four(lmat[:]), over(cc("inv1"), 4), ALU.mult).then_inc(dl_dve, 1)
                yield
                yield
                wp("tok")
                V.tensor_copy(egl[:], ps[:, 6, :].rearrange("p (i c n) -> p i c n", i=2, c=4)[:, :, :, CHUNK - 1])
                for i in range(LEVELS):
                    wp(f"p{i}")
                    if i + 1 < LEVELS:
                        tt(four(mlev[:]), four(lmat[:]), over(cc(f"inv{i + 2}"), 4), ALU.mult).then_inc(dl_dve, 1)
                        ts(of(u_v, i), ps[:, 4, i * P:(i + 1) * P], col(0, i), None, ALU.mult)
                        ts(of(w_k, i), ps[:, 7, i * P:(i + 1) * P], col(2, i), None, ALU.mult)
                        ts(of(k_dec, i), ps[:, 7, i * P:(i + 1) * P], col(3, i), None, ALU.mult)
                    else:
                        tt(two(q_dec[:]), qT[:, sl, :], two(ps[:, 6, :]), ALU.mult).then_inc(dl_dve, 1)
                    yield
                    wp(f"q{i}")
                    if i + 1 < LEVELS:
                        tt(xinv[:], xinv[:], ps[:, 5, :], ALU.subtract)
                    tt(yinv[:], yinv[:], ps[:, 2, :], ALU.subtract).then_inc(dl_dve, 1)
                    yield
                yield
                pair = lambda buf, rr, t: buf[rr, :].rearrange("p (i t n) -> p i t n", i=2, t=2)[:, :, t, :]
                wp("kv0")
                V.tensor_copy(state[:, 0, :, :], ps[:, 4, 0:S].rearrange("p (i n) -> p i n", i=2)).then_inc(dl_dve, 1)
                yield
                for ch in range(1, 4):
                    t, half = divmod(ch, 2)
                    rr = slice(64 * half, 64 * half + 64)
                    wp(f"ws{ch}")
                    u = pair(u_v, rr, t)
                    tt(u, u, ps[rr, 5, 0:S].rearrange("p (i n) -> p i n", i=2), ALU.subtract).then_inc(dl_dve, 1)
                    yield
                    if ch < 3:
                        wp(f"kv{ch}")
                        me(f"s{ch - 1}")
                        for i in range(2):
                            ins = stt(out=state[:, ch, i, :], in0=state[:, ch - 1, i, :], scalar=egl[:, i, ch:ch + 1],
                                      in1=ps[:, 4, i * P:(i + 1) * P], op0=ALU.mult, op1=ALU.add)
                        ins.then_inc(dl_dve, 1)
                        yield
                pre_norm(l, c + 1)
                yield
                wa("ors")
                t1 = sq[:, 1, :]
                for i in range(2):
                    ins = stt(out=t1[:, i * S:(i + 1) * S], in0=ps[:, 6 + i, 0:S], scalar=vec1[:, V1_ON:V1_ON + 1], in1=rs[:, 0, i * S:(i + 1) * S],
                              op0=ALU.mult, op1=ALU.mult)
                own.link(ins)
                own.link(tt(two(t1), two(t1), zT[:, sl, :], ALU.mult))
                halve(o_h[:, sl, :], o_l[:, sl, :], two(t1)).then_inc(dl_dve, 1)
                yield

            def stick(l, c):
                g = NPAIR * l + c
                wp = lambda name: dve.wait_ge(sb_pe, SB_PE.at(g, name))
                wa = lambda name: dve.wait_ge(sb_act, SB_ACT.at(g, name))
                sl = slice(2 * c, 2 * c + 2)
                two = lambda v: v.rearrange("p (k n) -> p k n", n=S)
                pair = lambda v: v.rearrange("p (i n) -> p i n", i=2)
                soft, neg = sqf[:, 0:768], rsf[:, 0:768]
                wa("soft")
                own.link(stt(out=pair(neg), in0=ps[:, 4:6, 0:384], scalar=0.0, in1=pair(soft), op0=ALU.max, op1=ALU.add))
                tt(pair(neg), pair(neg), over(cc("sbneg"), 2), ALU.mult).then_inc(sb_dve, 1)
                yield
                wp("tri")
                stt(out=pair(soft), in0=ps[:, 4:6, 0:384], scalar=0.0, in1=over(cc("sbadd"), 2), op0=ALU.min, op1=ALU.add).then_inc(sb_dve, 1)
                if c + 1 < NPAIR:
                    pre_norm(l, NPAIR + c + 1)
                yield
                wa("o")
                tt(hT_l[:, sl, :], two(ps[:, 6, :]), hT_h[:, sl, :].bitcast(F32), ALU.subtract).then_inc(sb_dve, 1)
                yield

            def with_units(steps, todo, l, b):
                late = []
                for at, _ in enumerate(steps):
                    if late:
                        evac1(l, b, *late.pop(0))
                    for r, part in todo[at] if at < len(todo) else ():
                        while part == 0 and late and late[0][0] <= r - 2:
                            evac1(l, b, *late.pop(0))
                        if part == PARTS - 1:
                            late += [(r, (0,)), (r, (1,))] if mix1_unit(r)[0] in ("q", "k", "v") else [(r,)]
                while late:
                    evac1(l, b, *late.pop(0))

            def mixer1(l, b):
                h8 = slice(0, HEADS)
                y, e = sq[h8, 0, 0:S], sq[h8, 0, S:2 * S]
                dve.wait_ge(unit_done, RING * b + (1 + RING + 1))
                ts(y, ps[h8, 1, 0:S], hcol[:, 0:1], None, ALU.add).then_inc(bank_free[1], 1)
                freed(l, 0)
                own.link(ts(beta_r[:, :], beta_r[:, :], 1.0, None, ALU.add))
                own.link(V.reciprocal(beta_r[:, :], beta_r[:, :]))
                dve.wait_ge(rows_act, ROWS_ACT.at(l, "ln"))
                freed(l, 1)
                g0, d = sq[h8, 1, 0:S], sq[h8, 1, S:2 * S]
                own.link(stt(out=g0, in0=y, scalar=0.0, in1=e, op0=ALU.max, op1=ALU.add))
                own.link(ts(g0, g0, hcol[:, 2:3], -1.0, ALU.mult, ALU.mult))
                own.link(V.tensor_tensor_scan(out=g_r[:, :], data0=cc("scan")[h8, :], data1=g0, initial=0.0, op0=ALU.mult, op1=ALU.add))
                gc = g_r[:, :].rearrange("h (c n) -> h c n", n=CHUNK)
                tt(d.rearrange("h (c n) -> h c n", n=CHUNK), gc[:, :, CHUNK - 1:CHUNK].to_broadcast([HEADS, 4, CHUNK]), gc,
                   ALU.subtract).then_inc(rows_dve, 1)
                dve.wait_ge(rows_act, ROWS_ACT.at(l, "eg"))
                tt(y, beta_r[:, :], eg_r[:, :], ALU.mult).then_inc(rows_dve, 1)
                dve.wait_ge(rows_pe, l + 1)
                V.tensor_copy(tcol[:].rearrange("p a t h -> p (a t h)"), ps[:, 7, 0:4 * ST * HEADS]).then_inc(rows_dve, 1)
                dve.wait_ge(rows_dve, ROWS_DVE.at(l, "cols"))
                for r in range(2, len(FIRST)):
                    evac1(l, b, r)
                pre_norm(l, 0)
                with_units(chain(*(delta(l, c) for c in range(NPAIR))), DELTA_PLAN, l, b)
                with_units(chain(*(stick(l, c) for c in range(NPAIR))), SB_PLAN, l, b)
                for r in range(MIX1_UNITS - len(LAST), MIX1_UNITS):
                    evac1(l, b, r)

            V.memset(stage[:], 0.0).then_inc(zeroed, 1)
            V.memset(eps_t[:], EPS).then_inc(eps_ready, 1)
            dve.wait_ge(start_loaded, 32)
            dve.sem_inc(x_ready, ST)
            dve.sem_inc(act_ready, 1)
            with dve.Fori(0, DEPTH) as l:
                own.restart()
                b = LAYER1_TURNS * l
                columns(l, vec1[:, :], 1)
                dve.wait_ge(vec_ready, l + 1)
                ts(gcol[:, 0:1], vec1[:, V1_SBQ:V1_SBQ + 1], float(P) ** -0.5, None, ALU.mult)
                scaled(x, 3 * l)
                low(3 * l, lambda k: vec1[:, V1_FFN1 + k:V1_FFN1 + k + 1], hT_h, hT_l)
                ffn(2 * l, b)
                dve.wait_ge(x_ready, updates(3 * l + 1))
                scaled(x, 3 * l + 1)
                low(3 * l + 1, lambda k: vec1[:, V1_MIX + k:V1_MIX + k + 1], hT_h, hT_l)
                mixer1(l, b + NCH)
                dve.wait_ge(x_ready, updates(3 * l + 2))
                scaled(x, 3 * l + 2)
                low(3 * l + 2, lambda k: vec1[:, V1_FFN2 + k:V1_FFN2 + k + 1], hT_h, hT_l)
                ffn(2 * l + 1, b + (FFN_UNITS + MIX1_UNITS) // RING)
                dve.wait_ge(x_ready, updates(3 * l + 3))

            def mixer2(l, b, q):
                wp = lambda name: dve.wait_ge(m2_pe, M2_PE.at(l, name))
                wa = lambda name: dve.wait_ge(m2_act, M2_ACT.at(l, name))
                me = lambda name: dve.wait_ge(m2_dve, M2_DVE.at(l, name))
                sig = lambda ins: ins.then_inc(m2_dve, 1)
                v2 = lambda c: vec2[:, c:c + 1]
                wa("rs")
                for j in range(4):
                    ins = stt(out=qT[:, j, :], in0=qT[:, j, :], scalar=v2(V2_GK if j == 3 else V2_GQ), in1=vT[:, 2 + j, :], op0=ALU.mult, op1=ALU.mult)
                sig(ins)
                for k in range(3):
                    ins = stt(out=zT[:, k, :], in0=zT[:, k, :], scalar=v2(V2_CQ + k), in1=vT[:, (0, 0, 1)[k], :], op0=ALU.mult, op1=ALU.mult)
                own.link(ins)
                dve.wait_ge(unit_done, RING * b + (6 + RING + 1))
                sig(halve(cn_h, cn_l, zT[:, 0:3, :]))
                wp("rope")
                me("gn")
                r = slice(64, 96)
                t1 = rs[r, 0, 0:S]
                tt(t1, ps[r, 4, 0:S], cc("sina")[r, :], ALU.mult)
                own.link(tt(zT[r, 3, :], zT[r, 3, :], cc("cosa")[r, :], ALU.mult))
                own.link(tt(zT[r, 3, :], zT[r, 3, :], t1, ALU.add))
                sig(V.tensor_copy(vT[r, 0:6, :], over(zT[r, 3, :], 6)))
                turned = sqf.rearrange("p (k n) -> p k n", n=S)
                tt(turned, ps[:, 2:4, :].rearrange("p b (k n) -> p (b k) n", n=S), over(cc("sinb"), 4), ALU.mult)
                own.link(tt(qT[:, 0:4, :], qT[:, 0:4, :], over(cc("cosb"), 4), ALU.mult))
                sig(tt(qT[:, 0:4, :], qT[:, 0:4, :], turned, ALU.add))
                wp("qrope")
                h = slice(0, 96)
                turned = tok[h].rearrange("p t (k n) -> p (t k) n", n=S)[:, 0:6, :]
                tt(turned[:, 0:4, :], ps[h, 0:2, :].rearrange("p b (k n) -> p (b k) n", n=S), over(cc("sina")[h, :], 4), ALU.mult)
                tt(turned[:, 4:6, :], ps[h, 5, :].rearrange("p (k n) -> p k n", n=S), over(cc("sina")[h, :], 2), ALU.mult)
                own.link(tt(kT[h, 0:6, :], kT[h, 0:6, :], over(cc("cosa")[h, :], 6), ALU.mult))
                sig(tt(kT[h, 0:6, :], kT[h, 0:6, :], turned, ALU.add))
                wa("vrs")
                for t in range(ST):
                    c = slice(t * S, (t + 1) * S)
                    ins = stt(out=yinv[:, c], in0=yinv[:, c], scalar=rstd[:, t:t + 1], in1=lmat[:, 0:S], op0=ALU.mult, op1=ALU.mult)
                sig(ins)
                wp("mix")
                me("qr")
                for t in range(ST):
                    for g in range(4):
                        c = slice(t * S + 64 * g, t * S + 64 * g + 64)
                        ins = stt(out=tok[:, t, 768 + 64 * g:832 + 64 * g], in0=ps[:, 6, c], scalar=v2(V2_BS + g), in1=xinv[:, c], op0=ALU.add, op1=ALU.mult)
                sig(ins)

                def seg(i, t):
                    c0, c1 = ((0, 384), (384, 768), (768, D))[i]
                    return ts(tok[:, t, c0:c1], tok[:, t, c0:c1], rstd[:, 2 * i + t:2 * i + t + 1], None, ALU.mult)

                def top(beta):
                    maxima(beta, wp, sig, MLA_DK if beta < 3 else 64)

                top(0)
                for beta in range(M2_BATCHES):
                    if beta + 1 < M2_BATCHES:
                        top(beta + 1)
                    if beta == M2_SEG_AFTER + 1:
                        for i, name in ((2, "seg2"), (0, "seg0")):
                            wa(name)
                            for t in range(ST):
                                seg(i, t)
                    wp(f"v{beta}")
                    w = beta % 2
                    own.link(V.reciprocal(rinv[:, w, :], psum_p[:, w, :]))
                    for i in range(2):
                        c0 = 64 * (2 * beta + i) if beta < 3 else 384 + 64 * (beta - 3 + 3 * i)
                        ins = tt(tok[:, :, c0:c0 + 64], ps[:, 2 * w, 128 * i:128 * (i + 1)].rearrange("p (t e) -> p t e", t=ST),
                                 rinv[:, w, 2 * i:2 * i + 2].unsqueeze(2).to_broadcast([P, ST, 64]), ALU.mult)
                    sig(ins)
                wa("seg1")
                for t in range(ST):
                    seg(1, t).then_inc(xn_ready, 1)
                low(q + 2, gain2(V2_ON), hT_h, hT_l)
                for m in range(4):
                    dve.wait_ge(unit_done, RING * b + (13 + m + RING + 1))
                    c = slice(S * m, S * (m + 1))
                    src = ps[:, 4 + m % 2, :].rearrange("p (t n) -> p t n", n=S)
                    if m < 3:
                        tt(x[:, :, c], x[:, :, c], src, ALU.add).then_inc(added, 1)
                    else:
                        for t in range(ST):
                            tt(x[:, t, c], x[:, t, c], src[:, t, :], ALU.add).then_inc(x_ready, 1)

            def maxima(beta, wp, sig, dk):
                wp(f"s{beta}")
                w = beta % 2
                own.link(V.tensor_reduce(negmax[:, w, :], ps[:, 2 * w:2 * w + 2, :].rearrange("p b (t n) -> p (b t) n", n=S), AX_X, ALU.max))
                sig(ts(negmax[:, w, :], negmax[:, w, :], -float(dk) ** -0.5, None, ALU.mult))

            def memory(l, b, n, q):
                wp = lambda name: dve.wait_ge(me_pe, ME_PE.at(l, name))
                wa = lambda name: dve.wait_ge(me_act, ME_ACT.at(l, name))
                sig = lambda ins: ins.then_inc(me_dve, 1)
                scaled(x, n)
                low(q + 3, gain2(V2_MEMX), hT_h, hT_l)
                for beta in range(ME_BATCHES):
                    maxima(beta, wp, sig, P)
                for beta in range(ME_BATCHES):
                    pbuf = (sqf, rsf)[beta]
                    wa(f"e{beta}")
                    own.link(V.reciprocal(rinv[:, beta, :], psum_p[:, beta, :]))
                    for i in range(2 * ST):
                        ins = ts(pbuf[:, i * S:(i + 1) * S], pbuf[:, i * S:(i + 1) * S], rinv[:, beta, i:i + 1], None, ALU.mult)
                    sig(ins)
                for beta in range(ME_BATCHES):
                    wa(f"oh{beta}")
                    sl = slice(2 * beta, 2 * beta + 2)
                    sig(tt(hT_l[:, sl, :], ps[:, 2 * beta, :].rearrange("p (k n) -> p k n", n=S), hT_h[:, sl, :].bitcast(F32), ALU.subtract))
                dve.wait_ge(unit_done, RING * b + (20 + RING + 1))
                for t in range(ST):
                    for m in range(2):
                        c = slice(512 * m, 512 * (m + 1))
                        ins = tt(x[:, t, c], x[:, t, c], ps[:, 4 + 2 * m + t, :], ALU.add)
                    ins.then_inc(x_ready, 1)

            def conv_ffn(l, b):
                F0, G0 = NCH * l + 2 * NCH * DEPTH, NCH * l

                def convolve(dst, bank, blk):
                    for i in range(2):
                        c0, src = i * S, ps[:, bank, i * S:(i + 1) * S]
                        ins = ts(dst[:, c0:c0 + S], src, vcol(V2_TAP[1], blk, i), vcol(V2_CB, blk, i), ALU.mult, ALU.add)
                    own.link(ins)
                    for i in range(2):
                        c0 = i * S
                        o = dst[:, c0 + 1:c0 + S]
                        ins = stt(out=o, in0=ps[:, bank, c0:c0 + S - 1], scalar=vcol(V2_TAP[0], blk, i), in1=o, op0=ALU.mult, op1=ALU.add)
                    own.link(ins)
                    for i in range(2):
                        c0 = i * S
                        o = dst[:, c0:c0 + S - 1]
                        ins = stt(out=o, in0=ps[:, bank, c0 + 1:c0 + S], scalar=vcol(V2_TAP[2], blk, i), in1=o, op0=ALU.mult, op1=ALU.add)
                    return ins

                def vcol(at, blk, i):
                    return vec2[:, bass.ds(blk + (at + i), 1)]

                def chunk(bb, kg, ku, kd, j, parts=act_parts):
                    dve.wait_ge(unit_done, RING * bb + (kg + RING + 1))
                    dve.wait_ge(sil_ready, F0 + j)
                    dve.wait_ge(act_ready, F0 + j + 1)
                    convolve(decay, 0, 2 * j).then_inc(gate_used, 1)
                    dve.wait_ge(unit_done, RING * bb + (ku + RING + 1))
                    convolve(mlev, 1, 2 * j + FB).then_inc(up_used, 1)
                    dve.wait_ge(sil_ready, F0 + j + 1)
                    dve.wait_ge(up_used, F0 + j + 1)
                    own.link(tt(prod[:], sil[:], mlev[:], ALU.mult))
                    if kd is not None:
                        dve.wait_ge(unit_done, RING * bb + (kd + RING + 1))
                    own.link(V.tensor_copy(parts[0], prod[:]))
                    tt(parts[1], prod[:], parts[0].bitcast(F32), ALU.subtract).then_inc(act_ready, 1)

                chunk(b, 0, 1, None, 0)
                chunk(b, 2, 3, 4, 1)
                with dve.Fori(1, NCH - 2) as j:
                    own.restart()
                    chunk(b + j, 2, 3, 4, j + 1)
                own.restart()
                chunk(b + (NCH - 2), 2, 3, None, NCH - 1, last_act)
                add_ffn(l + 2 * DEPTH, b, 1.0)

            def gain2(at):
                return lambda k: vec2[:, at + k:at + k + 1]

            with dve.Fori(0, DEPTH) as l:
                own.restart()
                b = LAYER2_TURNS * l + DEPTH * LAYER1_TURNS
                n, q = 3 * l + 3 * DEPTH, 5 * l + 3 * DEPTH
                columns(l + DEPTH, vec2[:, :], 3)
                scaled(x, n)
                for t in range(ST):
                    dve.wait_ge(mem_rstd, ST * l + (t + 1))
                    ts(memx[:, t, :], memx[:, t, :], rstd[:, 6 + t:7 + t], None, ALU.mult).then_inc(xn_ready, 1)
                dve.wait_ge(vec_ready, l + (DEPTH + 1))
                low(q, gain2(V2_MIX), hT_h, hT_l)
                low(q + 1, gain2(V2_MEMKV), o_h, o_l, 4)
                mixer2(l, b, q)
                memory(l, b, n + 1, q)
                scaled(x, n + 2)
                low(q + 4, gain2(V2_FFN), hT_h, hT_l)
                conv_ffn(l, b + MIX2_UNITS // RING)
                dve.wait_ge(x_ready, updates(3 * l + (3 * DEPTH + 3)))
            dve.wait_ge(start_loaded, 48)
            for t in range(ST):
                dve.wait_ge(rstd_ready, ST * (6 * DEPTH) + (t + 1))
                stt(out=result[:, t, :], in0=x[:, t, :], scalar=rstd[:, t:t + 1], in1=gain_row, op0=ALU.mult, op1=ALU.mult).then_inc(out_ready, 1)


def kernel(**inputs):
    import numpy as _np
    import concourse.bacc as _bacc
    from concourse import mybir as _mybir
    from concourse.bass_utils import run_bass_kernel_spmd as _run

    nc = _bacc.Bacc("TRN2", target_bir_lowering=False, num_devices=1)
    arrays, args = {}, {}

    def give(name, value):
        arrays[name] = value
        return nc.dram_tensor(name, value.shape, _mybir.dt.from_np(value.dtype), kind="ExternalInput").ap()

    for name, value in inputs.items():
        args[name] = give(f"in_{name}", _np.ascontiguousarray(value))
    const = give("const", constants())
    out = nc.dram_tensor("out", (1, S, D), F32, kind="ExternalOutput").ap()
    build_program(nc, args, const, out)
    r = _run(nc, [arrays], core_ids=[0])
    return r.results[0]["out"]
```
